# Optimizing a Trainium2 kernel written in Bass

```python
import jax, jax.numpy as jnp
from jax import lax
import numpy as np
import math
import jax
import jax.numpy as jnp

D_MODEL = 1024
BATCH = 1
SEQ = 512
DEPTH = 1

EPS = 1e-6
A_HEAD_DIM = 64
A_HEADS_PER_GROUP = 4
A_GROUPS = ((128, 1), (512, 4), (2048, 16))
A_HEADS = A_HEADS_PER_GROUP * len(A_GROUPS)
A_WIDTH = A_HEADS * A_HEAD_DIM
A_OUT = A_HEADS_PER_GROUP * A_HEAD_DIM
A_ROT_DIM = A_HEAD_DIM // 4
A_ROPE_THETA = 500000.0
B_HEADS = 8
B_NOPE = 64
B_ROPE = 32
B_QK = B_NOPE + B_ROPE
B_V = 64
B_Q_RANK = 512
B_KV_RANK = 256
B_ROPE_THETA = 10000.0
B_BLOCK = 128
B_OUT = B_HEADS * B_V
D_FF = 4 * D_MODEL
IN_A = 3 * A_WIDTH
IN_B = B_Q_RANK + B_KV_RANK + B_ROPE
IN_G = 2 * D_MODEL
IN_TOTAL = IN_A + IN_B + IN_G


def rms_norm(x, g):
    xf = x.astype(jnp.float32)
    y = xf * lax.rsqrt(jnp.mean(xf * xf, axis=-1, keepdims=True) + EPS)
    return (y * g.astype(jnp.float32)).astype(x.dtype)

def rotary(x, pos, theta, rot_dim):
    half = rot_dim // 2
    inv = jnp.float32(theta) ** (-(jnp.arange(half, dtype=jnp.float32) * 2.0 / rot_dim))
    ang = pos.astype(jnp.float32)[:, None] * inv[None, :]
    cos = jnp.cos(ang)[:, None, :]
    sin = jnp.sin(ang)[:, None, :]
    xr = x[..., :rot_dim].astype(jnp.float32)
    x1, x2 = xr[..., :half], xr[..., half:]
    rot = jnp.concatenate([x1 * cos - x2 * sin, x2 * cos + x1 * sin], axis=-1).astype(x.dtype)
    return jnp.concatenate([rot, x[..., rot_dim:]], axis=-1)

def banded_attention(q, k, v, radius):
    N, L, H, D = q.shape
    C = radius
    nb = -(-L // C)
    Lp = nb * C
    qb = jnp.pad(q, ((0, 0), (0, Lp - L), (0, 0), (0, 0))).reshape(N, nb, C, H, D)
    pad_kv = ((0, 0), (C, Lp - L + C), (0, 0), (0, 0))
    kp = jnp.pad(k, pad_kv).reshape(N, nb + 2, C, H, D)
    vp = jnp.pad(v, pad_kv).reshape(N, nb + 2, C, H, D)
    kb = jnp.concatenate([kp[:, :-2], kp[:, 1:-1], kp[:, 2:]], axis=2)
    vb = jnp.concatenate([vp[:, :-2], vp[:, 1:-1], vp[:, 2:]], axis=2)
    q_idx = jnp.arange(nb)[:, None] * C + jnp.arange(C)[None, :]
    k_idx = jnp.arange(nb)[:, None] * C - C + jnp.arange(3 * C)[None, :]
    dist = q_idx[:, :, None] - k_idx[:, None, :]
    valid = (jnp.abs(dist) <= radius) & (k_idx[:, None, :] >= 0) & (k_idx[:, None, :] < L)
    s = jnp.einsum('nbqhd,nbkhd->nbhqk', qb, kb).astype(jnp.float32) * (D ** -0.5)
    s = jnp.where(valid[None, :, None], s, -jnp.inf)
    m = jnp.max(s, axis=-1, keepdims=True)
    p = jnp.exp(s - m)
    l = jnp.sum(p, axis=-1, keepdims=True)
    o = jnp.einsum('nbhqk,nbkhd->nbqhd', (p / l).astype(v.dtype), vb)
    lse = (m + jnp.log(l))[..., 0]
    o = o.reshape(N, Lp, H, D)[:, :L]
    lse = lse.transpose(0, 1, 3, 2).reshape(N, Lp, H)[:, :L]
    return o, lse

def dilated_group(q, k, v, window, dilation):
    B, S, H, D = q.shape
    L = S // dilation
    radius = window // (2 * dilation)

    def to_sub(t):
        return t.reshape(B, L, dilation, H, D).transpose(0, 2, 1, 3, 4).reshape(B * dilation, L, H, D)

    o, lse = banded_attention(to_sub(q), to_sub(k), to_sub(v), radius)
    o = o.reshape(B, dilation, L, H, D).transpose(0, 2, 1, 3, 4).reshape(B, S, H, D)
    lse = lse.reshape(B, dilation, L, H).transpose(0, 2, 1, 3).reshape(B, S, H)
    return o, lse

def mixer_dilated(qkv, pos):
    B, S, _ = qkv.shape
    q, k, v = jnp.split(qkv, 3, axis=-1)
    q = rotary(q.reshape(B, S, A_HEADS, A_HEAD_DIM), pos, A_ROPE_THETA, A_ROT_DIM)
    k = rotary(k.reshape(B, S, A_HEADS, A_HEAD_DIM), pos, A_ROPE_THETA, A_ROT_DIM)
    v = v.reshape(B, S, A_HEADS, A_HEAD_DIM)
    outs, lses = [], []
    for g, (window, dilation) in enumerate(A_GROUPS):
        hs = slice(g * A_HEADS_PER_GROUP, (g + 1) * A_HEADS_PER_GROUP)
        o, lse = dilated_group(q[:, :, hs], k[:, :, hs], v[:, :, hs], window, dilation)
        outs.append(o)
        lses.append(lse)
    o = jnp.stack(outs, axis=0)
    w = jax.nn.softmax(jnp.stack(lses, axis=0), axis=0)
    o = jnp.sum(w[..., None].astype(o.dtype) * o, axis=0)
    return o.reshape(B, S, A_OUT)

def mixer_mla(q_c, kv_c, k_pe, pos, q_norm, w_uq, kv_norm, w_ukv):
    B, S, _ = q_c.shape
    q = (rms_norm(q_c, q_norm) @ w_uq).reshape(B, S, B_HEADS, B_QK)
    q = jnp.concatenate([q[..., :B_NOPE], rotary(q[..., B_NOPE:], pos, B_ROPE_THETA, B_ROPE)], axis=-1)
    kv = (rms_norm(kv_c, kv_norm) @ w_ukv).reshape(B, S, B_HEADS, B_NOPE + B_V)
    k_nope, v = kv[..., :B_NOPE], kv[..., B_NOPE:]
    k_pe = rotary(k_pe[:, :, None, :], pos, B_ROPE_THETA, B_ROPE)
    k = jnp.concatenate([k_nope, jnp.broadcast_to(k_pe, (B, S, B_HEADS, B_ROPE))], axis=-1)
    k = k.transpose(0, 2, 1, 3)
    v = v.transpose(0, 2, 1, 3)
    nb = S // B_BLOCK
    q_blocks = q.transpose(0, 2, 1, 3).reshape(B, B_HEADS, nb, B_BLOCK, B_QK).transpose(2, 0, 1, 3, 4)
    scale = B_QK ** -0.5

    def block(qb):
        s = jnp.einsum('bhqd,bhkd->bhqk', qb, k).astype(jnp.float32) * scale
        p = jax.nn.softmax(s, axis=-1)
        return jnp.einsum('bhqk,bhkd->bhqd', p.astype(v.dtype), v)

    o = lax.map(block, q_blocks)
    return o.transpose(1, 0, 3, 2, 4).reshape(B, S, B_OUT)

def first_inputs(seed: int = 0) -> dict:
    key = jax.random.key(seed)
    ks = jax.random.split(key, 18)
    f = jnp.float32

    def w(k, shape):
        return jax.random.normal(k, shape, f) * (shape[0] ** -0.5)

    def gain(k, n):
        return 1.0 + 0.05 * jax.random.normal(k, (n,), f)

    return {
        "x": jax.random.normal(ks[0], (BATCH, SEQ, D_MODEL), f),
        "norm_mix_pre": gain(ks[1], D_MODEL),
        "w_in": w(ks[2], (D_MODEL, IN_TOTAL)),
        "b_gate": 0.02 * jax.random.normal(ks[3], (IN_G,), f),
        "mla_q_norm": gain(ks[4], B_Q_RANK),
        "mla_w_uq": w(ks[5], (B_Q_RANK, B_HEADS * B_QK)),
        "mla_kv_norm": gain(ks[6], B_KV_RANK),
        "mla_w_ukv": w(ks[7], (B_KV_RANK, B_HEADS * (B_NOPE + B_V))),
        "w_o_a": w(ks[8], (A_OUT, D_MODEL)),
        "w_o_b": w(ks[9], (B_OUT, D_MODEL)),
        "w_out": w(ks[10], (D_MODEL, D_MODEL)),
        "norm_mix_post": gain(ks[11], D_MODEL),
        "norm_mlp_pre": gain(ks[12], D_MODEL),
        "w_ff1": w(ks[13], (D_MODEL, D_FF)),
        "w_ff2": w(ks[14], (D_FF, D_MODEL)),
        "norm_mlp_post": gain(ks[15], D_MODEL),
    }

def first_block(x, norm_mix_pre, w_in, b_gate, mla_q_norm, mla_w_uq, mla_kv_norm, mla_w_ukv,
              w_o_a, w_o_b, w_out, norm_mix_post, norm_mlp_pre, w_ff1, w_ff2, norm_mlp_post):
    B, S, D = x.shape
    pos = jnp.arange(S, dtype=jnp.int32)
    h = x
    for _ in range(DEPTH):
        xn = rms_norm(h, norm_mix_pre)
        proj = xn @ w_in
        qkv_a = proj[..., :IN_A]
        q_c = proj[..., IN_A:IN_A + B_Q_RANK]
        kv_c = proj[..., IN_A + B_Q_RANK:IN_A + B_Q_RANK + B_KV_RANK]
        k_pe = proj[..., IN_A + B_Q_RANK + B_KV_RANK:IN_A + IN_B]
        gates = jax.nn.sigmoid(proj[..., IN_A + IN_B:] + b_gate)
        g_a, g_b = gates[..., :D_MODEL], gates[..., D_MODEL:]
        o_a = mixer_dilated(qkv_a, pos) @ w_o_a
        o_b = mixer_mla(q_c, kv_c, k_pe, pos, mla_q_norm, mla_w_uq, mla_kv_norm, mla_w_ukv) @ w_o_b
        mix = (g_a * o_a + g_b * o_b) @ w_out
        h = h + rms_norm(mix, norm_mix_post)
        hn = rms_norm(h, norm_mlp_pre)
        ff = jnp.square(jax.nn.relu(hn @ w_ff1)) @ w_ff2
        h = h + rms_norm(ff, norm_mlp_post)
    return h


CHUNK = 64
Q_BLOCK = 128
NEG_BIG = -1e30
EXP_CLIP = 60.0

D_MIX = D_MODEL
N_MIXERS = 4
GROUP_W = D_MIX // N_MIXERS

S5_CH = 16
S5_GROUPS = GROUP_W // S5_CH
S5_STATE = 64
S5_DT_MIN = 1e-3
S5_DT_MAX = 1e-1

HG_HEADS = 4
HG_DH = GROUP_W // HG_HEADS

FOX_HEADS = 4
FOX_DH = GROUP_W // FOX_HEADS

ML_HEADS = 4
ML_DH = GROUP_W // ML_HEADS
ML_CONV = 4

D_FF_2 = int(math.ceil(8 * D_MODEL / 3 / 256)) * 256

COL_WIDTHS = (GROUP_W,) * 8 + (FOX_HEADS,) + (GROUP_W,) * 4 + (ML_HEADS, ML_HEADS)
D_IN = sum(COL_WIDTHS)
SPLIT_IDX = tuple(int(c) for c in np.cumsum(COL_WIDTHS)[:-1])


F32 = jnp.float32

def rms_norm_2(x, gain):
    xf = x.astype(F32)
    y = xf * lax.rsqrt(jnp.mean(xf * xf, axis=-1, keepdims=True) + EPS)
    return (y * gain.astype(F32)).astype(x.dtype)

def headwise_rms_norm(x, gain, head_dim):
    shp = x.shape
    xf = x.astype(F32).reshape(shp[:-1] + (shp[-1] // head_dim, head_dim))
    y = xf * lax.rsqrt(jnp.mean(xf * xf, axis=-1, keepdims=True) + EPS)
    return (y.reshape(shp) * gain.astype(F32)).astype(x.dtype)

def causal_depthwise_conv(x, w):
    k_w, ch = w.shape
    return lax.conv_general_dilated(
        x, w[:, None, :].astype(x.dtype), window_strides=(1,), padding=[(k_w - 1, 0)],
        dimension_numbers=('NWC', 'WIO', 'NWC'), feature_group_count=ch)

def to_chunks(t):
    b, s, h, d = t.shape
    return t.reshape(b, s // CHUNK, CHUNK, h, d).transpose(1, 0, 3, 2, 4)

def from_chunks(t):
    nc, b, h, l, d = t.shape
    return t.transpose(1, 0, 3, 2, 4).reshape(b, nc * l, h, d)

def _complex_affine_combine(e1, e2):
    a1r, a1i, b1r, b1i = e1
    a2r, a2i, b2r, b2i = e2
    return (a2r * a1r - a2i * a1i, a2r * a1i + a2i * a1r,
            a2r * b1r - a2i * b1i + b2r, a2r * b1i + a2i * b1r + b2i)

def s5_mixer(u, lam_re, lam_im, b_re, b_im, c_re, c_im, d_skip, log_dt, w_glu, gain):
    bsz, seq, _ = u.shape
    uf = u.astype(F32)
    ug = uf.reshape(bsz, seq, S5_GROUPS, S5_CH)
    lr = jnp.minimum(lam_re.astype(F32), -1e-4)
    li = lam_im.astype(F32)
    dt = jnp.exp(log_dt.astype(F32))[:, None]
    mag = jnp.exp(lr * dt)
    ab_re = mag * jnp.cos(li * dt)
    ab_im = mag * jnp.sin(li * dt)
    den = lr * lr + li * li
    cf_re = ((ab_re - 1.0) * lr + ab_im * li) / den
    cf_im = (ab_im * lr - (ab_re - 1.0) * li) / den
    bre = b_re.astype(F32)
    bim = b_im.astype(F32)
    bb_re = cf_re[..., None] * bre - cf_im[..., None] * bim
    bb_im = cf_re[..., None] * bim + cf_im[..., None] * bre
    bu_re = jnp.einsum('bsgp,gnp->bsgn', ug, bb_re)
    bu_im = jnp.einsum('bsgp,gnp->bsgn', ug, bb_im)
    a_re = jnp.broadcast_to(ab_re, bu_re.shape)
    a_im = jnp.broadcast_to(ab_im, bu_im.shape)
    _, _, x_re, x_im = lax.associative_scan(
        _complex_affine_combine, (a_re, a_im, bu_re, bu_im), axis=1)
    y = (jnp.einsum('bsgn,gpn->bsgp', x_re, c_re.astype(F32))
         - jnp.einsum('bsgn,gpn->bsgp', x_im, c_im.astype(F32))).reshape(bsz, seq, GROUP_W)
    y = y + d_skip.astype(F32) * uf
    g = jax.nn.gelu(y)
    y = g * jax.nn.sigmoid(g @ w_glu.astype(F32))
    return rms_norm_2(y, gain).astype(u.dtype)

def _hgrn2_chunk(state, inp):
    q, k, v, lf = inp
    l = q.shape[2]
    b = jnp.cumsum(lf, axis=2)
    o_inter = jnp.einsum('bhtk,bhkv->bhtv', q * jnp.exp(b), state)
    causal = jnp.tril(jnp.ones((l, l), dtype=bool))
    diff = b[:, :, :, None, :] - b[:, :, None, :, :]
    decay = jnp.exp(jnp.where(causal[:, :, None], diff, NEG_BIG))
    scores = jnp.einsum('bhtk,bhsk,bhtsk->bhts', q, k, decay)
    o_intra = jnp.einsum('bhts,bhsv->bhtv', scores, v)
    b_last = b[:, :, -1:, :]
    new_state = (jnp.exp(b_last[:, :, 0, :])[..., None] * state
                 + jnp.einsum('bhsk,bhsv->bhkv', k * jnp.exp(b_last - b), v))
    return new_state, o_inter + o_intra

def hgrn2_mixer(q, fz, i, g, lb, gain):
    bsz, seq, _ = q.shape
    z = fz.astype(F32)
    logf = jax.nn.log_sigmoid(z) + jnp.log1p(lb * jnp.exp(jnp.minimum(-z, EXP_CLIP)))
    k = (1.0 - lb) * jax.nn.sigmoid(-z)

    def heads(t):
        return to_chunks(t.astype(F32).reshape(bsz, seq, HG_HEADS, HG_DH))

    s0 = jnp.zeros((bsz, HG_HEADS, HG_DH, HG_DH), F32)
    _, o = lax.scan(_hgrn2_chunk, s0, (heads(q), heads(k), heads(i), heads(logf)))
    o = from_chunks(o).reshape(bsz, seq, GROUP_W)
    o = headwise_rms_norm(o, gain, HG_DH) * jax.nn.silu(g.astype(F32))
    return o.astype(q.dtype)

def fox_mixer(q, k, v, fz, gain):
    bsz, seq, _ = q.shape

    def heads(t):
        return t.reshape(bsz, seq, FOX_HEADS, FOX_DH).transpose(0, 2, 1, 3)

    qh, kh, vh = heads(q), heads(k), heads(v)
    cum_logf = jnp.cumsum(jax.nn.log_sigmoid(fz.astype(F32)), axis=1).transpose(0, 2, 1)
    n_blk = seq // Q_BLOCK
    q_blocks = qh.reshape(bsz, FOX_HEADS, n_blk, Q_BLOCK, FOX_DH).transpose(2, 0, 1, 3, 4)
    f_blocks = cum_logf.reshape(bsz, FOX_HEADS, n_blk, Q_BLOCK).transpose(2, 0, 1, 3)
    k_pos = jnp.arange(seq)
    scale = FOX_DH ** -0.5

    def attend(args):
        blk, qb, fq = args
        q_pos = blk * Q_BLOCK + jnp.arange(Q_BLOCK)
        s = (jnp.einsum('bhqd,bhkd->bhqk', qb, kh).astype(F32) * scale
             + fq[..., None] - cum_logf[:, :, None, :])
        s = jnp.where(k_pos[None, :] <= q_pos[:, None], s, NEG_BIG)
        p = jax.nn.softmax(s, axis=-1)
        return jnp.einsum('bhqk,bhkd->bhqd', p.astype(vh.dtype), vh)

    out = lax.map(attend, (jnp.arange(n_blk), q_blocks, f_blocks))
    out = out.transpose(1, 0, 3, 2, 4).reshape(bsz, seq, GROUP_W)
    return headwise_rms_norm(out, gain, FOX_DH)

def _mlstm_chunk(carry, inp):
    c_mat, n_vec, m_prev = carry
    q, k, v, ig, lf = inp
    l = q.shape[2]
    b = jnp.cumsum(lf, axis=-1)
    causal = jnp.tril(jnp.ones((l, l), dtype=bool))
    d_log = jnp.where(causal, b[..., :, None] - b[..., None, :] + ig[..., None, :], NEG_BIG)
    inter_log = b + m_prev[..., None]
    m_t = jnp.maximum(inter_log, jnp.max(d_log, axis=-1))
    w_inter = jnp.exp(inter_log - m_t)
    qk = jnp.einsum('bhtd,bhsd->bhts', q, k) * jnp.exp(d_log - m_t[..., None])
    num = (w_inter[..., None] * jnp.einsum('bhtk,bhkv->bhtv', q, c_mat)
           + jnp.einsum('bhts,bhsv->bhtv', qk, v))
    den = w_inter * jnp.einsum('bhtk,bhk->bht', q, n_vec) + jnp.sum(qk, axis=-1)
    h = num / jnp.maximum(jnp.abs(den), jnp.exp(-m_t))[..., None]
    b_last = b[..., -1]
    src_log = b_last[..., None] - b + ig
    m_new = jnp.maximum(b_last + m_prev, jnp.max(src_log, axis=-1))
    w_src = jnp.exp(src_log - m_new[..., None])
    decay = jnp.exp(b_last + m_prev - m_new)
    c_new = decay[..., None, None] * c_mat + jnp.einsum('bhs,bhsk,bhsv->bhkv', w_src, k, v)
    n_new = decay[..., None] * n_vec + jnp.einsum('bhs,bhsk->bhk', w_src, k)
    return (c_new, n_new, m_new), h

def mlstm_mixer(q, k, v, o, ig, fz, conv_w, gain):
    bsz, seq, _ = q.shape
    qk = jax.nn.silu(causal_depthwise_conv(jnp.concatenate([q, k], axis=-1), conv_w))
    q_c, k_c = qk[..., :GROUP_W], qk[..., GROUP_W:]

    def heads(t):
        return to_chunks(t.astype(F32).reshape(bsz, seq, ML_HEADS, ML_DH))

    def gates(t):
        return to_chunks(t.astype(F32)[..., None])[..., 0]

    lf = jax.nn.log_sigmoid(fz.astype(F32))
    init = (jnp.zeros((bsz, ML_HEADS, ML_DH, ML_DH), F32),
            jnp.zeros((bsz, ML_HEADS, ML_DH), F32),
            jnp.zeros((bsz, ML_HEADS), F32))
    _, h = lax.scan(_mlstm_chunk, init,
                    (heads(q_c), heads(k_c * ML_DH ** -0.5), heads(v), gates(ig), gates(lf)))
    h = from_chunks(h).reshape(bsz, seq, GROUP_W)
    h = headwise_rms_norm(h, gain, ML_DH) * jax.nn.sigmoid(o.astype(F32))
    return h.astype(q.dtype)

def second_inputs(seed: int = 0) -> dict:
    key = jax.random.key(seed)
    ks = jax.random.split(key, 26)

    def nrm(k, shape, scale):
        return scale * jax.random.normal(k, shape, F32)

    x = nrm(ks[0], (BATCH, SEQ, D_MODEL), 1.0)
    w_in = nrm(ks[1], (DEPTH, D_MODEL, D_IN), D_MODEL ** -0.5)
    fox_fb = 2.0 + nrm(ks[2], (DEPTH, FOX_HEADS), 0.1)
    ml_ib = nrm(ks[3], (DEPTH, ML_HEADS), 0.1)
    ml_fb = jnp.linspace(3.0, 6.0, ML_HEADS, dtype=F32)[None, :] + nrm(ks[4], (DEPTH, ML_HEADS), 0.1)
    gate_bias = jnp.concatenate([fox_fb, ml_ib, ml_fb], axis=-1)
    n_idx = jnp.arange(S5_STATE, dtype=F32)
    s5_lambda_re = -0.5 + nrm(ks[5], (DEPTH, S5_GROUPS, S5_STATE), 0.01)
    s5_lambda_im = math.pi * n_idx + nrm(ks[6], (DEPTH, S5_GROUPS, S5_STATE), 0.01)
    s5_b_re = nrm(ks[7], (DEPTH, S5_GROUPS, S5_STATE, S5_CH), (2 * S5_CH) ** -0.5)
    s5_b_im = nrm(ks[8], (DEPTH, S5_GROUPS, S5_STATE, S5_CH), (2 * S5_CH) ** -0.5)
    s5_c_re = nrm(ks[9], (DEPTH, S5_GROUPS, S5_CH, S5_STATE), (2 * S5_STATE) ** -0.5)
    s5_c_im = nrm(ks[10], (DEPTH, S5_GROUPS, S5_CH, S5_STATE), (2 * S5_STATE) ** -0.5)
    s5_d = nrm(ks[11], (DEPTH, GROUP_W), 1.0)
    s5_log_dt = jax.random.uniform(ks[12], (DEPTH, S5_GROUPS), F32,
                                   math.log(S5_DT_MIN), math.log(S5_DT_MAX))
    s5_w_glu = nrm(ks[13], (DEPTH, GROUP_W, GROUP_W), GROUP_W ** -0.5)
    hgrn_lb_logits = nrm(ks[14], (DEPTH, GROUP_W), 0.5)
    mlstm_conv_w = nrm(ks[15], (DEPTH, ML_CONV, 2 * GROUP_W), ML_CONV ** -0.5)
    mix_gain = 1.0 + nrm(ks[16], (DEPTH, D_MIX), 0.02)
    w_out = nrm(ks[17], (DEPTH, D_MIX, D_MODEL), D_MIX ** -0.5)
    ln_mix_pre = 1.0 + nrm(ks[18], (DEPTH, D_MODEL), 0.02)
    ln_mix_post = 1.0 + nrm(ks[19], (DEPTH, D_MODEL), 0.02)
    ln_ffn_pre = 1.0 + nrm(ks[20], (DEPTH, D_MODEL), 0.02)
    ln_ffn_post = 1.0 + nrm(ks[21], (DEPTH, D_MODEL), 0.02)
    w_ffn_gate = nrm(ks[22], (DEPTH, D_MODEL, D_FF_2), D_MODEL ** -0.5)
    w_ffn_up = nrm(ks[23], (DEPTH, D_MODEL, D_FF_2), D_MODEL ** -0.5)
    w_ffn_down = nrm(ks[24], (DEPTH, D_FF_2, D_MODEL), D_FF_2 ** -0.5)
    return {'x': x, 'w_in': w_in, 'gate_bias': gate_bias,
            's5_lambda_re': s5_lambda_re, 's5_lambda_im': s5_lambda_im,
            's5_b_re': s5_b_re, 's5_b_im': s5_b_im, 's5_c_re': s5_c_re, 's5_c_im': s5_c_im,
            's5_d': s5_d, 's5_log_dt': s5_log_dt, 's5_w_glu': s5_w_glu,
            'hgrn_lb_logits': hgrn_lb_logits, 'mlstm_conv_w': mlstm_conv_w,
            'mix_gain': mix_gain, 'w_out': w_out,
            'ln_mix_pre': ln_mix_pre, 'ln_mix_post': ln_mix_post,
            'ln_ffn_pre': ln_ffn_pre, 'ln_ffn_post': ln_ffn_post,
            'w_ffn_gate': w_ffn_gate, 'w_ffn_up': w_ffn_up, 'w_ffn_down': w_ffn_down}

def second_block(x, w_in, gate_bias, s5_lambda_re, s5_lambda_im, s5_b_re, s5_b_im, s5_c_re, s5_c_im,
              s5_d, s5_log_dt, s5_w_glu, hgrn_lb_logits, mlstm_conv_w, mix_gain, w_out,
              ln_mix_pre, ln_mix_post, ln_ffn_pre, ln_ffn_post, w_ffn_gate, w_ffn_up, w_ffn_down):
    lb_prob = jax.nn.softmax(hgrn_lb_logits.astype(F32), axis=0)
    lb_all = jnp.maximum(jnp.cumsum(lb_prob, axis=0) - lb_prob[0:1], 0.0)

    h = x
    for l in range(DEPTH):
        a = rms_norm_2(h, ln_mix_pre[l])
        proj = a @ w_in[l]
        (s5_u, hg_q, hg_f, hg_i, hg_g, fox_q, fox_k, fox_v, fox_f,
         ml_q, ml_k, ml_v, ml_o, ml_i, ml_f) = jnp.split(proj, SPLIT_IDX, axis=-1)
        gb = gate_bias[l]
        gain = mix_gain[l]
        y_a = s5_mixer(s5_u, s5_lambda_re[l], s5_lambda_im[l], s5_b_re[l], s5_b_im[l],
                       s5_c_re[l], s5_c_im[l], s5_d[l], s5_log_dt[l], s5_w_glu[l],
                       gain[0:GROUP_W])
        y_b = hgrn2_mixer(hg_q, hg_f, hg_i, hg_g, lb_all[l], gain[GROUP_W:2 * GROUP_W])
        y_c = fox_mixer(fox_q, fox_k, fox_v, fox_f + gb[0:FOX_HEADS],
                        gain[2 * GROUP_W:3 * GROUP_W])
        y_d = mlstm_mixer(ml_q, ml_k, ml_v, ml_o,
                          ml_i + gb[FOX_HEADS:FOX_HEADS + ML_HEADS],
                          ml_f + gb[FOX_HEADS + ML_HEADS:FOX_HEADS + 2 * ML_HEADS],
                          mlstm_conv_w[l], gain[3 * GROUP_W:4 * GROUP_W])
        mix = jnp.concatenate([y_a, y_b, y_c, y_d], axis=-1) @ w_out[l]
        h = h + rms_norm_2(mix, ln_mix_post[l])

        a = rms_norm_2(h, ln_ffn_pre[l])
        ff = (jax.nn.silu(a @ w_ffn_gate[l]) * (a @ w_ffn_up[l])) @ w_ffn_down[l]
        h = h + rms_norm_2(ff, ln_ffn_post[l])
    return h


def setup_inputs(seed=0):
    out = dict(first_inputs(seed))
    for name, value in second_inputs(seed + 1).items():
        if name != "x":
            out[name + "_2"] = value
    return out


def reference(
    x, norm_mix_pre, w_in, b_gate, mla_q_norm, mla_w_uq, mla_kv_norm, mla_w_ukv, w_o_a, w_o_b,
    w_out, norm_mix_post, norm_mlp_pre, w_ff1, w_ff2, norm_mlp_post, w_in_2, gate_bias_2,
    s5_lambda_re_2, s5_lambda_im_2, s5_b_re_2, s5_b_im_2, s5_c_re_2, s5_c_im_2, s5_d_2,
    s5_log_dt_2, s5_w_glu_2, hgrn_lb_logits_2, mlstm_conv_w_2, mix_gain_2, w_out_2,
    ln_mix_pre_2, ln_mix_post_2, ln_ffn_pre_2, ln_ffn_post_2, w_ffn_gate_2, w_ffn_up_2,
    w_ffn_down_2,
):
    x = first_block(
        x, norm_mix_pre, w_in, b_gate, mla_q_norm, mla_w_uq, mla_kv_norm, mla_w_ukv, w_o_a,
        w_o_b, w_out, norm_mix_post, norm_mlp_pre, w_ff1, w_ff2, norm_mlp_post,
    )
    return second_block(
        x, w_in_2, gate_bias_2, s5_lambda_re_2, s5_lambda_im_2, s5_b_re_2, s5_b_im_2, s5_c_re_2,
        s5_c_im_2, s5_d_2, s5_log_dt_2, s5_w_glu_2, hgrn_lb_logits_2, mlstm_conv_w_2,
        mix_gain_2, w_out_2, ln_mix_pre_2, ln_mix_post_2, ln_ffn_pre_2, ln_ffn_post_2,
        w_ffn_gate_2, w_ffn_up_2, w_ffn_down_2,
    )


_drawn_inputs = setup_inputs


def setup_inputs(seed=0):
    import zlib

    import numpy as np

    out = dict(_drawn_inputs(seed))
    spreads = {}
    factors = {'b_gate': 7.981,
     's5_lambda_re_2': 64.0,
     's5_c_re_2': 2.726,
     'mix_gain_2': 5.301,
     'ln_mix_pre_2': 3.481,
     'ln_mix_post_2': 4.694,
     'ln_ffn_pre_2': 4.369,
     'ln_ffn_post_2': 22.994,
     's5_b_re_2': 2.791,
     's5_b_im_2': 2.947,
     's5_c_im_2': 5.696}
    for name, (base, spread) in spreads.items():
        noise = np.random.default_rng([zlib.crc32(name.encode()), seed]).standard_normal(out[name].shape)
        drawn = base * np.exp(spread * noise) if base else spread * noise
        out[name] = jnp.asarray(drawn.astype(out[name].dtype))
    for name, factor in factors.items():
        out[name] = (out[name] * factor).astype(out[name].dtype)
    return out
```

```python
from contextlib import ExitStack

import numpy as np

import concourse.bass as bass
from concourse import mybir

ALU = mybir.AluOpType
ACT = mybir.ActivationFunctionType
AX = mybir.AxisListType
F32 = mybir.dt.float32
BF16 = mybir.dt.bfloat16

P = 128
S = 512
T = S // P
D = 1024
KD = D // P
EPS = 1e-6
KB = 1024
DH = 64
NEG = -1e30

A_HEADS = 4
A_DIL = (1, 4, 16)
B_HEADS = 8
B_QK = 96
FF1 = 4096
FF2 = 2816
COLS = {}
_at = 0
for _name, _n in (("mix_pre", 8), ("b_gate", 16), ("q_norm", 4), ("kv_norm", 2), ("mlp_pre", 8),
                  ("mix_pre2", 8), ("ffn_pre2", 8), ("mix_gain2", 8), ("hg_lb", 2), ("conv_w", 16),
                  ("lam_re", 8), ("lam_im", 8), ("log_dt", 8), ("s5_d", 2), ("gate_b", 3)):
    COLS[_name] = (_at, _n)
    _at += _n
NCOLS = _at


class Signal:

    def __init__(self, sem):
        self.sem = sem
        self.base = 0


class Kernel:
    pass


def allocate(nc, ctx, d):
    k = Kernel()
    k.nc, k.d = nc, d

    def sb(name, kb, shape, dt=F32):
        return nc.alloc_sbuf_tensor_at(name, shape, dt, offset=int(kb * KB) + k.sb0)

    k.sb0 = (nc.sbuf_base + 63) // 64 * 64
    k.sb = sb
    k.h = sb("h", 0, [P, T, D])
    k.xT = sb("xT", 16, [P, KD, S])
    k.ring = sb("ring", 32, [P, 2, 4096])
    k.ident = sb("ident", 64, [P, P])
    k.identb = sb("identb", 64.5, [P, P], BF16)
    k.mask_band = sb("mask_band", 64.75, [P, 3 * P], BF16)
    k.mask_d4 = sb("mask_d4", 65.5, [P, P], BF16)
    k.mask_d16 = sb("mask_d16", 65.75, [P, P], BF16)
    k.mask_row = sb("mask_row", 66, [P, P], BF16)
    k.mask_col = sb("mask_col", 66.25, [P, P], BF16)
    k.mask_lev = sb("mask_lev", 66.5, [P, 8, P], BF16)
    k.ropeA = sb("ropeA", 68.5, [P, 3, T, 16])
    k.ropeB = sb("ropeB", 69.25, [P, T, 32])
    k.cols = sb("cols", 69.75, [P, NCOLS])
    k.stat = sb("stat", 70.25 + 0.25, [P, 64])
    k.ones = sb("ones", 70.75, [P, 16])
    k.pb = [ctx.enter_context(nc.psum_tensor(f"bank{i}", [P, 512], F32)) for i in range(8)]
    k.sems = {}

    def sig(name):
        if name not in k.sems:
            k.sems[name] = Signal(ctx.enter_context(nc.semaphore(name)))
        return k.sems[name]

    k.sig = sig
    k.w_landed = [sig("w_landed0"), sig("w_landed1")]
    k.w_used = sig("w_used")
    k.freed = {}
    k.c_in = sig("consts_in")
    k.x_in = sig("x_in")
    k.chunks = []
    k.att_n = 0
    k.issued = 0
    return k


def col(k, name, i=0, n=1):
    a, _ = COLS[name]
    return k.cols[:, a + i:a + i + n]


def issue_chunks(k, eng, upto):
    for g in range(k.issued, min(upto, len(k.chunks))):
        src = k.chunks[g]
        if g >= 2:
            sem, count = k.freed[g - 2]
            eng.wait_ge(sem, count)
        eng.dma_start(k.ring[:, g % 2, 0:src.shape[1]], src).then_inc(k.w_landed[g % 2].sem, 16)
    k.issued = max(k.issued, min(upto, len(k.chunks)))


def wait_chunk(k, pe, g):
    pe.wait_ge(k.w_landed[g % 2].sem, 16 * (g // 2 + 1))


def slot(k, g, a, b):
    return k.ring[:, g % 2, a:b]


def note_freed(k, steps, done):
    final = {s[0]: i for i, s in enumerate(steps)}
    marks = set()
    for g, i in final.items():
        if steps[i][5]:
            k.freed[g] = (done.sem, done.base + sum(s[5] for s in steps[:i + 1]))
        else:
            k.w_used.base += 1
            k.freed[g] = (k.w_used.sem, k.w_used.base)
            marks.add(i)
    return marks


class Chain:

    def __init__(self, eng, signal):
        self.eng, self.s = eng, signal

    def __call__(self, ins):
        self.s.base += 1
        ins.then_inc(self.s.sem, 1)
        self.eng.wait_ge(self.s.sem, self.s.base)


def stage_load(k):
    nc, d = k.nc, k.d
    with nc.Block() as block:
        @block.sync
        def _(sp):
            sp.dma_start(k.h[:, :, :], d["x"].rearrange("(t p) n -> p t n", p=P)).then_inc(k.x_in.sem, 16)
            issue_chunks(k, sp, 2)

        @block.scalar
        def _(act):
            for dst, name in ((k.cols[:, :], "cols"), (k.ident[:, :], "ident"),
                              (k.identb[:, :], "identb"), (k.mask_band[:, :], "mask_band"),
                              (k.mask_d4[:, :], "mask_d4"), (k.mask_d16[:, :], "mask_d16"),
                              (k.mask_row[:, :], "mask_row"), (k.mask_col[:, :], "mask_col"),
                              (k.mask_lev[:, :, :], "mask_lev"), (k.ropeA[:, :, :, :], "ropeA"),
                              (k.ropeB[:, :, :], "ropeB")):
                act.dma_start(dst, d[name]).then_inc(k.c_in.sem, 16)
            act.wait_ge(k.c_in.sem, 16 * 11)
            act.wait_ge(k.x_in.sem, 16)

        @block.vector
        def _(dve):
            nc.vector.memset(k.ones[:, :], 1.0)


def stage_norm_T(k, tag, src, width, gain, dst, xn_kb, upto=0):
    nc = k.nc
    kt = width // P
    sq, root, scaled, turned, ev_act, ev_dve = (
        k.sig(n) for n in ("norm_sumsq", "norm_root", "norm_scaled", "norm_turned", "norm_evac_act", "norm_evac_dve"))
    ms, rs, half = k.stat[:, 0:T], k.stat[:, T:2 * T], k.stat[:, 2 * T:3 * T]
    xn = k.sb(f"xn_{tag}", xn_kb, [P, T, width])
    with nc.Block() as block:
        @block.sync
        def _(sp):
            issue_chunks(k, sp, upto)

        @block.scalar
        def _(act):
            for t in range(T):
                nc.scalar.activation(xn[:, t, :], src[:, t, :], ACT.Square,
                                     accum_out=k.stat[:, t:t + 1]).then_inc(sq.sem, 1)
            for f in range(0, kt, 2):
                act.wait_ge(turned.sem, turned.base + f + 1)
                nc.scalar.mul(dst[:, f, :], k.pb[f % 2][:, :], col(k, gain, f)).then_inc(ev_act.sem, 1)

        @block.gpsimd
        def _(pool):
            pool.wait_ge(root.sem, root.base + 1)
            nc.gpsimd.tensor_tensor(rs, ms, half, ALU.pow).then_inc(root.sem, 1)

        @block.vector
        def _(dve):
            nc.vector.memset(half, -0.5).then_inc(sq.sem, 1)
            dve.wait_ge(sq.sem, sq.base + T + 1)
            nc.vector.tensor_scalar(ms, ms, 1.0 / width, EPS, ALU.mult, ALU.add).then_inc(root.sem, 1)
            dve.wait_ge(root.sem, root.base + 2)
            for t in range(T):
                nc.vector.tensor_scalar(xn[:, t, :], src[:, t, :], rs[:, t:t + 1], None,
                                        ALU.mult).then_inc(scaled.sem, 1)
            for f in range(1, kt, 2):
                dve.wait_ge(turned.sem, turned.base + f + 1)
                nc.vector.tensor_scalar(dst[:, f, :], k.pb[f % 2][:, :], col(k, gain, f), None,
                                        ALU.mult).then_inc(ev_dve.sem, 1)

        @block.tensor
        def _(pe):
            for f in range(kt):
                if f >= 2:
                    ev = (ev_act, ev_dve)[f % 2]
                    pe.wait_ge(ev.sem, ev.base + f // 2)
                for t in range(T):
                    if f == 0:
                        pe.wait_ge(scaled.sem, scaled.base + t + 1)
                    last = nc.tensor.transpose(k.pb[f % 2][:, t * P:(t + 1) * P],
                                               xn[:, t, f * P:(f + 1) * P], k.ident[:, :])
                last.then_inc(turned.sem, 1)
    sq.base += T + 1
    root.base += 2
    scaled.base += T
    turned.base += kt
    ev_act.base += (kt + 1) // 2
    ev_dve.base += kt // 2


def stage_gemm(k, steps, evac, upto):
    nc = k.nc
    done, free_act, free_dve = (k.sig(n) for n in ("gemm_done", "gemm_free_act", "gemm_free_dve"))
    n = 1 + max(s[1] for s in steps)
    outs = {s[1]: s[2] for s in steps}
    marks = note_freed(k, steps, done)
    with nc.Block() as block:
        @block.sync
        def _(sp):
            issue_chunks(k, sp, upto)

        @block.tensor
        def _(pe):
            seen = set()
            for i, (g, j, out, pairs, first, last) in enumerate(steps):
                if g is not None and g not in seen:
                    seen.add(g)
                    wait_chunk(k, pe, g)
                if first and j >= 4:
                    free = (free_act, free_dve)[j % 2]
                    pe.wait_ge(free.sem, free.base + (j - 4) // 2 + 1)
                for m, (a, b) in enumerate(pairs):
                    mm = nc.tensor.matmul(out, a, b, start=first and m == 0, stop=last and m == len(pairs) - 1)
                if last:
                    mm.then_inc(done.sem, 1)
                if i in marks:
                    mm.then_inc(k.w_used.sem, 1)

        @block.scalar
        def _(act):
            for j in range(0, n, 2):
                act.wait_ge(done.sem, done.base + j + 1)
                evac("act", act, j, outs[j]).then_inc(free_act.sem, 1)

        @block.vector
        def _(dve):
            for j in range(1, n, 2):
                dve.wait_ge(done.sem, done.base + j + 1)
                evac("dve", dve, j, outs[j]).then_inc(free_dve.sem, 1)
    done.base += n
    free_act.base += (n + 1) // 2
    free_dve.base += n // 2


def copy_out(k, who, dst, src):
    return k.nc.scalar.copy(dst, src) if who == "act" else k.nc.vector.tensor_copy(dst, src)


def tokens(k, perm, kt, t):
    if perm == 0:
        return k.xT[:, kt, t * P:(t + 1) * P]
    return k.xT[:, kt, t::T]


def stage_attention(k, batches, scale, bufs_kb, upto, lse=None):
    nc = k.nc
    nb = len(batches)
    scored, negmax, expd, turned, ev_act, ev_dve, mixed, out_free = (
        k.sig(n) for n in ("att_scored", "att_negmax", "att_exp", "att_turned", "att_ptT_act", "att_ptT_dve",
                           "att_mixed", "att_out"))
    k.att_n += 1
    probs = k.sb(f"probs{k.att_n}", bufs_kb, [P, 2, 512])
    probsT = k.sb(f"probsT{k.att_n}", bufs_kb + 4, [P, 2, 512])
    ns = max(len(b["segs"]) for b in batches)
    mx = k.sb(f"mx{k.att_n}", bufs_kb + 8, [P, nb, ns])
    nm = k.sb(f"nm{k.att_n}", bufs_kb + 8.5, [P, nb, ns])
    ls = k.sb(f"ls{k.att_n}", bufs_kb + 9, [P, nb, ns])
    li = k.sb(f"li{k.att_n}", bufs_kb + 9.5, [P, nb, ns])
    chain = k.sig("dve_chain")
    chain_act = k.sig("act_chain")

    def width(b):
        return b["segs"][-1][1]

    with nc.Block() as block:
        @block.sync
        def _(sp):
            issue_chunks(k, sp, upto)

        @block.tensor
        def _(pe):
            def scores(i):
                b = batches[i]
                if i >= 2:
                    pe.wait_ge(expd.sem, expd.base + i - 1)
                for (c0, c1), parts in zip(b["segs"], b["scores"]):
                    for m, (a, r, lo, hi) in enumerate(parts):
                        mm = nc.tensor.matmul(k.pb[i % 2][:, lo:hi], a, r, start=m == 0,
                                              stop=m == len(parts) - 1, skip_group_check=True)
                mm.then_inc(scored.sem, 1)

            def turn(i):
                b = batches[i]
                pe.wait_ge(expd.sem, expd.base + i + 1)
                if i >= 2:
                    ev = (ev_act, ev_dve)[i % 2]
                    pe.wait_ge(ev.sem, ev.base + i // 2)
                for c in range(0, width(b), P):
                    mm = nc.tensor.transpose(k.pb[2 + i % 2][:, c:c + P], probs[:, i % 2, c:c + P], k.ident[:, :])
                mm.then_inc(turned.sem, 1)

            def mix(i):
                b = batches[i]
                ev = (ev_act, ev_dve)[i % 2]
                pe.wait_ge(ev.sem, ev.base + i // 2 + 1)
                if i >= 2:
                    pe.wait_ge(out_free.sem, out_free.base + i - 1)
                for n, ((c0, c1), vs) in enumerate(zip(b["segs"], b["values"])):
                    for m, v in enumerate(vs):
                        mm = nc.tensor.matmul(k.pb[4 + i % 2][:, n * DH:(n + 1) * DH],
                                              probsT[:, i % 2, c0 + m * P:c0 + (m + 1) * P], v,
                                              start=m == 0, stop=m == len(vs) - 1, skip_group_check=True)
                mm.then_inc(mixed.sem, 1)

            for i in range(nb + 2):
                if i < nb:
                    scores(i)
                if 1 <= i <= nb:
                    turn(i - 1)
                if i >= 2:
                    mix(i - 2)

        def evac(who, eng, i):
            w = width(batches[i])
            eng.wait_ge(turned.sem, turned.base + i + 1)
            if i >= 2:
                eng.wait_ge(mixed.sem, mixed.base + i - 1)
            copy_out(k, who, probsT[:, i % 2, 0:w], k.pb[2 + i % 2][:, 0:w]).then_inc(
                (ev_act if who == "act" else ev_dve).sem, 1)

        @block.scalar
        def _(act):
            for i in range(nb + 1):
                if i < nb:
                    b = batches[i]
                    act.wait_ge(negmax.sem, negmax.base + i + 1)
                    if i >= 2:
                        act.wait_ge(turned.sem, turned.base + i - 1)
                    for n, (c0, c1) in enumerate(b["segs"]):
                        e = nc.scalar.activation(probs[:, i % 2, c0:c1], k.pb[i % 2][:, c0:c1], ACT.Exp,
                                                 bias=nm[:, i, n:n + 1], scale=scale,
                                                 accum_out=ls[:, i, n:n + 1])
                    e.then_inc(expd.sem, 1)
                if i >= 1 and (i - 1) % 2 == 0:
                    evac("act", act, i - 1)
            if lse is not None:
                act.wait_ge(expd.sem, expd.base + nb)
                nc.scalar.activation(mx[:, :, :], ls[:, :, :], ACT.Ln).then_inc(chain_act.sem, 1)

        @block.vector
        def _(dve):
            link = Chain(dve, chain)
            if lse is not None:
                link(nc.vector.memset(ls[:, :, :], 1.0))
            for i in range(nb + 2):
                if i < nb:
                    b = batches[i]
                    m = len(b["segs"])
                    dve.wait_ge(scored.sem, scored.base + i + 1)
                    w = width(b)
                    link(nc.vector.tensor_reduce(
                        mx[:, i, 0:m], k.pb[i % 2][:, 0:w].rearrange("p (m w) -> p m w", m=m), AX.X, ALU.max))
                    nc.vector.tensor_scalar(nm[:, i, 0:m], mx[:, i, 0:m], -scale, None,
                                            ALU.mult).then_inc(negmax.sem, 1)
                if 1 <= i <= nb and (i - 1) % 2 == 1:
                    evac("dve", dve, i - 1)
                if i >= 2:
                    j = i - 2
                    b = batches[j]
                    m = len(b["segs"])
                    dve.wait_ge(expd.sem, expd.base + j + 1)
                    link(nc.vector.reciprocal(li[:, j, 0:m], ls[:, j, 0:m]))
                    dve.wait_ge(mixed.sem, mixed.base + j + 1)
                    if m == 1:
                        nc.vector.tensor_scalar(b["out"], k.pb[4 + j % 2][:, 0:DH], li[:, j, 0:1], None,
                                                ALU.mult).then_inc(out_free.sem, 1)
                    else:
                        nc.vector.tensor_tensor(
                            b["out"], k.pb[4 + j % 2][:, 0:m * DH].rearrange("p (m e) -> p m e", m=m),
                            li[:, j, 0:m].unsqueeze(2).to_broadcast([P, m, DH]), ALU.mult).then_inc(out_free.sem, 1)
            if lse is not None:
                dve.wait_ge(chain_act.sem, chain_act.base + 1)
                for dst, i, n in lse:
                    nc.vector.tensor_tensor(dst, mx[:, i, 0:n], nm[:, i, 0:n], ALU.subtract)
                chain_act.base += 1
    for s in (scored, negmax, expd, turned, mixed, out_free):
        s.base += nb
    ev_act.base += (nb + 1) // 2
    ev_dve.base += nb // 2


def stage_turn(k, items, upto=0, before=None):
    nc = k.nc
    n = len(items)
    turned, ev_act, ev_dve, fed = (k.sig(x) for x in ("turn_done", "turn_evac_act", "turn_evac_dve", "turn_fed"))
    with nc.Block() as block:
        @block.sync
        def _(sp):
            issue_chunks(k, sp, upto)

        @block.vector
        def _(dve):
            if before is not None:
                before(dve).then_inc(fed.sem, 1)
            for j in range(1, n, 2):
                dve.wait_ge(turned.sem, turned.base + j + 1)
                _, m, dst, gain = items[j]
                src = k.pb[j % 4][0:m, :]
                if gain is None:
                    nc.vector.tensor_copy(dst, src).then_inc(ev_dve.sem, 1)
                else:
                    nc.vector.tensor_scalar(dst, src, gain, None, ALU.mult).then_inc(ev_dve.sem, 1)

        @block.scalar
        def _(act):
            for j in range(0, n, 2):
                act.wait_ge(turned.sem, turned.base + j + 1)
                _, m, dst, gain = items[j]
                src = k.pb[j % 4][0:m, :]
                if gain is None:
                    nc.scalar.copy(dst, src).then_inc(ev_act.sem, 1)
                else:
                    nc.scalar.mul(dst, src, gain).then_inc(ev_act.sem, 1)

        @block.tensor
        def _(pe):
            if before is not None:
                pe.wait_ge(fed.sem, fed.base + 1)
            for j, (srcs, m, dst, gain) in enumerate(items):
                if j >= 4:
                    ev = (ev_act, ev_dve)[j % 2]
                    pe.wait_ge(ev.sem, ev.base + (j - 4) // 2 + 1)
                for t, s in enumerate(srcs):
                    last = nc.tensor.transpose(k.pb[j % 4][0:m, t * P:(t + 1) * P], s, k.ident[:, :])
                last.then_inc(turned.sem, 1)
    turned.base += n
    ev_act.base += (n + 1) // 2
    ev_dve.base += n // 2
    fed.base += 1 if before is not None else 0


def rotate(k, dve, x1, x2, cos, sin, tmp):
    v, s = k.nc.vector, k.sig("dve_chain")
    link = Chain(dve, s)
    for dst, a, b in ((tmp[0], x1, cos), (tmp[1], x2, sin), (tmp[2], x2, cos)):
        v.tensor_tensor(dst, a, b, ALU.mult)
    link(v.tensor_tensor(tmp[3], x1, sin, ALU.mult))
    v.tensor_tensor(x1, tmp[0], tmp[1], ALU.subtract)
    return v.tensor_tensor(x2, tmp[2], tmp[3], ALU.add)


def stage_residual(k, tag, y, gain_name, tmp_kb, upto, out=None):
    nc, d = k.nc, k.d
    sq, root, g_in, scaled, added = (k.sig(x) for x in ("res_sumsq", "res_root", "res_gain", "res_scaled", "res_added"))
    gain = k.sb(f"resgain_{tag}", tmp_kb, [P, D])
    tmp = k.sb(f"restmp_{tag}", tmp_kb + 4, [P, 2, D])
    ms, rs, half = k.stat[:, 0:T], k.stat[:, T:2 * T], k.stat[:, 2 * T:3 * T]
    stored = k.sig("stored")
    with nc.Block() as block:
        @block.sync
        def _(sp):
            sp.dma_start(gain[:, :], d[gain_name].rearrange("(a n) -> a n", a=1).to_broadcast([P, D])).then_inc(g_in.sem, 16)
            issue_chunks(k, sp, upto)
            if out is not None:
                for t in range(T):
                    sp.wait_ge(added.sem, added.base + t + 1)
                    sp.dma_start(out[t * P:(t + 1) * P, :], k.h[:, t, :]).then_inc(stored.sem, 16)
                sp.wait_ge(stored.sem, 16 * T)

        @block.scalar
        def _(act):
            for t in range(T):
                nc.scalar.activation(tmp[:, 0, :], y[:, t, :], ACT.Square,
                                     accum_out=k.stat[:, t:t + 1]).then_inc(sq.sem, 1)
                act.wait_ge(sq.sem, sq.base + t + 1)

        @block.gpsimd
        def _(pool):
            pool.wait_ge(root.sem, root.base + 2)
            nc.gpsimd.tensor_tensor(rs, ms, half, ALU.pow).then_inc(root.sem, 1)

        @block.vector
        def _(dve):
            nc.vector.memset(half, -0.5).then_inc(root.sem, 1)
            dve.wait_ge(sq.sem, sq.base + T)
            nc.vector.tensor_scalar(ms, ms, 1.0 / D, EPS, ALU.mult, ALU.add).then_inc(root.sem, 1)
            dve.wait_ge(root.sem, root.base + 3)
            dve.wait_ge(g_in.sem, g_in.base + 16)
            for t in range(T):
                if t >= 2:
                    dve.wait_ge(added.sem, added.base + t - 1)
                nc.vector.scalar_tensor_tensor(out=tmp[:, t % 2, :], in0=y[:, t, :], scalar=rs[:, t:t + 1],
                                               in1=gain[:, :], op0=ALU.mult, op1=ALU.mult).then_inc(scaled.sem, 1)
                dve.wait_ge(scaled.sem, scaled.base + t + 1)
                nc.vector.tensor_tensor(k.h[:, t, :], k.h[:, t, :], tmp[:, t % 2, :], ALU.add).then_inc(added.sem, 1)
    sq.base += T
    root.base += 3
    g_in.base += 16
    scaled.base += T
    added.base += T


def gemm_tokens(k, chunk, kt, lhs, cols, j0, width=512):
    steps = []
    j = j0
    for c0, n, perm in cols:
        for t in range(T):
            pairs = [(lhs(perm, f, t), slot(k, chunk, f * width + c0, f * width + c0 + n)) for f in range(kt)]
            steps.append((chunk, j, k.pb[j % 4][:, 0:n], pairs, True, True))
            j += 1
    return steps, j


def gemm_features(k, chunk, kt, rhs, cols, j0, width=512, m=P):
    steps = []
    j = j0
    for c0 in cols:
        pairs = [(slot(k, chunk, f * width + c0, f * width + c0 + m), rhs[:, f, :]) for f in range(kt)]
        steps.append((chunk, j, k.pb[j % 4][0:m, :], pairs, True, True))
        j += 1
    return steps, j


def first_block(k):
    nc, d = k.nc, k.d
    g = 0
    stage_norm_T(k, "x", k.h, D, "mix_pre", k.xT, 190)

    qk = k.sb("qkA", 72, [P, 3, T, 512])
    v = k.sb("vA", 96, [P, 3, T, 256])
    kvc = k.sb("kvc", 108, [P, T, 256])
    qc = k.sb("qc", 112, [P, T, 512])
    kpe = k.sb("kpe", 120, [P, T, 32])
    steps, dst, j = [], [], 0
    plan = [([(0, 512, 0)], [qk[:, 0]]), ([(0, 512, 1)], [qk[:, 1]]), ([(0, 512, 2)], [qk[:, 2]]),
            ([(0, 256, 0), (256, 256, 1)], [v[:, 0], v[:, 1]]), ([(0, 256, 2), (256, 256, 0)], [v[:, 2], kvc]),
            ([(0, 512, 0)], [qc])]
    lhs = lambda perm, f, t: tokens(k, perm, f, t)
    for cols, dsts in plan:
        s, j = gemm_tokens(k, g, KD, lhs, cols, j)
        steps += s
        for x in dsts:
            dst += [x[:, t, :] for t in range(T)]
        g += 1
    s, j = gemm_tokens(k, g, KD, lhs, [(0, 32, 0)], j, width=32)
    steps += s
    dst += [kpe[:, t, :] for t in range(T)]
    g += 1
    stage_gemm(k, steps, lambda who, eng, j, ps: copy_out(k, who, dst[j], ps), g + 2)

    gates = k.sb("gates", 121, [P, 16, S])
    steps, j = [], 0
    for _ in range(4):
        s, j = gemm_features(k, g, KD, k.xT, range(0, 512, P), j)
        steps += s
        g += 1
    stage_gates(k, steps, gates, g + 2)

    tmp = k.sb("ropetmp", 190, [P, 4, 3 * T, 8, 8])
    qh = qk[:, :, :, :].rearrange("p g t (h e) -> p (g t) h e", h=8)
    tab = k.ropeA[:, :, :, :].rearrange("p g t c -> p (g t) c")
    cos = tab[:, :, 0:8].unsqueeze(2).to_broadcast([P, 3 * T, 8, 8])
    sin = tab[:, :, 8:16].unsqueeze(2).to_broadcast([P, 3 * T, 8, 8])
    qkT = k.sb("qkT", 153, [P, 3, 4, S])
    items = [([qk[:, g_, t, f * P:(f + 1) * P] for t in range(T)], P, qkT[:, g_, f, :], None)
             for g_ in range(3) for f in range(4)]

    def rope_a(dve):
        return rotate(k, dve, qh[:, :, :, 0:8], qh[:, :, :, 8:16], cos, sin, [tmp[:, i] for i in range(4)])

    stage_turn(k, items, 0, rope_a)
    oA = k.sb("oA", 177, [P, 3, T, 260])
    batches, lse = [], []
    for grp in range(3):
        for h in range(A_HEADS):
            lo = DH * (h % 2)
            q, kk = qkT[lo:lo + DH, grp, h // 2, :], qkT[lo:lo + DH, grp, 2 + h // 2, :]
            if grp:
                mask = (k.mask_d4, k.mask_d16)[grp - 1]
                batches.append(dict(
                    segs=[(t * P, (t + 1) * P) for t in range(T)],
                    scores=[[(q[:, t * P:(t + 1) * P], kk[:, t * P:(t + 1) * P], t * P, (t + 1) * P),
                             (k.identb[:, :], mask[:, :], t * P, (t + 1) * P)] for t in range(T)],
                    values=[[v[:, grp, t, h * DH:(h + 1) * DH]] for t in range(T)],
                    out=oA[:, grp, :, h * DH:(h + 1) * DH]))
                lse.append((oA[:, grp, :, 256 + h], len(batches) - 1, T))
            else:
                for t in range(T):
                    a, b = max(t - 1, 0), min(t + 2, T)
                    w = (b - a) * P
                    m0 = (a - t + 1) * P
                    batches.append(dict(
                        segs=[(0, w)],
                        scores=[[(q[:, t * P:(t + 1) * P], kk[:, a * P:b * P], 0, w),
                                 (k.identb[:, :], k.mask_band[:, m0:m0 + w], 0, w)]],
                        values=[[v[:, grp, u, h * DH:(h + 1) * DH] for u in range(a, b)]],
                        out=oA[:, grp, t, h * DH:(h + 1) * DH]))
                    lse.append((oA[:, grp, t, 256 + h:257 + h], len(batches) - 1, 1))
    stage_attention(k, batches, DH ** -0.5, 190, 0, lse)
    mixAT = k.sb("mixAT", 200, [P, 2, S])
    stage_combine(k, oA)
    oc = k.oc
    stage_turn(k, [([oc[:, t, f * P:(f + 1) * P] for t in range(T)], P, mixAT[:, f, :], None) for f in range(2)])

    qcT = k.sb("qcT", 72, [P, 4, S])
    kvcT = k.sb("kvcT", 80, [P, 2, S])
    stage_norm_T(k, "qc", qc, 512, "q_norm", qcT, 190)
    stage_norm_T(k, "kvc", kvc, 256, "kv_norm", kvcT, 190)
    qB = k.sb("qB", 84, [P, T, 8, 96])
    kB = k.sb("kB", 96, [P, T, 8, 96])
    vB = k.sb("vB", 108, [P, T, 8, DH])
    steps, dst, j = [], [], 0
    s, j = gemm_tokens(k, g, 4, lambda perm, f, t: qcT[:, f, t * P:(t + 1) * P],
                       [(0, 384, 0), (384, 384, 0)], j, width=768)
    steps += s
    s, j = gemm_tokens(k, g + 1, 2, lambda perm, f, t: kvcT[:, f, t * P:(t + 1) * P],
                       [(0, 512, 0), (512, 512, 0)], j, width=1024)
    steps += s
    g += 2

    def evac_b(who, eng, j, ps):
        t, half = j % 4, (j // 4) % 2
        if j < 8:
            return copy_out(k, who, qB[:, t, half * 4:half * 4 + 4, :].rearrange("p h e -> p (h e)"), ps)
        kv = ps.rearrange("p (h e) -> p h e", h=4)
        copy_out(k, who, kB[:, t, half * 4:half * 4 + 4, 0:DH], kv[:, :, 0:DH])
        return copy_out(k, who, vB[:, t, half * 4:half * 4 + 4, :], kv[:, :, DH:])

    stage_gemm(k, steps, evac_b, g + 2)
    tmpq = k.sb("ropetmpq", 190, [P, 4, T, 8, 16])
    tmpk = k.sb("ropetmpk", 198, [P, 4, T, 16])
    qTb = k.sb("qTb", 153, [P, 8, S])
    kTb = k.sb("kTb", 169, [P, 8, S])

    def rope_b(dve):
        link = Chain(dve, k.sig("dve_chain"))
        cos, sin = k.ropeB[:, :, 0:16], k.ropeB[:, :, 16:32]
        rotate(k, dve, qB[:, :, :, 64:80], qB[:, :, :, 80:96], cos.unsqueeze(2).to_broadcast([P, T, 8, 16]),
               sin.unsqueeze(2).to_broadcast([P, T, 8, 16]), [tmpq[:, i] for i in range(4)])
        link(rotate(k, dve, kpe[:, :, 0:16], kpe[:, :, 16:32], cos, sin, [tmpk[:, i] for i in range(4)]))
        return nc.vector.tensor_copy(kB[:, :, :, DH:96], kpe[:, :, :].unsqueeze(2).to_broadcast([P, T, 8, 32]))

    items = []
    for h in range(B_HEADS):
        items.append(([qB[:, t, h, :] for t in range(T)], 96, qTb[0:96, h, :], None))
        items.append(([kB[:, t, h, :] for t in range(T)], 96, kTb[0:96, h, :], None))
    stage_turn(k, items, 0, rope_b)
    oB = k.sb("oB", 84, [P, T, 512])
    batches = []
    for t in range(T):
        for h in range(B_HEADS):
            batches.append(dict(
                segs=[(0, S)], scores=[[(qTb[0:96, h, t * P:(t + 1) * P], kTb[0:96, h, :], 0, S)]],
                values=[[vB[:, u, h, :] for u in range(T)]], out=oB[:, t, h * DH:(h + 1) * DH]))
    stage_attention(k, batches, B_QK ** -0.5, 190, 0)
    oBT = k.sb("oBT", 96, [P, 4, S])
    stage_turn(k, [([oB[:, t, f * P:(f + 1) * P] for t in range(T)], P, oBT[:, f, :], None) for f in range(4)])

    mixT = k.sb("mixT", 153, [P, KD, S])
    tmp2 = k.sb("gatetmp", 190, [P, 2, S])
    steps, j = [], 0
    for f in range(KD):
        steps.append((g, j, k.pb[j % 4][:, :],
                      [(slot(k, g, c * D + f * P, c * D + (f + 1) * P), mixAT[:, c, :]) for c in range(2)], True, True))
        steps.append((g + 1, j + 1, k.pb[(j + 1) % 4][:, :],
                      [(slot(k, g + 1, c * D + f * P, c * D + (f + 1) * P), oBT[:, c, :]) for c in range(4)], True, True))
        j += 2
    g += 2
    link2 = k.sig("dve_chain")
    fa = k.sig("gemm_free_act")

    def gated(who, eng, j, ps):
        f = j // 2
        if who == "act":
            return nc.scalar.copy(mixT[:, f, :], ps)
        link = Chain(eng, link2)
        nc.vector.tensor_tensor(tmp2[:, f % 2, :], ps, gates[:, 8 + f, :], ALU.mult)
        eng.wait_ge(fa.sem, fa.base + f + 1)
        link(nc.vector.tensor_tensor(mixT[:, f, :], mixT[:, f, :], gates[:, f, :], ALU.mult))
        return nc.vector.tensor_tensor(mixT[:, f, :], mixT[:, f, :], tmp2[:, f % 2, :], ALU.add)

    stage_gemm(k, steps, gated, g + 2)
    y = k.sb("y1", 72, [P, T, D])
    g = stage_out_product(k, g, mixT, y)
    stage_residual(k, "mix1", y, "norm_mix_post", 88, 0)

    stage_norm_T(k, "h1", k.h, D, "mlp_pre", k.xT, 190)
    hid = k.sb("hid1", 88, [P, FF1 // P, S])
    steps, j = [], 0
    for _ in range(8):
        s, j = gemm_features(k, g, KD, k.xT, range(0, 512, P), j)
        steps += s
        g += 1

    def relu2(who, eng, j, ps):
        if who == "act":
            nc.scalar.activation(hid[:, j, :], ps, ACT.Relu).then_inc(k.sig("act_chain").sem, 1)
            k.sig("act_chain").base += 1
            eng.wait_ge(k.sig("act_chain").sem, k.sig("act_chain").base)
            return nc.scalar.activation(hid[:, j, :], hid[:, j, :], ACT.Square)
        Chain(eng, link2)(nc.vector.tensor_scalar(hid[:, j, :], ps, 0.0, None, ALU.max))
        return nc.vector.tensor_tensor(hid[:, j, :], hid[:, j, :], hid[:, j, :], ALU.mult)

    stage_gemm(k, steps, relu2, g + 2)
    y = k.sb("y2", 72, [P, T, D])
    g = stage_down_product(k, g, hid, FF1 // P, y)
    stage_residual(k, "mlp1", y, "norm_mlp_post", 88, 0)
    k.g = g
    return None


def stage_gates(k, steps, gates, upto):
    nc = k.nc
    done, free = k.sig("gates_done"), k.sig("gates_free")
    n = len(steps)
    note_freed(k, steps, done)
    with nc.Block() as block:
        @block.sync
        def _(sp):
            issue_chunks(k, sp, upto)

        @block.tensor
        def _(pe):
            seen = set()
            for i, (g, j, out, pairs, first, last) in enumerate(steps):
                if g not in seen:
                    seen.add(g)
                    wait_chunk(k, pe, g)
                if j >= 4:
                    pe.wait_ge(free.sem, free.base + j - 3)
                for m, (a, b) in enumerate(pairs):
                    mm = nc.tensor.matmul(out, a, b, start=m == 0, stop=m == len(pairs) - 1)
                mm.then_inc(done.sem, 1)

        @block.scalar
        def _(act):
            for j in range(n):
                act.wait_ge(done.sem, done.base + j + 1)
                nc.scalar.activation(gates[:, j, :], steps[j][2], ACT.Sigmoid,
                                     bias=col(k, "b_gate", j)).then_inc(free.sem, 1)
    done.base += n
    free.base += n


def stage_out_product(k, g, lhs, y):
    steps, j = [], 0
    for _ in range(2):
        s, j = gemm_tokens(k, g, KD, lambda perm, f, t: lhs[:, f, t * P:(t + 1) * P], [(0, 512, 0)], j)
        steps += s
        g += 1
    stage_gemm(k, steps, lambda who, eng, j, ps: copy_out(k, who, y[:, j % T, (j // T) * 512:(j // T) * 512 + 512], ps),
               g + 2)
    return g


def stage_down_product(k, g, hid, kt, y):
    steps = []
    for c in range(2):
        for k0 in range(0, kt, 8):
            k1 = min(k0 + 8, kt)
            for t in range(T):
                j = c * T + t
                pairs = [(hid[:, f, t * P:(t + 1) * P], slot(k, g, (f - k0) * 512, (f - k0 + 1) * 512))
                         for f in range(k0, k1)]
                steps.append((g, j, k.pb[j % 4][:, :], pairs, k0 == 0, k1 == kt))
            g += 1
    stage_gemm(k, steps, lambda who, eng, j, ps: copy_out(k, who, y[:, j % T, (j // T) * 512:(j // T) * 512 + 512], ps),
               g + 2)
    return g


def stage_combine(k, oA):
    nc, d = k.nc, k.d
    sent, back, done = k.sig("combine_sent"), k.sig("combine_back"), k.sig("combine_done")
    W = 260
    nat = k.sb("natA", 72, [P, 2, T, W])
    oc = k.sb("oc", 82, [P, T, 256])
    t2 = k.sb("combtmp", 86, [P, T, 256])
    w3 = k.sb("w3", 90, [P, 3, T, 4])
    mxw = k.sb("mxw", 90.5, [P, T, 4])
    sumw = k.sb("sumw", 91, [P, T, 4])
    k.oc = oc
    scr = d["scratch"]
    with nc.Block() as block:
        @block.sync
        def _(sp):
            n = 0
            for t in range(T):
                for i in range(2):
                    sp.dma_start(scr[i, t::T, :], oA[:, 1 + i, t, :]).then_inc(sent.sem, 16)
                    n += 1
            sp.wait_ge(sent.sem, 16 * n)
            for i in range(2):
                sp.dma_start(nat[:, i, :, :], scr[i].rearrange("(t p) n -> p t n", p=P)).then_inc(back.sem, 16)

        @block.vector
        def _(dve):
            link = Chain(dve, k.sig("dve_chain"))
            v = nc.vector
            dve.wait_ge(back.sem, 32)
            src = [oA[:, 0, :, :], nat[:, 0, :, :], nat[:, 1, :, :]]
            ls = [s[:, :, 256:260] for s in src]
            link(v.tensor_tensor(mxw[:, :, :], ls[0], ls[1], ALU.max))
            link(v.tensor_tensor(mxw[:, :, :], mxw[:, :, :], ls[2], ALU.max))
            for i in range(3):
                v.tensor_tensor(w3[:, i], ls[i], mxw[:, :, :], ALU.subtract).then_inc(done.sem, 1)
            dve.wait_ge(done.sem, 4)
            link(v.tensor_tensor(sumw[:, :, :], w3[:, 0], w3[:, 1], ALU.add))
            link(v.tensor_tensor(sumw[:, :, :], sumw[:, :, :], w3[:, 2], ALU.add))
            link(v.reciprocal(sumw[:, :, :], sumw[:, :, :]))
            link(v.tensor_tensor(w3[:, :, :, :], w3[:, :, :, :],
                                 sumw[:, :, :].unsqueeze(1).to_broadcast([P, 3, T, 4]), ALU.mult))
            for i in range(3):
                dst = (oc if i == 0 else t2)[:, :, :].rearrange("p t (h e) -> p (t h) e", h=4)
                link(v.tensor_tensor(
                    dst.rearrange("p (t h) e -> p t h e", t=T), src[i][:, :, 0:256].rearrange("p t (h e) -> p t h e", h=4),
                    w3[:, i].unsqueeze(3).to_broadcast([P, T, 4, DH]), ALU.mult))
                if i:
                    link(v.tensor_tensor(oc[:, :, :], oc[:, :, :], t2[:, :, :], ALU.add))

        @block.scalar
        def _(act):
            act.wait_ge(done.sem, 3)
            nc.scalar.activation(w3[:, :, :, :], w3[:, :, :, :], ACT.Exp).then_inc(done.sem, 1)


def second_block(k, out):
    nc, d, g = k.nc, k.d, k.g
    stage_norm_T(k, "h2", k.h, D, "mix_pre2", k.xT, 190)

    s5 = stage_s5_parameters(k)

    fm = k.sb("fm", 72, [P, 14, S])
    grow = k.sb("grow", 100, [P, 3, S])
    tm = k.sb("tm", 106, [P, 5, T, 256])
    steps, j = [], 0
    for c in range(4):
        cols = range(0, 512, P) if c < 3 else range(0, 256, P)
        w = 512 if c < 3 else 352
        s, j = gemm_features(k, g, KD, k.xT, cols, j, width=w)
        steps += s
        if c == 3:
            s, j = gemm_features(k, g, KD, k.xT, [256], j, width=w, m=96)
            steps += s
        g += 1
    j_tm = j
    lhs = lambda perm, f, t: tokens(k, 0, f, t)
    for c in range(3):
        s, j = gemm_tokens(k, g, KD, lhs, [(0, 256, 0), (256, 256, 0)] if c < 2 else [(0, 256, 0)], j,
                           width=512 if c < 2 else 256)
        steps += s
        g += 1
    FOX_Q = 6

    def evac(who, eng, j, ps):
        if j < 14:
            if FOX_Q <= j < FOX_Q + 2:
                return (nc.scalar.mul(fm[:, j, :], ps, DH ** -0.5) if who == "act" else
                        nc.vector.tensor_scalar(fm[:, j, :], ps, DH ** -0.5, None, ALU.mult))
            return copy_out(k, who, fm[:, j, :], ps)
        if j == 14:
            for i in range(3):
                x = nc.scalar.activation(grow[0:4, i, :], ps[32 * i:32 * i + 4, :], ACT.Identity,
                                         bias=col(k, "gate_b", i)[0:4, :])
            return x
        i = j - j_tm
        return copy_out(k, who, tm[:, i // T, i % T, :], ps)

    stage_gemm(k, steps, evac, g + 2)
    k.fm, k.grow, k.tm = fm, grow, tm
    k.ycat = k.sb("ycat", 126, [P, T, D])
    k.sel = k.sb("sel", 142, [P, 4, S])
    g = stage_s5(k, s5, g)
    stage_gate_rows(k)
    stage_fox(k)
    stage_mlstm(k)
    stage_hgrn(k)
    stage_finish(k)
    ycT = k.sb("ycT", 72, [P, KD, S])
    stage_turn(k, [([k.ycat[:, t, f * P:(f + 1) * P] for t in range(T)], P, ycT[:, f, :], col(k, "mix_gain2", f))
                   for f in range(KD)])
    y = k.sb("y3", 88, [P, T, D])
    g = stage_out_product(k, g, ycT, y)
    stage_residual(k, "mix2", y, "ln_mix_post_2", 104, 0)
    stage_norm_T(k, "h3", k.h, D, "ffn_pre2", k.xT, 190)
    KF = FF2 // P
    hid = k.sb("hid2", 88, [P, KF, S])
    sg = k.sb("sg2", 133, [P, 2, S])
    steps, j = [], 0
    for _ in range(KF // 2):
        s, j = gemm_features(k, g, KD, k.xT, (0, 256, 128, 384), j)
        steps += s
        g += 1
    stage_swiglu(k, steps, hid, sg, g + 2)
    y = k.sb("y4", 72, [P, T, D])
    g = stage_down_product(k, g, hid, KF, y)
    stage_residual(k, "mlp2", y, "ln_ffn_post_2", 140, 0, out=out[0])
    return None


def stage_swiglu(k, steps, hid, sg, upto):
    nc = k.nc
    done, sgd, free = k.sig("glu_done"), k.sig("glu_sigmoid"), k.sig("glu_free")
    n = len(steps) // 2
    note_freed(k, steps, done)
    link = k.sig("dve_chain")
    with nc.Block() as block:
        @block.sync
        def _(sp):
            issue_chunks(k, sp, upto)

        @block.tensor
        def _(pe):
            seen = set()
            for g, j, out, pairs, first, last in steps:
                if g not in seen:
                    seen.add(g)
                    wait_chunk(k, pe, g)
                if j >= 4 and j % 2 == 0:
                    pe.wait_ge(free.sem, free.base + j // 2 - 1)
                for m, (a, b) in enumerate(pairs):
                    mm = nc.tensor.matmul(out, a, b, start=m == 0, stop=m == len(pairs) - 1)
                mm.then_inc(done.sem, 1)

        @block.scalar
        def _(act):
            for f in range(n):
                act.wait_ge(done.sem, done.base + 2 * f + 1)
                if f >= 2:
                    act.wait_ge(free.sem, free.base + f - 1)
                nc.scalar.activation(sg[:, f % 2, :], k.pb[(2 * f) % 4][:, :], ACT.Sigmoid).then_inc(sgd.sem, 1)

        @block.vector
        def _(dve):
            chain = Chain(dve, link)
            for f in range(n):
                dve.wait_ge(sgd.sem, sgd.base + f + 1)
                chain(nc.vector.tensor_tensor(hid[:, f, :], sg[:, f % 2, :], k.pb[(2 * f) % 4][:, :], ALU.mult))
                dve.wait_ge(done.sem, done.base + 2 * f + 2)
                nc.vector.tensor_tensor(hid[:, f, :], hid[:, f, :], k.pb[(2 * f + 1) % 4][:, :],
                                        ALU.mult).then_inc(free.sem, 1)
    done.base += 2 * n
    sgd.base += n
    free.base += n


def stage_s5_parameters(k):
    nc, d = k.nc, k.d
    v, a = nc.vector, nc.scalar
    sm = k.sb("s5_small", 176, [P, 24, 8])
    er, ei = k.sb("s5_er", 142, [P, 8, S]), k.sb("s5_ei", 158, [P, 8, S])
    br, bi = k.sb("s5_b_re", 177, [P, 8, 32]), k.sb("s5_b_im", 178, [P, 8, 32])
    bb = k.sb("s5_bb", 179, [P, 2, 8, 32])
    bt = k.sb("s5_bt", 181, [P, 2, 8, 32])
    bT = k.sb("s5_bT", 183, [P, 2, 2, P])
    cT = k.sb("s5_cT", 185, [P, 4, 8, 32])
    tmp = k.sb("s5_tmp", 189, [P, 2, 8, 256])
    (DT, LR, MAG, TH, N1, RE, SN, AB, CS, AR, AI, DEN, A1, T1, T2, CR, CI, WR, WI, W2, W3) = [
        sm[:, i, :] for i in range(21)]
    p_in, hand = k.sig("s5_in"), k.sig("s5_hand")
    s = k.sig("dve_chain")
    h0 = hand.base
    turned = k.sig("s5_turned")
    PI = float(np.pi)
    with nc.Block() as block:
        @block.sync
        def _(sp):
            for dst, n in ((br, "s5_b_re"), (bi, "s5_b_im")):
                sp.dma_start(dst[:, :, :], d[n]).then_inc(p_in.sem, 16)
            sp.dma_start(cT[:, 0:2, :, :], d["s5_cT"]).then_inc(p_in.sem, 16)

        @block.scalar
        def _(act):
            a.activation(DT, col(k, "log_dt", 0, 8), ACT.Exp).then_inc(hand.sem, 1)
            act.wait_ge(hand.sem, h0 + 2)
            a.activation(MAG, MAG, ACT.Exp).then_inc(hand.sem, 1)
            a.activation(SN, RE, ACT.Sin).then_inc(hand.sem, 1)
            a.activation(CS, AB, ACT.Sin).then_inc(hand.sem, 1)

        @block.vector
        def _(dve):
            link = Chain(dve, s)
            tt, ts = v.tensor_tensor, v.tensor_scalar
            link(ts(LR, col(k, "lam_re", 0, 8), -1e-4, None, ALU.min))
            dve.wait_ge(hand.sem, h0 + 1)
            tt(MAG, LR, DT, ALU.mult)
            link(tt(TH, col(k, "lam_im", 0, 8), DT, ALU.mult))
            link(ts(N1, TH, 1.0 / (2 * PI), 12582912.0, ALU.mult, ALU.add))
            link(ts(N1, N1, 12582912.0, None, ALU.subtract))
            link(v.scalar_tensor_tensor(out=RE, in0=N1, scalar=-6.28125, in1=TH, op0=ALU.mult, op1=ALU.add))
            c2 = float(np.float32(np.round((2 * np.pi - 6.28125) * 2 ** 22) / 2 ** 22))
            link(v.scalar_tensor_tensor(out=RE, in0=N1, scalar=-c2, in1=RE, op0=ALU.mult, op1=ALU.add))
            link(v.scalar_tensor_tensor(out=RE, in0=N1, scalar=-float(2 * np.pi - 6.28125 - c2), in1=RE,
                                        op0=ALU.mult, op1=ALU.add))
            link(ts(RE, RE, 3.1415925, -3.1415925, ALU.min, ALU.max))
            link(ts(AB, RE, -1.0, None, ALU.mult))
            link(tt(AB, AB, RE, ALU.max))
            ts(AB, AB, -1.0, PI / 2, ALU.mult, ALU.add).then_inc(hand.sem, 1)
            dve.wait_ge(hand.sem, h0 + 5)
            tt(AR, MAG, CS, ALU.mult)
            link(tt(AI, MAG, SN, ALU.mult))
            li = col(k, "lam_im", 0, 8)
            tt(T1, LR, LR, ALU.mult)
            link(tt(T2, li, li, ALU.mult))
            link(tt(DEN, T1, T2, ALU.add))
            link(v.reciprocal(DEN, DEN))
            link(ts(A1, AR, -1.0, None, ALU.add))
            tt(T1, A1, LR, ALU.mult)
            link(tt(T2, AI, li, ALU.mult))
            link(tt(CR, T1, T2, ALU.add))
            tt(CR, CR, DEN, ALU.mult)
            tt(T1, AI, LR, ALU.mult)
            link(tt(T2, A1, li, ALU.mult))
            link(tt(CI, T1, T2, ALU.subtract))
            link(tt(CI, CI, DEN, ALU.mult))
            dve.wait_ge(p_in.sem, p_in.base + 48)
            crb, cib = (c.unsqueeze(2).to_broadcast([P, 8, 32]) for c in (CR, CI))
            tt(bb[:, 0], br[:, :, :], crb, ALU.mult)
            tt(bb[:, 1], bi[:, :, :], crb, ALU.mult)
            tt(bt[:, 0], bi[:, :, :], cib, ALU.mult)
            link(tt(bt[:, 1], br[:, :, :], cib, ALU.mult))
            link(tt(bb[:, 0], bb[:, 0], bt[:, 0], ALU.subtract))
            tt(bb[:, 1], bb[:, 1], bt[:, 1], ALU.add).then_inc(turned.sem, 1)
            ts(cT[:, 2], cT[:, 1], -1.0, None, ALU.mult)
            ts(cT[:, 3], cT[:, 0], -1.0, None, ALU.mult)
            for c in range(2):
                for jj in range(2):
                    dve.wait_ge(turned.sem, turned.base + 2 + 2 * c + jj)
                    v.tensor_copy(bT[:, c, jj, :], k.pb[c * 2 + jj][:, 0:P])
            v.memset(er[:, :, 0:1], 1.0)
            v.memset(ei[:, :, 0:1], 0.0)
            v.tensor_copy(WR, CS)
            link(v.tensor_copy(WI, SN))
            n = 1
            while n < S:
                wr, wi = (w.unsqueeze(2).to_broadcast([P, 8, n]) for w in (WR, WI))
                t0, t1 = tmp[:, 0, :, 0:n], tmp[:, 1, :, 0:n]
                tt(t0, er[:, :, 0:n], wr, ALU.mult)
                link(tt(t1, ei[:, :, 0:n], wi, ALU.mult))
                link(tt(er[:, :, n:2 * n], t0, t1, ALU.subtract))
                tt(t0, er[:, :, 0:n], wi, ALU.mult)
                link(tt(t1, ei[:, :, 0:n], wr, ALU.mult))
                tt(ei[:, :, n:2 * n], t0, t1, ALU.add)
                tt(T1, WR, WR, ALU.mult)
                tt(T2, WI, WI, ALU.mult)
                link(tt(W2, WR, WI, ALU.mult))
                link(tt(WR, T1, T2, ALU.subtract))
                link(ts(WI, W2, 2.0, None, ALU.mult))
                n *= 2

        @block.tensor
        def _(pe):
            pe.wait_ge(turned.sem, turned.base + 1)
            for c in range(2):
                for jj in range(2):
                    nc.tensor.transpose(k.pb[c * 2 + jj][:, 0:P],
                                        bb[:, c, 4 * jj:4 * jj + 4, :].rearrange("p j c -> p (j c)"),
                                        k.ident[:, :]).then_inc(turned.sem, 1)
    p_in.base += 48
    hand.base += 5
    turned.base += 5
    return dict(mag=MAG, er=er, ei=ei, bT=bT, cT=cT)


def stage_s5(k, s5, g):
    nc, d = k.nc, k.d
    er, ei, bT, cT, mag = s5["er"], s5["ei"], s5["bT"], s5["cT"], s5["mag"]
    pr = k.sb("s5_pr", 16, [P, 4, S])
    vv = k.sb("s5_v", 24, [P, 2, S])
    yy = k.sb("s5_y", 28, [P, 2, S])
    qq = k.sb("s5_q", 190, [P, 2, 4, S])
    yS = k.sb("s5_yS", 177, [P, 2, S])
    bu, scanned, prod, out_done, outp = (k.sig(x) for x in ("s5_bu", "s5_scan", "s5_prod", "s5_out", "s5_bu_free"))
    chain = k.sig("dve_chain")
    uT = k.fm[:, 0:2, :]
    with nc.Block() as block:
        @block.tensor
        def _(pe):
            def inject(j):
                q = 32 * (j % 4)
                if j >= 2:
                    pe.wait_ge(outp.sem, outp.base + j - 1)
                for c in range(2):
                    mm = nc.tensor.matmul(k.pb[2 * (j % 2) + c][:, :], bT[q:q + 32, c, j // 4, :],
                                          uT[q:q + 32, j // 4, :], start=True, stop=True,
                                          tile_position=(q, 0))
                mm.then_inc(bu.sem, 1)

            def project(j):
                q = 32 * (j % 4)
                pe.wait_ge(prod.sem, prod.base + j + 1)
                for m, c in enumerate((0, 3, 2, 2)):
                    mm = nc.tensor.matmul(k.pb[6 + j // 4][q:q + 32, :], cT[:, c, j, :],
                                          qq[:, j % 2, m, :], start=m == 0, stop=m == 3,
                                          tile_position=(0, q), skip_group_check=True)
                mm.then_inc(out_done.sem, 1)

            for j in range(9):
                if j < 8:
                    inject(j)
                if j >= 1:
                    project(j - 1)

        @block.vector
        def _(dve):
            v = nc.vector
            link = Chain(dve, chain)
            for j in range(8):
                dve.wait_ge(bu.sem, bu.base + j + 1)
                r, i = k.pb[2 * (j % 2)][:, :], k.pb[2 * (j % 2) + 1][:, :]
                v.tensor_tensor(pr[:, 0, :], er[:, j, :], r, ALU.mult)
                v.tensor_tensor(pr[:, 1, :], ei[:, j, :], i, ALU.mult)
                v.tensor_tensor(pr[:, 2, :], er[:, j, :], i, ALU.mult)
                x = v.tensor_tensor(pr[:, 3, :], ei[:, j, :], r, ALU.mult)
                x.then_inc(outp.sem, 1)
                dve.wait_ge(outp.sem, outp.base + j + 1)
                v.tensor_tensor(vv[:, 0, :], pr[:, 0, :], pr[:, 1, :], ALU.add)
                link(v.tensor_tensor(vv[:, 1, :], pr[:, 2, :], pr[:, 3, :], ALU.subtract))
                if j >= 1:
                    dve.wait_ge(prod.sem, prod.base + j)
                m = mag[:, j:j + 1].to_broadcast([P, S])
                v.tensor_tensor_scan(yy[:, 0, :], m, vv[:, 0, :], 0.0, ALU.mult, ALU.add)
                v.tensor_tensor_scan(yy[:, 1, :], m, vv[:, 1, :], 0.0, ALU.mult, ALU.add).then_inc(scanned.sem, 1)
            dve.wait_ge(out_done.sem, out_done.base + 8)
            for f in range(2):
                v.scalar_tensor_tensor(out=yS[:, f, :], in0=uT[:, f, :], scalar=col(k, "s5_d", f),
                                       in1=k.pb[6 + f][:, :], op0=ALU.mult, op1=ALU.add)

        @block.gpsimd
        def _(pool):
            for j in range(8):
                pool.wait_ge(scanned.sem, scanned.base + j + 1)
                if j >= 2:
                    pool.wait_ge(out_done.sem, out_done.base + j - 1)
                nc.gpsimd.tensor_tensor(qq[:, j % 2, 0, :], yy[:, 0, :], er[:, j, :], ALU.mult)
                nc.gpsimd.tensor_tensor(qq[:, j % 2, 1, :], yy[:, 1, :], ei[:, j, :], ALU.mult)
                nc.gpsimd.tensor_tensor(qq[:, j % 2, 2, :], yy[:, 0, :], ei[:, j, :], ALU.mult)
                nc.gpsimd.tensor_tensor(qq[:, j % 2, 3, :], yy[:, 1, :], er[:, j, :], ALU.mult).then_inc(prod.sem, 1)
    for s in (bu, scanned, prod, out_done, outp):
        s.base += 8

    t1 = k.sb("s5_g1", 16, [P, 2, S])
    gT = k.sb("s5_g", 20, [P, 2, S])
    sgd = k.sb("s5_sg", 24, [P, T, 256])
    hand = k.sig("s5_gelu")
    free = k.sig("s5_glu")
    turned = k.sig("s5_turned")
    k.freed[g] = (free.sem, free.base + T)
    with nc.Block() as block:
        @block.sync
        def _(sp):
            issue_chunks(k, sp, g + 2)

        @block.vector
        def _(dve):
            v = nc.vector
            link = Chain(dve, chain)
            link(v.tensor_tensor(t1[:, :, :], yS[:, :, :], yS[:, :, :], ALU.mult))
            link(v.tensor_scalar(t1[:, :, :], t1[:, :, :], 0.044715, 1.0, ALU.mult, ALU.add))
            v.tensor_tensor(t1[:, :, :], t1[:, :, :], yS[:, :, :], ALU.mult).then_inc(hand.sem, 1)
            dve.wait_ge(hand.sem, hand.base + 2)
            v.tensor_tensor(gT[:, :, :], yS[:, :, :], t1[:, :, :], ALU.mult).then_inc(hand.sem, 1)
            dve.wait_ge(hand.sem, hand.base + 3 + T)
            dve.wait_ge(turned.sem, turned.base + T)
            for t in range(T):
                v.tensor_tensor(k.ycat[:, t, 0:256], sgd[:, t, :], k.pb[4 + t // 2][:, (t % 2) * 256:(t % 2) * 256 + 256],
                                ALU.mult)

        @block.scalar
        def _(act):
            act.wait_ge(hand.sem, hand.base + 1)
            nc.scalar.activation(t1[:, :, :], t1[:, :, :], ACT.Sigmoid,
                                 scale=2.0 * float(np.sqrt(2.0 / np.pi))).then_inc(hand.sem, 1)
            for t in range(T):
                act.wait_ge(free.sem, free.base + t + 1)
                nc.scalar.activation(sgd[:, t, :], k.pb[t][:, 0:256], ACT.Sigmoid).then_inc(hand.sem, 1)

        @block.tensor
        def _(pe):
            pe.wait_ge(hand.sem, hand.base + 3)
            wait_chunk(k, pe, g)
            for t in range(T):
                for f in range(2):
                    mm = nc.tensor.matmul(k.pb[t][:, 0:256], gT[:, f, t * P:(t + 1) * P],
                                          slot(k, g, f * 256, f * 256 + 256), start=f == 0, stop=f == 1)
                mm.then_inc(free.sem, 1)
            for t in range(T):
                for f in range(2):
                    c = (t % 2) * 256 + f * P
                    mm = nc.tensor.transpose(k.pb[4 + t // 2][:, c:c + P], gT[:, f, t * P:(t + 1) * P], k.ident[:, :])
                mm.then_inc(turned.sem, 1)
    hand.base += 3 + T
    free.base += T
    turned.base += T
    return g + 1


def stage_gate_rows(k):
    nc, d = k.nc, k.d
    grow = k.grow
    rows = k.rows = k.sb("rows", 150, [P, 5, S])
    e = k.sb("rows_e", 160, [P, 2, S])
    mn = k.sb("rows_mn", 164, [P, 2, S])
    zero = k.sb("rows_zero", 168, [P, S])
    k.acol = k.sb("acol", 170, [P, T, 4])
    k.mcol = k.sb("mcol", 170.25, [P, T, 4])
    s_in, hand = k.sig("rows_in"), k.sig("rows_hand")
    chain = k.sig("dve_chain")
    with nc.Block() as block:
        @block.sync
        def _(sp):
            sp.dma_start(k.sel[0:4, :, :], d["sel"]).then_inc(s_in.sem, 16)
            sp.wait_ge(s_in.sem, s_in.base + 16)

        @block.scalar
        def _(act):
            act.wait_ge(hand.sem, hand.base + 1)
            nc.scalar.activation(e[0:4, :, :], e[0:4, :, :], ACT.Exp).then_inc(hand.sem, 1)
            act.wait_ge(hand.sem, hand.base + 2)
            nc.scalar.activation(e[0:4, :, :], e[0:4, :, :], ACT.Ln, bias=1.0).then_inc(hand.sem, 1)

        @block.vector
        def _(dve):
            v = nc.vector
            link = Chain(dve, chain)
            z = grow[0:4, 0::2, :]
            en, m = e[0:4, :, :], mn[0:4, :, :]
            v.memset(zero[0:4, :], 0.0)
            v.tensor_scalar(m, z, 0.0, None, ALU.min)
            link(v.tensor_scalar(en, z, -1.0, None, ALU.mult))
            v.tensor_tensor(en, en, z, ALU.min).then_inc(hand.sem, 1)
            dve.wait_ge(hand.sem, hand.base + 3)
            link(v.tensor_tensor(m, m, en, ALU.subtract))
            R = [rows[0:4, i, :] for i in range(5)]
            zz = zero[0:4, :]
            v.tensor_tensor_scan(R[0], m[:, 0, :], zz, 0.0, ALU.add, ALU.add)
            link(v.tensor_tensor_scan(e[0:4, 0, :], m[:, 1, :], zz, 0.0, ALU.add, ALU.add))
            v.tensor_scalar(R[1], R[0], -1.0, None, ALU.mult)
            link(v.tensor_tensor(R[2], grow[0:4, 1, :], e[0:4, 0, :], ALU.subtract))
            link(v.tensor_tensor_scan(e[0:4, 1, :], R[2], zz, 0.0, ALU.max, ALU.max))
            v.tensor_scalar(R[3], e[0:4, 1, :], -1.0, None, ALU.mult)
            link(v.tensor_tensor(e[0:4, 1, :], e[0:4, 1, :], e[0:4, 0, :], ALU.add))
            v.tensor_scalar(R[4], e[0:4, 1, :], -1.0, None, ALU.mult).then_inc(hand.sem, 1)

        @block.tensor
        def _(pe):
            pe.wait_ge(hand.sem, hand.base + 4)
            for t in range(T):
                nc.tensor.transpose(k.pb[0][:, 4 * t:4 * t + 4], rows[0:4, 2, t * P:(t + 1) * P], k.ident[0:4, 0:4])
                mm = nc.tensor.transpose(k.pb[1][:, 4 * t:4 * t + 4], rows[0:4, 4, t * P:(t + 1) * P],
                                         k.ident[0:4, 0:4])
            mm.then_inc(hand.sem, 1)
    hand.base += 5
    s_in.base += 16
    with nc.Block() as block:
        @block.scalar
        def _(act):
            nc.scalar.activation(k.mcol[:, :, :].rearrange("p t h -> p (t h)"), k.pb[1][:, 0:16], ACT.Exp)

        @block.vector
        def _(dve):
            nc.vector.tensor_copy(k.acol[:, :, :].rearrange("p t h -> p (t h)"), k.pb[0][:, 0:16])


def stage_fox(k):
    batches = []
    for h in range(4):
        lo = DH * (h % 2)
        q, kk = k.fm[lo:lo + DH, 6 + h // 2, :], k.fm[lo:lo + DH, 8 + h // 2, :]
        for t in range(T):
            w = (t + 1) * P
            batches.append(dict(
                segs=[(0, w)],
                scores=[[(q[:, t * P:w], kk[:, 0:w], 0, w),
                         (k.rows[0:4, 0, t * P:w], k.sel[0:4, h, 0:w], 0, w),
                         (k.sel[0:4, h, 0:P], k.rows[0:4, 1, 0:w], 0, w),
                         (k.identb[:, :], k.mask_row[:, :], t * P, w)]],
                values=[[k.tm[:, 2, u, h * DH:(h + 1) * DH] for u in range(t + 1)]],
                out=k.ycat[:, t, 512 + h * DH:512 + (h + 1) * DH]))
    stage_attention(k, batches, 1.0, 190, 0)


def stage_mlstm(k):
    nc = k.nc
    fm = k.fm
    cv = k.sb("conv", 172, [P, 4, S])
    cs = k.sb("convs", 180, [P, 4, S])
    v1 = k.sb("v_one", 188, [P, T, 4, DH + 1])
    hand = k.sig("conv_hand")
    chain = k.sig("dve_chain")
    with nc.Block() as block:
        @block.vector
        def _(dve):
            v = nc.vector
            link = Chain(dve, chain)
            v.tensor_copy(v1[:, :, :, 0:DH], k.tm[:, 3, :, :].rearrange("p t (h e) -> p t h e", h=4))
            v.memset(v1[:, :, :, DH:DH + 1], 1.0)
            for f in range(4):
                x = fm[:, 10 + f, :]
                link(v.tensor_scalar(cv[:, f, :], x, col(k, "conv_w", 4 * f + 3), None, ALU.mult))
                for i in (1, 2):
                    link(v.scalar_tensor_tensor(out=cv[:, f, i:], in0=x[:, 0:S - i],
                                                scalar=col(k, "conv_w", 4 * f + 3 - i), in1=cv[:, f, i:],
                                                op0=ALU.mult, op1=ALU.add))
                v.scalar_tensor_tensor(out=cv[:, f, 3:], in0=x[:, 0:S - 3], scalar=col(k, "conv_w", 4 * f),
                                       in1=cv[:, f, 3:], op0=ALU.mult, op1=ALU.add).then_inc(hand.sem, 1)
            for f in range(4):
                dve.wait_ge(hand.sem, hand.base + 5 + f)
                v.scalar_tensor_tensor(out=cv[:, f, :], in0=cs[:, f, :], scalar=1.0 if f < 2 else DH ** -0.5,
                                       in1=cv[:, f, :], op0=ALU.mult, op1=ALU.mult)

        @block.scalar
        def _(act):
            act.wait_ge(hand.sem, hand.base + 4)
            for f in range(4):
                nc.scalar.activation(cs[:, f, :], cv[:, f, :], ACT.Sigmoid).then_inc(hand.sem, 1)
    hand.base += 8

    decay = k.sb("ml_decay", 193, [P, 2, S])
    pT = k.sb("ml_pT", 16, [P, 2, T, S])
    nb = 16
    dm, qk, ex, pp, mixed, outd = (k.sig(x) for x in ("ml_logs", "ml_scores", "ml_decay", "ml_probs", "ml_mixed", "ml_out"))
    dn = k.sb("ml_den", 197, [P, 3, T])
    with nc.Block() as block:
        @block.tensor
        def _(pe):
            def scores(b):
                h, u = divmod(b, T)
                lo = DH * (h % 2)
                c0 = u * P
                if b >= 2:
                    pe.wait_ge(ex.sem, ex.base + b - 1)
                nc.tensor.matmul(k.pb[b % 2][:, c0:S], k.sel[0:4, h, 0:P], k.rows[0:4, 3, c0:S], start=True,
                                 stop=False, skip_group_check=True)
                nc.tensor.matmul(k.pb[b % 2][:, c0:c0 + P], k.identb[:, :], k.mask_col[:, :], start=False,
                                 stop=True, skip_group_check=True).then_inc(dm.sem, 1)
                if b >= 2:
                    pe.wait_ge(pp.sem, pp.base + b - 1)
                nc.tensor.matmul(k.pb[2 + b % 2][:, c0:S], cv[lo:lo + DH, 2 + h // 2, c0:c0 + P],
                                 cv[lo:lo + DH, h // 2, c0:S], start=True, stop=True).then_inc(qk.sem, 1)

            def mix(h):
                pe.wait_ge(pp.sem, pp.base + 4 * h + 4)
                if h >= 2:
                    pe.wait_ge(outd.sem, outd.base + h - 1)
                for t in range(T):
                    for u in range(t + 1):
                        mm = nc.tensor.matmul(k.pb[4 + h % 2][:, t * 65:t * 65 + 65], pT[:, h % 2, u, t * P:(t + 1) * P],
                                              v1[:, u, h, :], start=u == 0, stop=u == t, skip_group_check=True)
                mm.then_inc(mixed.sem, 1)

            for h in range(5):
                if h < 4:
                    for u in range(T):
                        scores(4 * h + u)
                if h >= 1:
                    mix(h - 1)

        @block.scalar
        def _(act):
            for b in range(nb):
                h, u = divmod(b, T)
                act.wait_ge(dm.sem, dm.base + b + 1)
                if b >= 2:
                    act.wait_ge(pp.sem, pp.base + b - 1)
                nc.scalar.activation(decay[:, b % 2, u * P:S], k.pb[b % 2][:, u * P:S], ACT.Exp,
                                     bias=k.acol[:, u, h:h + 1]).then_inc(ex.sem, 1)

        @block.vector
        def _(dve):
            v = nc.vector
            link = Chain(dve, chain)

            def finish(h):
                dve.wait_ge(mixed.sem, mixed.base + h + 1)
                o = k.pb[4 + h % 2][:, 0:260].rearrange("p (t e) -> p t e", e=65)
                den = o[:, :, 64]
                link(v.tensor_scalar(dn[:, 0, :], den, -1.0, None, ALU.mult))
                link(v.tensor_tensor(dn[:, 0, :], dn[:, 0, :], den, ALU.max))
                link(v.tensor_tensor(dn[:, 0, :], dn[:, 0, :], k.mcol[:, :, h], ALU.max))
                link(v.reciprocal(dn[:, 1, :], dn[:, 0, :]))
                v.tensor_tensor(k.ycat[:, :, 768 + h * DH:768 + (h + 1) * DH], o[:, :, 0:DH],
                                dn[:, 1, :].unsqueeze(2).to_broadcast([P, T, DH]), ALU.mult).then_inc(outd.sem, 1)

            for b in range(nb):
                h, u = divmod(b, T)
                dve.wait_ge(ex.sem, ex.base + b + 1)
                dve.wait_ge(qk.sem, qk.base + b + 1)
                if u == 0 and h >= 2:
                    dve.wait_ge(mixed.sem, mixed.base + h - 1)
                v.tensor_tensor(pT[:, h % 2, u, u * P:S], decay[:, b % 2, u * P:S], k.pb[2 + b % 2][:, u * P:S],
                                ALU.mult).then_inc(pp.sem, 1)
                if u == 3 and h >= 1:
                    finish(h - 1)
            finish(3)
    for s in (dm, qk, ex, pp):
        s.base += nb
    mixed.base += 4
    outd.base += 4


def stage_hgrn(k):
    nc = k.nc
    q, z = k.fm[:, 2:4, :], k.fm[:, 4:6, :]
    lf = k.sb("hg_lf", 142, [P, 2, S])
    b = k.sb("hg_b", 146, [P, 2, S])
    kk = k.sb("hg_k", 150, [P, 2, S])
    X = k.sb("hg_x", 154, [P, 2, 2, S])
    Z = k.sb("hg_z", 162, [P, 2, 2, S])
    acc = k.sb("hg_acc", 170, [P, 4, S])
    off = k.sb("hg_off", 178, [P, 4, 6, P])
    rst = k.sb("hg_reset", 190, [P, 2, S])
    lbt = k.sb("hg_lbt", 194, [P, 4, 2])
    hand = k.sig("hg_hand")
    chain = k.sig("dve_chain")
    chain_a = k.sig("act_chain")
    with nc.Block() as block:
        @block.scalar
        def _(act):
            link = Chain(act, chain_a)
            act.wait_ge(hand.sem, hand.base + 1)
            nc.scalar.activation(lbt[:, 0, :], lbt[:, 0, :], ACT.Exp)
            link(nc.scalar.activation(X[:, 0], X[:, 0], ACT.Exp))
            nc.scalar.activation(X[:, 0], X[:, 0], ACT.Ln, bias=1.0)
            nc.scalar.activation(X[:, 1], X[:, 1], ACT.Exp).then_inc(hand.sem, 1)
            act.wait_ge(hand.sem, hand.base + 3)
            nc.scalar.activation(X[:, 1], X[:, 1], ACT.Ln, bias=1.0)
            nc.scalar.activation(kk[:, :, :], z, ACT.Sigmoid, scale=-1.0).then_inc(hand.sem, 1)

        @block.vector
        def _(dve):
            v = nc.vector
            link = Chain(dve, chain)
            lb = col(k, "hg_lb", 0, 2)
            v.tensor_tensor(lbt[:, 0, :], lb, lb, ALU.subtract)
            v.tensor_scalar(X[:, 1], z, -1.0, 60.0, ALU.mult, ALU.min)
            v.tensor_scalar(lf[:, :, :], z, 0.0, None, ALU.min)
            link(v.tensor_scalar(X[:, 0], z, -1.0, None, ALU.mult))
            v.tensor_tensor(X[:, 0], X[:, 0], z, ALU.min).then_inc(hand.sem, 1)
            v.memset(acc[:, :, :], 0.0)
            v.memset(rst[:, :, :], 1.0)
            dve.wait_ge(hand.sem, hand.base + 2)
            link(v.reciprocal(lbt[:, 1, :], lbt[:, 0, :]))
            link(v.tensor_tensor(lbt[:, 1, :], lbt[:, 1, :], lbt[:, 0, :], ALU.mult))
            link(v.tensor_tensor(lbt[:, 2, :], lbt[:, 1, :], lbt[:, 1, :], ALU.subtract))
            link(v.tensor_scalar(lbt[:, 2, :], lbt[:, 2, :], 0.0, None, ALU.max))
            v.tensor_scalar(lbt[:, 3, :], lbt[:, 2, :], -1.0, 1.0, ALU.mult, ALU.add)
            link(v.tensor_tensor(lf[:, :, :], lf[:, :, :], X[:, 0], ALU.subtract))
            v.tensor_tensor(X[:, 1], X[:, 1], lbt[:, 2, :].unsqueeze(2).to_broadcast([P, 2, S]),
                            ALU.mult).then_inc(hand.sem, 1)
            dve.wait_ge(hand.sem, hand.base + 4)
            link(v.tensor_tensor(lf[:, :, :], lf[:, :, :], X[:, 1], ALU.add))
            v.tensor_tensor(kk[:, :, :], kk[:, :, :], lbt[:, 3, :].unsqueeze(2).to_broadcast([P, 2, S]), ALU.mult)
            link(v.memset(rst[:, :, 0::64], 0.0))
            v.tensor_tensor_scan(b[:, :, :].rearrange("p f s -> p (f s)"), rst[:, :, :].rearrange("p f s -> p (f s)"),
                                 lf[:, :, :].rearrange("p f s -> p (f s)"), 0.0, ALU.mult, ALU.add)
    hand.base += 4

    halves = [0, 1, 2, 4, 8, 16, 32, 64, 128, 256]
    made, ex, sc, sel = (k.sig(x) for x in ("hg_exponent", "hg_exp", "hg_scores", "hg_selected"))
    zr = k.sig("hg_z")
    nl = len(halves)
    with nc.Block() as block:
        @block.vector
        def _(dve):
            v = nc.vector
            link = Chain(dve, chain)

            def cut(t, n):
                return t.rearrange("p f (b c h) -> p (f b) c h", c=2, h=n)

            def exponents(i):
                n = halves[i]
                x = cut(X[:, i % 2], n)
                if i >= 3:
                    dve.wait_ge(zr.sem, zr.base + i - 2)
                if n <= 32:
                    bb = cut(b[:, :, :], n)
                    ref = bb[:, :, 0, n - 1:n].to_broadcast([P, S // n, n])
                    v.tensor_tensor(x[:, :, 1, :], bb[:, :, 1, :], ref, ALU.subtract)
                    v.tensor_tensor(x[:, :, 0, :], ref, bb[:, :, 0, :], ALU.subtract).then_inc(made.sem, 1)
                    return
                if n > 64:
                    link(v.memset(rst[:, :, n // 2::n], 1.0))
                    link(v.tensor_tensor_scan(
                        b[:, :, :].rearrange("p f s -> p (f s)"), rst[:, :, :].rearrange("p f s -> p (f s)"),
                        lf[:, :, :].rearrange("p f s -> p (f s)"), 0.0, ALU.mult, ALU.add))
                bb = cut(b[:, :, :], n)
                v.tensor_copy(x[:, :, 1, :], bb[:, :, 1, :])
                v.tensor_tensor(x[:, :, 0, :], bb[:, :, 0, n - 1:n].to_broadcast([P, S // n, n]), bb[:, :, 0, :],
                                ALU.subtract).then_inc(made.sem, 1)

            def operands(i):
                n = halves[i]
                dve.wait_ge(ex.sem, ex.base + i)
                if i >= 2:
                    dve.wait_ge(sc.sem, sc.base + 4 * (i - 1))
                x, zz = cut(X[:, i % 2], n), cut(Z[:, i % 2], n)
                v.tensor_tensor(zz[:, :, 1, :], x[:, :, 1, :], cut(q, n)[:, :, 1, :], ALU.mult)
                v.tensor_tensor(zz[:, :, 0, :], x[:, :, 0, :], cut(kk[:, :, :], n)[:, :, 0, :],
                                ALU.mult).then_inc(zr.sem, 1)

            def select(i, h):
                m = 4 * i + h
                dve.wait_ge(sc.sem, sc.base + m + 1)
                ps = k.pb[m % 4]
                n = halves[i]
                if n <= 64:
                    mask = k.mask_lev[:, i, :].bitcast(mybir.dt.uint16).unsqueeze(1).to_broadcast([P, T, P])
                    v.copy_predicated(acc[:, h, :].rearrange("p (t s) -> p t s", t=T), mask,
                                      ps[:, :].rearrange("p (t s) -> p t s", t=T)).then_inc(sel.sem, 1)
                elif n == 128:
                    v.tensor_copy(off[:, h, 0:2, :], ps[:, 0:256].rearrange("p (c s) -> p c s", c=2)).then_inc(sel.sem, 1)
                else:
                    v.tensor_copy(off[:, h, 2:6, :], ps[:, :].rearrange("p (c s) -> p c s", c=4)).then_inc(sel.sem, 1)

            exponents(1)
            exponents(2)
            for i in range(nl):
                if i + 1 < nl:
                    operands(i + 1)
                if 1 <= i < nl - 2:
                    exponents(i + 2)
                for h in range(4):
                    select(i, h)

        @block.scalar
        def _(act):
            for i in range(1, nl):
                act.wait_ge(made.sem, made.base + i)
                nc.scalar.activation(X[:, i % 2], X[:, i % 2], ACT.Exp).then_inc(ex.sem, 1)

        @block.tensor
        def _(pe):
            for i in range(nl):
                if i >= 1:
                    pe.wait_ge(zr.sem, zr.base + i)
                for h in range(4):
                    m = 4 * i + h
                    if m >= 4:
                        pe.wait_ge(sel.sem, sel.base + m - 3)
                    lo, f = DH * (h % 2), h // 2
                    L = kk[lo:lo + DH, f, :] if i == 0 else Z[lo:lo + DH, i % 2, f, :]
                    R = q[lo:lo + DH, f, :] if i == 0 else Z[lo:lo + DH, i % 2, f, :]
                    ps = k.pb[m % 4]
                    n = halves[i]
                    if n <= 64:
                        blocks = [(t * P, t * P, P, t * P) for t in range(T)]
                    elif n == 128:
                        blocks = [(0, 128, P, 0), (256, 384, P, 128)]
                    else:
                        blocks = [(0, 256, 256, 0), (128, 256, 256, 256)]
                    for s0, t0, w, c in blocks:
                        mm = nc.tensor.matmul(ps[:, c:c + w], L[:, s0:s0 + P], R[:, t0:t0 + w], start=True, stop=True,
                                              skip_group_check=True)
                    mm.then_inc(sc.sem, 1)
    for s, n in ((made, nl - 1), (ex, nl - 1), (zr, nl - 1), (sc, 4 * nl), (sel, 4 * nl)):
        s.base += n

    mixed, evd = k.sig("hg_mixed"), k.sig("hg_out")
    at = {(0, 1): 0, (2, 3): 1, (0, 2): 2, (0, 3): 3, (1, 2): 4, (1, 3): 5}
    with nc.Block() as block:
        @block.tensor
        def _(pe):
            for h in range(4):
                for t in range(T):
                    for u in range(t + 1):
                        a = acc[:, h, t * P:(t + 1) * P] if u == t else off[:, h, at[(u, t)], :]
                        mm = nc.tensor.matmul(k.pb[4 + h][:, t * DH:(t + 1) * DH], a, k.tm[:, 0, u, h * DH:(h + 1) * DH],
                                              start=u == 0, stop=u == t, skip_group_check=True)
                mm.then_inc(mixed.sem, 1)

        @block.vector
        def _(dve):
            for h in range(4):
                dve.wait_ge(mixed.sem, mixed.base + h + 1)
                nc.vector.tensor_copy(k.ycat[:, :, 256 + h * DH:256 + (h + 1) * DH],
                                      k.pb[4 + h][:, 0:256].rearrange("p (t e) -> p t e", t=T))
    mixed.base += 4


def stage_finish(k):
    nc = k.nc
    sq = k.sb("fin_sq", 142, [P, T * 16, DH])
    ss = k.sb("fin_ss", 158, [P, T, 16])
    rs = k.sb("fin_rs", 158.25, [P, T, 16])
    mh = k.sb("fin_half", 158.5, [P, T, 16])
    s4 = k.sb("fin_s4", 158.75, [P, T])
    sg = k.sb("fin_sg", 160, [P, 2, T, 256])
    hand, sgs = k.sig("fin_hand"), k.sig("fin_gates")
    chain = k.sig("dve_chain")
    yh = k.ycat[:, :, :].rearrange("p t (h e) -> p (t h) e", e=DH)
    with nc.Block() as block:
        @block.scalar
        def _(act):
            nc.scalar.activation(sg[:, 0], k.tm[:, 1], ACT.Sigmoid).then_inc(sgs.sem, 1)
            nc.scalar.activation(sg[:, 1], k.tm[:, 4], ACT.Sigmoid).then_inc(sgs.sem, 1)

        @block.gpsimd
        def _(pool):
            pool.wait_ge(hand.sem, hand.base + 1)
            nc.gpsimd.tensor_tensor(rs[:, :, :], ss[:, :, :], mh[:, :, :], ALU.pow).then_inc(hand.sem, 1)

        @block.vector
        def _(dve):
            v = nc.vector
            link = Chain(dve, chain)
            v.memset(mh[:, :, :], -0.5)
            link(v.tensor_tensor(sq[:, :, :], yh, yh, ALU.mult))
            link(v.tensor_reduce(ss[:, :, :].rearrange("p t h -> p (t h)"), sq[:, :, :], AX.X, ALU.add))
            link(v.tensor_reduce(s4[:, :], ss[:, :, 0:4], AX.X, ALU.add))
            link(v.tensor_scalar(ss[:, :, 0:4], s4[:, :].unsqueeze(2).to_broadcast([P, T, 4]), 0.25, None, ALU.mult))
            v.tensor_scalar(ss[:, :, :], ss[:, :, :], 1.0 / DH, EPS, ALU.mult, ALU.add).then_inc(hand.sem, 1)
            dve.wait_ge(hand.sem, hand.base + 2)
            link(v.tensor_tensor(yh, yh, rs[:, :, :].rearrange("p t h -> p (t h)").unsqueeze(2)
                                 .to_broadcast([P, T * 16, DH]), ALU.mult))
            dve.wait_ge(sgs.sem, sgs.base + 2)
            link(v.tensor_tensor(sg[:, 0], sg[:, 0], k.tm[:, 1], ALU.mult))
            v.tensor_tensor(k.ycat[:, :, 256:512], k.ycat[:, :, 256:512], sg[:, 0], ALU.mult)
            v.tensor_tensor(k.ycat[:, :, 768:1024], k.ycat[:, :, 768:1024], sg[:, 1], ALU.mult)
    hand.base += 2
    sgs.base += 2


def build(nc, d, out):
    with ExitStack() as ctx:
        k = allocate(nc, ctx, d)
        for name, first, n in CHUNKS:
            k.chunks += [d[name][i] for i in range(first, first + n)]
        stage_load(k)
        first_block(k)
        second_block(k, out)


def chunked(w, width):
    kk, n = w.shape
    return np.ascontiguousarray(
        w.reshape(kk // P, P, n // width, width).transpose(2, 1, 0, 3).reshape(n // width, P, kk // P * width))


def columns(x):
    return np.ascontiguousarray(np.asarray(x).reshape(-1, P).T)


def constants():
    bf = mybir.dt.np(BF16)
    c = {"ident": np.eye(P, dtype=np.float32), "identb": np.eye(P).astype(bf)}
    q, kk = np.arange(P)[:, None], np.arange(3 * P)[None, :] - P
    c["mask_band"] = np.where(np.abs(q - kk) <= 64, 0.0, NEG).astype(bf)
    a, b = np.arange(P)[:, None], np.arange(P)[None, :]
    c["mask_d4"] = np.where(np.abs(a - b) <= 64, 0.0, NEG).astype(bf)
    c["mask_d16"] = np.where(a % 4 == b % 4, 0.0, NEG).astype(bf)
    c["mask_row"] = np.where(b <= a, 0.0, NEG).astype(bf)
    c["mask_col"] = np.where(a <= b, 0.0, NEG).astype(bf)
    lev = np.zeros((P, 8, P), np.float32)
    lev[:, 0, :] = a == b
    for i in range(7):
        hs = 1 << i
        lev[:, i + 1, :] = (a // (2 * hs) == b // (2 * hs)) & ((a // hs) % 2 == 0) & ((b // hs) % 2 == 1)
    c["mask_lev"] = lev.astype(bf)
    ra = np.zeros((P, 3, T, 16), np.float32)
    inv = np.float32(500000.0) ** (-(np.arange(8, dtype=np.float32) * 2.0 / 16))
    for g, r in enumerate(A_DIL):
        order = np.arange(S).reshape(T, P) if r == 1 else np.arange(S).reshape(P, T).T
        ang = order.T[:, :, None].astype(np.float32) * inv.astype(np.float32)
        ra[:, g, :, 0:8], ra[:, g, :, 8:16] = np.cos(ang), np.sin(ang)
    c["ropeA"] = ra
    c["sel"] = np.ascontiguousarray(np.broadcast_to(np.eye(4, dtype=np.float32)[:, :, None], (4, 4, S)))
    inv = (np.float32(10000.0) ** (-(np.arange(16, dtype=np.float32) * 2.0 / 32))).astype(np.float32)
    ang = np.arange(S).reshape(T, P).T[:, :, None].astype(np.float32) * inv
    c["ropeB"] = np.concatenate([np.cos(ang), np.sin(ang)], -1).astype(np.float32)
    return c


def layout(x):
    x = {n: np.asarray(a) for n, a in x.items()}
    a = {"x": x["x"].reshape(S, D)}
    w = x["w_in"]
    cols = []
    for g in range(3):
        cols += [w[:, 256 * g:256 * g + 256], w[:, 768 + 256 * g:1024 + 256 * g]]
    cols += [w[:, 1536:2304], w[:, 2816:3072], w[:, 2304:2816]]
    a["w_proj"] = chunked(np.concatenate(cols, 1), 512)
    a["w_kpe"] = chunked(w[:, 3072:3104], 32)
    a["w_gates"] = chunked(w[:, 3104:], 512)
    a["w_uq"] = chunked(x["mla_w_uq"], 768)
    a["w_ukv"] = chunked(x["mla_w_ukv"], 1024)
    a["w_oa"] = chunked(x["w_o_a"], 1024)
    a["w_ob"] = chunked(x["w_o_b"], 1024)
    a["w_out"] = chunked(x["w_out"], 512)
    a["w_ff1"] = chunked(x["w_ff1"], 512)
    a["w_ff2"] = np.ascontiguousarray(
        x["w_ff2"].reshape(4, 8, P, 2, 512).transpose(3, 0, 2, 1, 4).reshape(8, P, 4096))
    z = np.zeros((P, 3), np.float32)
    gb = x["gate_bias_2"].reshape(3, 4)
    z[0:4, :] = gb.T
    lb = lambda n: columns(x[n][0])
    parts = {"mix_pre": columns(x["norm_mix_pre"]), "b_gate": columns(x["b_gate"]),
             "q_norm": columns(x["mla_q_norm"]), "kv_norm": columns(x["mla_kv_norm"]),
             "mlp_pre": columns(x["norm_mlp_pre"]), "mix_pre2": lb("ln_mix_pre_2"),
             "ffn_pre2": lb("ln_ffn_pre_2"), "mix_gain2": lb("mix_gain_2"),
             "hg_lb": lb("hgrn_lb_logits_2"),
             "conv_w": np.ascontiguousarray(x["mlstm_conv_w_2"][0].reshape(4, 4, P).transpose(2, 1, 0).reshape(P, 16)),
             "lam_re": columns(x["s5_lambda_re_2"][0].reshape(-1)), "lam_im": columns(x["s5_lambda_im_2"][0].reshape(-1)),
             "log_dt": columns(np.repeat(x["s5_log_dt_2"][0], 64)), "s5_d": lb("s5_d_2"), "gate_b": z}
    a["cols"] = np.concatenate([parts[n] for n in COLS], 1)
    for n, m in (("norm_mix_post", "norm_mix_post"), ("norm_mlp_post", "norm_mlp_post")):
        a[n] = x[m].reshape(D)
    a["ln_mix_post_2"], a["ln_ffn_post_2"] = x["ln_mix_post_2"][0], x["ln_ffn_post_2"][0]
    w = x["w_in_2"][0]
    at = dict(s5u=0, hgq=256, hgf=512, hgi=768, hgg=1024, foxq=1280, foxk=1536, foxv=1792, mlq=2052, mlk=2308,
              mlv=2564, mlo=2820)
    part = lambda *names: [w[:, at[n]:at[n] + 256] for n in names]
    a["w_fm"] = chunked(np.concatenate(part("s5u", "hgq", "hgf", "foxq", "foxk", "mlq"), 1), 512)
    gates = np.zeros((D, 96), np.float32)
    for i, c in enumerate((2048, 3076, 3080)):
        gates[:, 32 * i:32 * i + 4] = w[:, c:c + 4]
    a["w_fg"] = chunked(np.concatenate(part("mlk") + [gates], 1), 352)
    a["w_tm"] = chunked(np.concatenate(part("hgi", "hgg", "foxv", "mlv"), 1), 512)
    a["w_tg"] = chunked(np.concatenate(part("mlo"), 1), 256)
    a["w_glu"] = chunked(x["s5_w_glu_2"][0], 256)
    a["w_out2"] = chunked(x["w_out_2"][0], 512)
    up = np.concatenate([x["w_ffn_gate_2"][0].reshape(D, 11, 1, 256), x["w_ffn_up_2"][0].reshape(D, 11, 1, 256)], 2)
    a["w_up"] = chunked(up.reshape(D, 11 * 512), 512)
    dn = x["w_ffn_down_2"][0].reshape(22, P, 2, 512).transpose(2, 1, 0, 3)
    a["w_dn8"] = np.ascontiguousarray(dn[:, :, 0:16].reshape(2, P, 2, 4096).transpose(0, 2, 1, 3).reshape(4, P, 4096))
    a["w_dn6"] = np.ascontiguousarray(dn[:, :, 16:22].reshape(2, P, 3072))
    for n, m in (("s5_b_re", "s5_b_re_2"), ("s5_b_im", "s5_b_im_2")):
        z = np.zeros((8, 2, 64, 2, 16), np.float32)
        for i in range(2):
            z[:, i, :, i, :] = x[m][0].reshape(8, 2, 64, 16)[:, i]
        a[n] = np.ascontiguousarray(z.reshape(8, P, 32).transpose(1, 0, 2))
    z = np.zeros((2, 8, 2, 64, 2, 16), np.float32)
    for c, m in enumerate(("s5_c_re_2", "s5_c_im_2")):
        for i in range(2):
            z[c, :, i, :, i, :] = x[m][0].reshape(8, 2, 16, 64)[:, i].transpose(0, 2, 1)
    a["s5_cT"] = np.ascontiguousarray(z.reshape(2, 8, P, 32).transpose(2, 0, 1, 3))
    a.update(constants())
    return a


CHUNKS = [("w_proj", 0, 6), ("w_kpe", 0, 1), ("w_gates", 0, 4), ("w_uq", 0, 1), ("w_ukv", 0, 1), ("w_oa", 0, 1),
          ("w_ob", 0, 1), ("w_out", 0, 2), ("w_ff1", 0, 8), ("w_ff2", 0, 8),
          ("w_fm", 0, 3), ("w_fg", 0, 1), ("w_tm", 0, 2), ("w_tg", 0, 1), ("w_glu", 0, 1), ("w_out2", 0, 2),
          ("w_up", 0, 11), ("w_dn8", 0, 2), ("w_dn6", 0, 1), ("w_dn8", 2, 2), ("w_dn6", 1, 1)]


def kernel(**inputs):
    import concourse.bacc as bacc
    from concourse.bass_utils import run_bass_kernel_spmd

    nc = bacc.Bacc("TRN2", target_bir_lowering=False, num_devices=1)
    arrays, d = {}, {}
    for name, a in layout(inputs).items():
        arrays[f"in_{name}"] = a
        d[name] = nc.dram_tensor(f"in_{name}", a.shape, mybir.dt.from_np(a.dtype), kind="ExternalInput").ap()
    d["scratch"] = nc.dram_tensor("scratch", (2, S, 260), F32, kind="Internal").ap()
    out = nc.dram_tensor("out_0_dram", (1, S, D), F32, kind="ExternalOutput").ap()
    build(nc, d, out)
    r = run_bass_kernel_spmd(nc, [arrays], core_ids=[0])
    return r.results[0]["out_0_dram"]
```

```python
from contextlib import ExitStack

import numpy as np

import concourse.bass as bass
from concourse import mybir

ALU = mybir.AluOpType
ACT = mybir.ActivationFunctionType
AX = mybir.AxisListType
F32 = mybir.dt.float32
BF16 = mybir.dt.bfloat16
F32R = mybir.dt.float32r

P = 128
S = 512
T = S // P
D = 1024
KD = D // P
EPS = 1e-6
KB = 1024
DH = 64
NEG = -1e30

A_HEADS = 4
A_DIL = (1, 4, 16)
B_HEADS = 8
B_QK = 96
FF1 = 4096
FF2 = 2816
FF2_PARTS = (12, 10)
SLOTS = 3
LEAD = 2
CHUNK = 2048
COLS = {}
_at = 0
for _name, _n in (("mix_pre", 8), ("b_gate", 16), ("q_norm", 4), ("kv_norm", 2), ("mlp_pre", 8),
                  ("mix_pre2", 8), ("ffn_pre2", 8), ("mix_gain2", 8), ("hg_lb", 2), ("conv_w", 16),
                  ("lam_re", 8), ("lam_im", 8), ("log_dt", 8), ("s5_d", 2), ("gate_b", 3)):
    COLS[_name] = (_at, _n)
    _at += _n
NCOLS = _at


class Signal:

    def __init__(self, sem):
        self.sem = sem
        self.base = 0


class Kernel:
    pass


class Split:

    def __init__(self, hi, lo):
        self.hi, self.lo = hi, lo

    def __getitem__(self, at):
        return Split(self.hi[at], self.lo[at])


def plain(x):
    return x.bitcast(F32)


def allocate(nc, ctx, d):
    k = Kernel()
    k.nc, k.d = nc, d

    def sb(name, kb, shape, dt=F32):
        return nc.alloc_sbuf_tensor_at(name, shape, dt, offset=int(kb * KB) + k.sb0)

    k.sb0 = (nc.sbuf_base + 63) // 64 * 64
    k.sb = sb
    k.split = lambda name, kb, shape, kb_lo: Split(sb(name + "_hi", kb, shape, F32R), sb(name + "_lo", kb_lo, shape, F32R))
    k.h = sb("h", 0, [P, T, D])
    k.xT = k.split("xT", 16, [P, KD, S], 32)
    k.raw = sb("ring_raw", 48, [P, SLOTS, CHUNK])
    k.ring = Split(sb("ring_hi", 72, [P, SLOTS, CHUNK], F32R), sb("ring_lo", 48, [P, SLOTS, CHUNK], F32R))
    k.ident = sb("ident", 96, [P, P])
    k.identb = sb("identb", 96.5, [P, P], BF16)
    k.mask_band = sb("mask_band", 96.75, [P, 3 * P], BF16)
    k.mask_d4 = sb("mask_d4", 97.5, [P, P], BF16)
    k.mask_d16 = sb("mask_d16", 97.75, [P, P], BF16)
    k.mask_row = sb("mask_row", 98, [P, P], BF16)
    k.mask_col = sb("mask_col", 98.25, [P, P], BF16)
    k.mask_lev = sb("mask_lev", 98.5, [P, 8, P], BF16)
    k.ropeA = sb("ropeA", 100.5, [P, 3, T, 16])
    k.ropeB = sb("ropeB", 101.25, [P, T, 32])
    k.cols = sb("cols", 101.75, [P, NCOLS])
    k.stat = sb("stat", 102.5, [P, 64])
    k.pb = [ctx.enter_context(nc.psum_tensor(f"bank{i}", [P, 512], F32)) for i in range(8)]
    k.sems = {}

    def sig(name):
        if name not in k.sems:
            k.sems[name] = Signal(ctx.enter_context(nc.semaphore(name)))
        return k.sems[name]

    k.sig = sig
    k.w_landed = [sig(f"w_landed{i}") for i in range(SLOTS)]
    k.w_hi, k.w_split = sig("w_hi"), sig("w_split")
    k.hi_next = k.lo_next = 0
    k.w_used = sig("w_used")
    k.freed = {}
    k.c_in = sig("consts_in")
    k.x_in = sig("x_in")
    k.chunks = []
    k.att_n = 0
    k.issued = 0
    return k


def col(k, name, i=0, n=1):
    a, _ = COLS[name]
    return k.cols[:, a + i:a + i + n]


def issue_chunks(k, eng, upto):
    upto = min(upto, len(k.chunks))
    for g in range(k.issued, upto):
        src = k.chunks[g]
        if g >= SLOTS:
            sem, count = k.freed[g - SLOTS]
            eng.wait_ge(sem, count)
        eng.dma_start(k.raw[:, g % SLOTS, 0:src.shape[1]], src).then_inc(k.w_landed[g % SLOTS].sem, 16)
    k.issued = max(k.issued, upto)


def split_hi(k, act, upto):
    upto = min(upto, len(k.chunks))
    for g in range(k.hi_next, upto):
        n = k.chunks[g].shape[1]
        act.wait_ge(k.w_landed[g % SLOTS].sem, 16 * (g // SLOTS + 1))
        if g >= SLOTS:
            sem, count = k.freed[g - SLOTS]
            act.wait_ge(sem, count)
        k.nc.scalar.copy(k.ring.hi[:, g % SLOTS, 0:n], k.raw[:, g % SLOTS, 0:n]).then_inc(k.w_hi.sem, 1)
    k.hi_next = max(k.hi_next, upto)


def split_lo(k, dve, upto):
    upto = min(upto, len(k.chunks))
    for g in range(k.lo_next, upto):
        n = k.chunks[g].shape[1]
        dve.wait_ge(k.w_hi.sem, g + 1)
        k.nc.vector.tensor_tensor(k.ring.lo[:, g % SLOTS, 0:n], k.raw[:, g % SLOTS, 0:n],
                                  plain(k.ring.hi[:, g % SLOTS, 0:n]), ALU.subtract).then_inc(k.w_split.sem, 1)
    k.lo_next = max(k.lo_next, upto)


def wait_chunk(k, pe, g):
    pe.wait_ge(k.w_split.sem, g + 1)


def slot(k, g, a, b):
    return k.ring[:, g % SLOTS, a:b]


def products(k, out, pairs, first, last):
    n = 0
    for a, b in pairs:
        for x, y in ((a.hi, b.hi), (a.hi, b.lo), (a.lo, b.hi)):
            mm = k.nc.tensor.matmul(out, x, y, start=first and n == 0, stop=last and n == 3 * len(pairs) - 1)
            n += 1
    return mm


def note_freed(k, steps, done):
    final = {s[0]: i for i, s in enumerate(steps)}
    marks = set()
    for g, i in final.items():
        if steps[i][5]:
            k.freed[g] = (done.sem, done.base + sum(s[5] for s in steps[:i + 1]))
        else:
            k.w_used.base += 1
            k.freed[g] = (k.w_used.sem, k.w_used.base)
            marks.add(i)
    return marks


class Chain:

    def __init__(self, eng, signal):
        self.eng, self.s = eng, signal

    def __call__(self, ins):
        self.s.base += 1
        ins.then_inc(self.s.sem, 1)
        self.eng.wait_ge(self.s.sem, self.s.base)


def stage_load(k):
    nc, d = k.nc, k.d
    with nc.Block() as block:
        @block.sync
        def _(sp):
            sp.dma_start(k.h[:, :, :], d["x"].rearrange("(t p) n -> p t n", p=P)).then_inc(k.x_in.sem, 16)
            issue_chunks(k, sp, SLOTS)

        @block.scalar
        def _(act):
            for dst, name in ((k.cols[:, :], "cols"), (k.ident[:, :], "ident"),
                              (k.identb[:, :], "identb"), (k.mask_band[:, :], "mask_band"),
                              (k.mask_d4[:, :], "mask_d4"), (k.mask_d16[:, :], "mask_d16"),
                              (k.mask_row[:, :], "mask_row"), (k.mask_col[:, :], "mask_col"),
                              (k.mask_lev[:, :, :], "mask_lev"), (k.ropeA[:, :, :, :], "ropeA"),
                              (k.ropeB[:, :, :], "ropeB")):
                act.dma_start(dst, d[name]).then_inc(k.c_in.sem, 16)
            act.wait_ge(k.c_in.sem, 16 * 11)
            act.wait_ge(k.x_in.sem, 16)



def stage_norm_T(k, tag, src, width, gain, dst, xn_kb):
    nc = k.nc
    kt = width // P
    sq, root, scaled, turned, ev_act, ev_dve = (
        k.sig(n) for n in ("norm_sumsq", "norm_root", "norm_scaled", "norm_turned", "norm_evac_act", "norm_evac_dve"))
    ms, rs, half = k.stat[:, 0:T], k.stat[:, T:2 * T], k.stat[:, 2 * T:3 * T]
    xn = k.sb(f"xn_{tag}", xn_kb, [P, T, width])
    with nc.Block() as block:
        @block.scalar
        def _(act):
            for t in range(T):
                nc.scalar.activation(xn[:, t, :], src[:, t, :], ACT.Square,
                                     accum_out=k.stat[:, t:t + 1]).then_inc(sq.sem, 1)
            for f in range(kt):
                act.wait_ge(turned.sem, turned.base + f + 1)
                nc.scalar.mul(dst.hi[:, f, :], k.pb[f % 4][:, :], col(k, gain, f)).then_inc(ev_act.sem, 1)

        @block.gpsimd
        def _(pool):
            pool.wait_ge(root.sem, root.base + 1)
            nc.gpsimd.tensor_tensor(rs, ms, half, ALU.pow).then_inc(root.sem, 1)

        @block.vector
        def _(dve):
            nc.vector.memset(half, -0.5).then_inc(sq.sem, 1)
            dve.wait_ge(sq.sem, sq.base + T + 1)
            nc.vector.tensor_scalar(ms, ms, 1.0 / width, EPS, ALU.mult, ALU.add).then_inc(root.sem, 1)
            dve.wait_ge(root.sem, root.base + 2)
            for t in range(T):
                nc.vector.tensor_scalar(xn[:, t, :], src[:, t, :], rs[:, t:t + 1], None,
                                        ALU.mult).then_inc(scaled.sem, 1)
            for f in range(kt):
                dve.wait_ge(ev_act.sem, ev_act.base + f + 1)
                nc.vector.scalar_tensor_tensor(out=dst.lo[:, f, :], in0=k.pb[f % 4][:, :], scalar=col(k, gain, f),
                                               in1=plain(dst.hi[:, f, :]), op0=ALU.mult,
                                               op1=ALU.subtract).then_inc(ev_dve.sem, 1)

        @block.tensor
        def _(pe):
            for f in range(kt):
                if f >= 4:
                    pe.wait_ge(ev_dve.sem, ev_dve.base + f - 3)
                for t in range(T):
                    if f == 0:
                        pe.wait_ge(scaled.sem, scaled.base + t + 1)
                    last = nc.tensor.transpose(k.pb[f % 4][:, t * P:(t + 1) * P],
                                               xn[:, t, f * P:(f + 1) * P], k.ident[:, :])
                last.then_inc(turned.sem, 1)
    sq.base += T + 1
    root.base += 2
    scaled.base += T
    turned.base += kt
    ev_act.base += kt
    ev_dve.base += kt


def schedule(k, steps):
    chunks, fin = [], {}
    for g, j, _, _, _, last in steps:
        if not chunks or chunks[-1] != g:
            chunks.append(g)
        if last:
            fin[j] = g
    return chunks, fin


def stage_gemm(k, steps, evac, owner=None, act_tail=None):
    nc = k.nc
    done, free_act, free_dve = (k.sig(n) for n in ("gemm_done", "gemm_free_act", "gemm_free_dve"))
    n = 1 + max(s[1] for s in steps)
    owner = owner or (lambda j: ("act", "dve")[j % 2])
    outs = {s[1]: s[2] for s in steps}
    chunks, fin = schedule(k, steps)
    end = chunks[-1] + 1
    marks = note_freed(k, steps, done)
    counts, release, a, v = {}, {}, free_act.base, free_dve.base
    for j in range(n):
        if owner(j) in ("act", "both"):
            a += 1
        if owner(j) in ("dve", "both"):
            v += 1
        counts[j] = (a, v)
        release[j] = (free_act.sem, a) if owner(j) == "act" else (free_dve.sem, v)
    with nc.Block() as block:
        @block.sync
        def _(sp):
            issue_chunks(k, sp, end + SLOTS)

        @block.tensor
        def _(pe):
            seen = set()
            for i, (g, j, out, pairs, first, last) in enumerate(steps):
                if g not in seen:
                    seen.add(g)
                    wait_chunk(k, pe, g)
                if first and j >= 8:
                    sem, count = release[j - 8]
                    pe.wait_ge(sem, count)
                mm = products(k, out, pairs, first, last)
                if last:
                    mm.then_inc(done.sem, 1)
                elif i in marks:
                    mm.then_inc(k.w_used.sem, 1)

        @block.scalar
        def _(act):
            split_hi(k, act, chunks[0] + LEAD)
            for j in range(n):
                split_hi(k, act, fin[j] + LEAD)
                if owner(j) in ("act", "both"):
                    act.wait_ge(done.sem, done.base + j + 1)
                    evac("act", act, j, outs[j]).then_inc(free_act.sem, 1)
            split_hi(k, act, end + LEAD)
            if act_tail is not None:
                act_tail(act)

        @block.vector
        def _(dve):
            split_lo(k, dve, chunks[0] + LEAD)
            for j in range(n):
                split_lo(k, dve, fin[j] + LEAD)
                if owner(j) == "both":
                    dve.wait_ge(free_act.sem, counts[j][0])
                elif owner(j) == "dve":
                    dve.wait_ge(done.sem, done.base + j + 1)
                if owner(j) != "act":
                    evac("dve", dve, j, outs[j]).then_inc(free_dve.sem, 1)
            split_lo(k, dve, end + LEAD)
    done.base += n
    free_act.base, free_dve.base = a, v


def copy_out(k, who, dst, src):
    return k.nc.scalar.copy(dst, src) if who == "act" else k.nc.vector.tensor_copy(dst, src)


def tokens(k, perm, kt, t):
    if perm == 0:
        return k.xT[:, kt, t * P:(t + 1) * P]
    return k.xT[:, kt, t::T]


def stage_attention(k, batches, scale, bufs_kb, lse=None):
    nc = k.nc
    nb = len(batches)
    scored, negmax, expd, turned, ev_act, ev_dve, mixed, out_free = (
        k.sig(n) for n in ("att_scored", "att_negmax", "att_exp", "att_turned", "att_ptT_act", "att_ptT_dve",
                           "att_mixed", "att_out"))
    k.att_n += 1
    probs = k.sb(f"probs{k.att_n}", bufs_kb, [P, 2, 512])
    probsT = k.sb(f"probsT{k.att_n}", bufs_kb + 4, [P, 2, 512])
    ns = max(len(b["segs"]) for b in batches)
    mx = k.sb(f"mx{k.att_n}", bufs_kb + 8, [P, nb, ns])
    nm = k.sb(f"nm{k.att_n}", bufs_kb + 8.5, [P, nb, ns])
    ls = k.sb(f"ls{k.att_n}", bufs_kb + 9, [P, nb, ns])
    li = k.sb(f"li{k.att_n}", bufs_kb + 9.5, [P, nb, ns])
    chain = k.sig("dve_chain")
    chain_act = k.sig("act_chain")

    def width(b):
        return b["segs"][-1][1]

    with nc.Block() as block:
        @block.tensor
        def _(pe):
            def scores(i):
                b = batches[i]
                if i >= 2:
                    pe.wait_ge(expd.sem, expd.base + i - 1)
                for (c0, c1), parts in zip(b["segs"], b["scores"]):
                    for m, (a, r, lo, hi) in enumerate(parts):
                        mm = nc.tensor.matmul(k.pb[i % 2][:, lo:hi], a, r, start=m == 0,
                                              stop=m == len(parts) - 1, skip_group_check=True)
                mm.then_inc(scored.sem, 1)

            def turn(i):
                b = batches[i]
                pe.wait_ge(expd.sem, expd.base + i + 1)
                if i >= 2:
                    ev = (ev_act, ev_dve)[i % 2]
                    pe.wait_ge(ev.sem, ev.base + i // 2)
                for c in range(0, width(b), P):
                    mm = nc.tensor.transpose(k.pb[2 + i % 2][:, c:c + P], probs[:, i % 2, c:c + P], k.ident[:, :])
                mm.then_inc(turned.sem, 1)

            def mix(i):
                b = batches[i]
                ev = (ev_act, ev_dve)[i % 2]
                pe.wait_ge(ev.sem, ev.base + i // 2 + 1)
                if i >= 2:
                    pe.wait_ge(out_free.sem, out_free.base + i - 1)
                for n, ((c0, c1), vs) in enumerate(zip(b["segs"], b["values"])):
                    for m, v in enumerate(vs):
                        mm = nc.tensor.matmul(k.pb[4 + i % 2][:, n * DH:(n + 1) * DH],
                                              probsT[:, i % 2, c0 + m * P:c0 + (m + 1) * P], v,
                                              start=m == 0, stop=m == len(vs) - 1, skip_group_check=True)
                mm.then_inc(mixed.sem, 1)

            for i in range(nb + 2):
                if i < nb:
                    scores(i)
                if 1 <= i <= nb:
                    turn(i - 1)
                if i >= 2:
                    mix(i - 2)

        def evac(who, eng, i):
            w = width(batches[i])
            eng.wait_ge(turned.sem, turned.base + i + 1)
            if i >= 2:
                eng.wait_ge(mixed.sem, mixed.base + i - 1)
            copy_out(k, who, probsT[:, i % 2, 0:w], k.pb[2 + i % 2][:, 0:w]).then_inc(
                (ev_act if who == "act" else ev_dve).sem, 1)

        @block.scalar
        def _(act):
            for i in range(nb + 1):
                if i < nb:
                    b = batches[i]
                    act.wait_ge(negmax.sem, negmax.base + i + 1)
                    if i >= 2:
                        act.wait_ge(turned.sem, turned.base + i - 1)
                    for n, (c0, c1) in enumerate(b["segs"]):
                        e = nc.scalar.activation(probs[:, i % 2, c0:c1], k.pb[i % 2][:, c0:c1], ACT.Exp,
                                                 bias=nm[:, i, n:n + 1], scale=scale,
                                                 accum_out=ls[:, i, n:n + 1])
                    e.then_inc(expd.sem, 1)
                if i >= 1 and (i - 1) % 2 == 0:
                    evac("act", act, i - 1)
            if lse is not None:
                act.wait_ge(expd.sem, expd.base + nb)
                nc.scalar.activation(mx[:, :, :], ls[:, :, :], ACT.Ln).then_inc(chain_act.sem, 1)

        @block.vector
        def _(dve):
            link = Chain(dve, chain)
            if lse is not None:
                link(nc.vector.memset(ls[:, :, :], 1.0))
            for i in range(nb + 2):
                if i < nb:
                    b = batches[i]
                    m = len(b["segs"])
                    dve.wait_ge(scored.sem, scored.base + i + 1)
                    w = width(b)
                    link(nc.vector.tensor_reduce(
                        mx[:, i, 0:m], k.pb[i % 2][:, 0:w].rearrange("p (m w) -> p m w", m=m), AX.X, ALU.max))
                    nc.vector.tensor_scalar(nm[:, i, 0:m], mx[:, i, 0:m], -scale, None,
                                            ALU.mult).then_inc(negmax.sem, 1)
                if 1 <= i <= nb and (i - 1) % 2 == 1:
                    evac("dve", dve, i - 1)
                if i >= 2:
                    j = i - 2
                    b = batches[j]
                    m = len(b["segs"])
                    dve.wait_ge(expd.sem, expd.base + j + 1)
                    link(nc.vector.reciprocal(li[:, j, 0:m], ls[:, j, 0:m]))
                    dve.wait_ge(mixed.sem, mixed.base + j + 1)
                    if m == 1:
                        nc.vector.tensor_scalar(b["out"], k.pb[4 + j % 2][:, 0:DH], li[:, j, 0:1], None,
                                                ALU.mult).then_inc(out_free.sem, 1)
                    else:
                        nc.vector.tensor_tensor(
                            b["out"], k.pb[4 + j % 2][:, 0:m * DH].rearrange("p (m e) -> p m e", m=m),
                            li[:, j, 0:m].unsqueeze(2).to_broadcast([P, m, DH]), ALU.mult).then_inc(out_free.sem, 1)
            if lse is not None:
                dve.wait_ge(chain_act.sem, chain_act.base + 1)
                for dst, i, n in lse:
                    nc.vector.tensor_tensor(dst, mx[:, i, 0:n], nm[:, i, 0:n], ALU.subtract)
                chain_act.base += 1
    for s in (scored, negmax, expd, turned, mixed, out_free):
        s.base += nb
    ev_act.base += (nb + 1) // 2
    ev_dve.base += nb // 2


def stage_turn(k, items, before=None):
    nc = k.nc
    n = len(items)
    turned, ev_act, ev_dve, fed = (k.sig(x) for x in ("turn_done", "turn_evac_act", "turn_evac_dve", "turn_fed"))
    release, a, v = [], ev_act.base, ev_dve.base
    for j, it in enumerate(items):
        both = isinstance(it[2], Split)
        a += both or j % 2 == 0
        v += both or j % 2 == 1
        release.append((ev_dve.sem, v) if both or j % 2 else (ev_act.sem, a))
    a0 = ev_act.base
    with nc.Block() as block:
        @block.vector
        def _(dve):
            if before is not None:
                before(dve).then_inc(fed.sem, 1)
            for j, (_, m, dst, gain) in enumerate(items):
                src = k.pb[j % 4][0:m, :]
                if isinstance(dst, Split):
                    dve.wait_ge(ev_act.sem, a0 + j + 1)
                    nc.vector.scalar_tensor_tensor(out=dst.lo, in0=src, scalar=1.0 if gain is None else gain,
                                                   in1=plain(dst.hi), op0=ALU.mult,
                                                   op1=ALU.subtract).then_inc(ev_dve.sem, 1)
                elif j % 2:
                    dve.wait_ge(turned.sem, turned.base + j + 1)
                    nc.vector.tensor_copy(dst, src).then_inc(ev_dve.sem, 1)

        @block.scalar
        def _(act):
            for j, (_, m, dst, gain) in enumerate(items):
                src = k.pb[j % 4][0:m, :]
                if isinstance(dst, Split):
                    act.wait_ge(turned.sem, turned.base + j + 1)
                    nc.scalar.mul(dst.hi, src, 1.0 if gain is None else gain).then_inc(ev_act.sem, 1)
                elif j % 2 == 0:
                    act.wait_ge(turned.sem, turned.base + j + 1)
                    nc.scalar.copy(dst, src).then_inc(ev_act.sem, 1)

        @block.tensor
        def _(pe):
            if before is not None:
                pe.wait_ge(fed.sem, fed.base + 1)
            for j, (srcs, m, dst, gain) in enumerate(items):
                if j >= 4:
                    sem, count = release[j - 4]
                    pe.wait_ge(sem, count)
                for t, s in enumerate(srcs):
                    last = nc.tensor.transpose(k.pb[j % 4][0:m, t * P:(t + 1) * P], s, k.ident[:, :])
                last.then_inc(turned.sem, 1)
    turned.base += n
    ev_act.base, ev_dve.base = a, v
    fed.base += before is not None


def rotate(k, dve, x1, x2, cos, sin, tmp):
    v, s = k.nc.vector, k.sig("dve_chain")
    link = Chain(dve, s)
    for dst, a, b in ((tmp[0], x1, cos), (tmp[1], x2, sin), (tmp[2], x2, cos)):
        v.tensor_tensor(dst, a, b, ALU.mult)
    link(v.tensor_tensor(tmp[3], x1, sin, ALU.mult))
    v.tensor_tensor(x1, tmp[0], tmp[1], ALU.subtract)
    return v.tensor_tensor(x2, tmp[2], tmp[3], ALU.add)


def stage_residual(k, tag, y, gain_name, tmp_kb, out=None):
    nc, d = k.nc, k.d
    sq, root, g_in, scaled, added = (k.sig(x) for x in ("res_sumsq", "res_root", "res_gain", "res_scaled", "res_added"))
    gain = k.sb(f"resgain_{tag}", tmp_kb, [P, D])
    tmp = k.sb(f"restmp_{tag}", tmp_kb + 4, [P, 2, D])
    ms, rs, half = k.stat[:, 0:T], k.stat[:, T:2 * T], k.stat[:, 2 * T:3 * T]
    stored = k.sig("stored")
    with nc.Block() as block:
        @block.sync
        def _(sp):
            sp.dma_start(gain[:, :], d[gain_name].rearrange("(a n) -> a n", a=1).to_broadcast([P, D])).then_inc(g_in.sem, 16)
            if out is not None:
                for t in range(T):
                    sp.wait_ge(added.sem, added.base + t + 1)
                    sp.dma_start(out[t * P:(t + 1) * P, :], k.h[:, t, :]).then_inc(stored.sem, 16)
                sp.wait_ge(stored.sem, 16 * T)

        @block.scalar
        def _(act):
            for t in range(T):
                nc.scalar.activation(tmp[:, 0, :], y[:, t, :], ACT.Square,
                                     accum_out=k.stat[:, t:t + 1]).then_inc(sq.sem, 1)
                act.wait_ge(sq.sem, sq.base + t + 1)

        @block.gpsimd
        def _(pool):
            pool.wait_ge(root.sem, root.base + 2)
            nc.gpsimd.tensor_tensor(rs, ms, half, ALU.pow).then_inc(root.sem, 1)

        @block.vector
        def _(dve):
            nc.vector.memset(half, -0.5).then_inc(root.sem, 1)
            dve.wait_ge(sq.sem, sq.base + T)
            nc.vector.tensor_scalar(ms, ms, 1.0 / D, EPS, ALU.mult, ALU.add).then_inc(root.sem, 1)
            dve.wait_ge(root.sem, root.base + 3)
            dve.wait_ge(g_in.sem, g_in.base + 16)
            for t in range(T):
                if t >= 2:
                    dve.wait_ge(added.sem, added.base + t - 1)
                nc.vector.scalar_tensor_tensor(out=tmp[:, t % 2, :], in0=y[:, t, :], scalar=rs[:, t:t + 1],
                                               in1=gain[:, :], op0=ALU.mult, op1=ALU.mult).then_inc(scaled.sem, 1)
                dve.wait_ge(scaled.sem, scaled.base + t + 1)
                nc.vector.tensor_tensor(k.h[:, t, :], k.h[:, t, :], tmp[:, t % 2, :], ALU.add).then_inc(added.sem, 1)
    sq.base += T
    root.base += 3
    g_in.base += 16
    scaled.base += T
    added.base += T


def gemm(k, g, kt, per, tiles, j):
    steps = []
    for k0 in range(0, kt, per):
        k1 = min(k0 + per, kt)
        for n, (m, cols, lhs, rhs, (c0, width, row)) in enumerate(tiles):
            pairs = []
            for f in range(k0, k1):
                w = slot(k, g, (f - k0) * row + c0, (f - k0) * row + c0 + width)
                pairs.append((lhs(f) if lhs else w, rhs(f) if rhs else w))
            steps.append((g, j + n, k.pb[(j + n) % 8][0:m, 0:cols], pairs, k0 == 0, k1 == kt))
        g += 1
    return steps, j + len(tiles), g


def token_tiles(lhs, cols, row):
    return [(P, n, lambda f, t=t, perm=perm: lhs(perm, f, t), None, (c0, n, row)) for c0, n, perm in cols for t in range(T)]


def feature_tiles(rhs, cols, row, m=P):
    return [(m, S, None, lambda f: rhs[:, f, :], (c0, m, row)) for c0 in cols]


def first_block(k):
    nc, d = k.nc, k.d
    g = 0
    stage_norm_T(k, "x", k.h, D, "mix_pre", k.xT, 104)

    qk = k.sb("qkA", 104, [P, 3, T, 512])
    v = k.sb("vA", 128, [P, 3, T, 256])
    kvc = k.sb("kvc", 140, [P, T, 256])
    qc = k.sb("qc", 144, [P, T, 512])
    kpe = k.sb("kpe", 152, [P, T, 32])
    gates = k.sb("gates", 152.5, [P, 16, S])
    steps, dst, j = [], [], 0
    plan = [([(0, 512, 0)], [qk[:, 0]]), ([(0, 512, 1)], [qk[:, 1]]), ([(0, 512, 2)], [qk[:, 2]]),
            ([(0, 256, 0), (256, 256, 1)], [v[:, 0], v[:, 1]]), ([(0, 256, 2), (256, 256, 0)], [v[:, 2], kvc]),
            ([(0, 512, 0)], [qc])]
    lhs = lambda perm, f, t: tokens(k, perm, f, t)
    for cols, dsts in plan:
        s, j, g = gemm(k, g, KD, 4, token_tiles(lhs, cols, 512), j)
        steps += s
        for x in dsts:
            dst += [x[:, t, :] for t in range(T)]
    s, j, g = gemm(k, g, KD, 8, token_tiles(lhs, [(0, 32, 0)], 32), j)
    steps += s
    dst += [kpe[:, t, :] for t in range(T)]
    gate0 = j
    for _ in range(4):
        s, j, g = gemm(k, g, KD, 4, feature_tiles(k.xT, range(0, 512, P), 512), j)
        steps += s

    def evac_proj(who, eng, j, ps):
        if j < gate0:
            return copy_out(k, who, dst[j], ps)
        i = j - gate0
        return nc.scalar.activation(gates[:, i, :], ps, ACT.Sigmoid, bias=col(k, "b_gate", i))

    stage_gemm(k, steps, evac_proj, lambda j: "act" if j >= gate0 or j % 2 == 0 else "dve")

    tmp = k.sb("ropetmp", 185, [P, 4, 3 * T, 8, 8])
    qh = qk[:, :, :, :].rearrange("p g t (h e) -> p (g t) h e", h=8)
    tab = k.ropeA[:, :, :, :].rearrange("p g t c -> p (g t) c")
    cos = tab[:, :, 0:8].unsqueeze(2).to_broadcast([P, 3 * T, 8, 8])
    sin = tab[:, :, 8:16].unsqueeze(2).to_broadcast([P, 3 * T, 8, 8])
    qkT = k.sb("qkT", 16, [P, 3, 4, S])
    items = [([qk[:, g_, t, f * P:(f + 1) * P] for t in range(T)], P, qkT[:, g_, f, :], None)
             for g_ in range(3) for f in range(4)]

    def rope_a(dve):
        return rotate(k, dve, qh[:, :, :, 0:8], qh[:, :, :, 8:16], cos, sin, [tmp[:, i] for i in range(4)])

    stage_turn(k, items, rope_a)
    oA = k.sb("oA", 195, [P, 3, T, 260])
    batches, lse = [], []
    for grp in range(3):
        for h in range(A_HEADS):
            lo = DH * (h % 2)
            q, kk = qkT[lo:lo + DH, grp, h // 2, :], qkT[lo:lo + DH, grp, 2 + h // 2, :]
            if grp:
                mask = (k.mask_d4, k.mask_d16)[grp - 1]
                batches.append(dict(
                    segs=[(t * P, (t + 1) * P) for t in range(T)],
                    scores=[[(q[:, t * P:(t + 1) * P], kk[:, t * P:(t + 1) * P], t * P, (t + 1) * P),
                             (k.identb[:, :], mask[:, :], t * P, (t + 1) * P)] for t in range(T)],
                    values=[[v[:, grp, t, h * DH:(h + 1) * DH]] for t in range(T)],
                    out=oA[:, grp, :, h * DH:(h + 1) * DH]))
                lse.append((oA[:, grp, :, 256 + h], len(batches) - 1, T))
            else:
                for t in range(T):
                    a, b = max(t - 1, 0), min(t + 2, T)
                    w = (b - a) * P
                    m0 = (a - t + 1) * P
                    batches.append(dict(
                        segs=[(0, w)],
                        scores=[[(q[:, t * P:(t + 1) * P], kk[:, a * P:b * P], 0, w),
                                 (k.identb[:, :], k.mask_band[:, m0:m0 + w], 0, w)]],
                        values=[[v[:, grp, u, h * DH:(h + 1) * DH] for u in range(a, b)]],
                        out=oA[:, grp, t, h * DH:(h + 1) * DH]))
                    lse.append((oA[:, grp, t, 256 + h:257 + h], len(batches) - 1, 1))
    stage_attention(k, batches, DH ** -0.5, 185, lse)
    mixAT = k.split("mixAT", 122, [P, 2, S], 126)
    stage_combine(k, oA)
    oc = k.oc
    stage_turn(k, [([oc[:, t, f * P:(f + 1) * P] for t in range(T)], P, mixAT[:, f, :], None) for f in range(2)])

    qcT = k.split("qcT", 16, [P, 4, S], 24)
    kvcT = k.split("kvcT", 32, [P, 2, S], 36)
    stage_norm_T(k, "qc", qc, 512, "q_norm", qcT, 104)
    stage_norm_T(k, "kvc", kvc, 256, "kv_norm", kvcT, 104)
    qB = k.sb("qB", 104, [P, T, 8, 96])
    kB = k.sb("kB", 130, [P, T, 8, 96])
    vB = k.sb("vB", 142, [P, T, 8, DH])
    steps, dst, j = [], [], 0
    for _ in range(2):
        s, j, g = gemm(k, g, 4, 4, token_tiles(lambda perm, f, t: qcT[:, f, t * P:(t + 1) * P], [(0, 384, 0)], 384), j)
        steps += s
    s, j, g = gemm(k, g, 2, 2, token_tiles(lambda perm, f, t: kvcT[:, f, t * P:(t + 1) * P],
                                           [(0, 512, 0), (512, 512, 0)], 1024), j)
    steps += s

    def evac_b(who, eng, j, ps):
        t, half = j % 4, (j // 4) % 2
        if j < 8:
            return copy_out(k, who, qB[:, t, half * 4:half * 4 + 4, :].rearrange("p h e -> p (h e)"), ps)
        kv = ps.rearrange("p (h e) -> p h e", h=4)
        copy_out(k, who, kB[:, t, half * 4:half * 4 + 4, 0:DH], kv[:, :, 0:DH])
        return copy_out(k, who, vB[:, t, half * 4:half * 4 + 4, :], kv[:, :, DH:])

    stage_gemm(k, steps, evac_b)
    tmpq = k.sb("ropetmpq", 195, [P, 4, T, 8, 16])
    tmpk = k.sb("ropetmpk", 203, [P, 4, T, 16])
    qTb = k.sb("qTb", 16, [P, 8, S])
    kTb = k.sb("kTb", 32, [P, 8, S])

    def rope_b(dve):
        link = Chain(dve, k.sig("dve_chain"))
        cos, sin = k.ropeB[:, :, 0:16], k.ropeB[:, :, 16:32]
        rotate(k, dve, qB[:, :, :, 64:80], qB[:, :, :, 80:96], cos.unsqueeze(2).to_broadcast([P, T, 8, 16]),
               sin.unsqueeze(2).to_broadcast([P, T, 8, 16]), [tmpq[:, i] for i in range(4)])
        link(rotate(k, dve, kpe[:, :, 0:16], kpe[:, :, 16:32], cos, sin, [tmpk[:, i] for i in range(4)]))
        return nc.vector.tensor_copy(kB[:, :, :, DH:96], kpe[:, :, :].unsqueeze(2).to_broadcast([P, T, 8, 32]))

    items = []
    for h in range(B_HEADS):
        items.append(([qB[:, t, h, :] for t in range(T)], 96, qTb[0:96, h, :], None))
        items.append(([kB[:, t, h, :] for t in range(T)], 96, kTb[0:96, h, :], None))
    stage_turn(k, items, rope_b)
    oB = k.sb("oB", 104, [P, T, 512])
    batches = []
    for t in range(T):
        for h in range(B_HEADS):
            batches.append(dict(
                segs=[(0, S)], scores=[[(qTb[0:96, h, t * P:(t + 1) * P], kTb[0:96, h, :], 0, S)]],
                values=[[vB[:, u, h, :] for u in range(T)]], out=oB[:, t, h * DH:(h + 1) * DH]))
    stage_attention(k, batches, B_QK ** -0.5, 185)
    oBT = k.split("oBT", 130, [P, 4, S], 138)
    stage_turn(k, [([oB[:, t, f * P:(f + 1) * P] for t in range(T)], P, oBT[:, f, :], None) for f in range(4)])

    mixT = k.split("mixT", 16, [P, KD, S], 32)
    ga, gb = k.sb("gated_a", 185, [P, KD, S]), k.sb("gated_b", 104, [P, 2, S])
    steps, j = [], 0
    s, j, g = gemm(k, g, 2, 2, feature_tiles(mixAT, range(0, D, P), D), j)
    steps += s
    for _ in range(2):
        s, j, g = gemm(k, g, 4, 4, feature_tiles(oBT, range(0, 512, P), 512), j)
        steps += s
    link2 = k.sig("dve_chain")
    made = k.sig("gated_made")
    base = made.base

    def gated(who, eng, j, ps):
        if j < KD:
            return nc.vector.tensor_tensor(ga[:, j, :], gates[:, j, :], ps, ALU.mult)
        f = j - KD
        link = Chain(eng, link2)
        link(nc.vector.tensor_tensor(gb[:, f % 2, :], gates[:, j, :], ps, ALU.mult))
        nc.vector.tensor_tensor(ga[:, f, :], ga[:, f, :], gb[:, f % 2, :], ALU.add).then_inc(made.sem, 1)
        eng.wait_ge(made.sem, base + 2 * f + 2)
        return nc.vector.tensor_tensor(mixT.lo[:, f, :], ga[:, f, :], plain(mixT.hi[:, f, :]), ALU.subtract)

    def high(act):
        for f in range(KD):
            act.wait_ge(made.sem, base + 2 * f + 1)
            nc.scalar.copy(mixT.hi[:, f, :], ga[:, f, :]).then_inc(made.sem, 1)

    stage_gemm(k, steps, gated, lambda j: "dve", high)
    made.base += 2 * KD
    y = k.sb("y1", 104, [P, T, D])
    g = stage_out_product(k, g, mixT, y)
    stage_residual(k, "mix1", y, "norm_mix_post", 130)

    stage_norm_T(k, "h1", k.h, D, "mlp_pre", k.xT, 104)
    H = FF1 // P // 2
    hid = k.split("hid1", 104, [P, H, S], 136)
    y = k.sb("y2", 168, [P, T, D])
    r, r2 = k.sb("relu", 185, [P, 2, S]), k.sb("relu2", 189, [P, 2, S])
    for half in range(2):
        steps, j = [], 0
        for _ in range(H // 4):
            s, j, g = gemm(k, g, KD, 4, feature_tiles(k.xT, range(0, 512, P), 512), j)
            steps += s
        fv, ra = k.sig("gemm_free_dve"), k.sig("relu_done")
        b_fv, b_ra = fv.base, ra.base

        def relu2(who, eng, j, ps):
            if who == "act":
                if j >= 2:
                    eng.wait_ge(fv.sem, b_fv + j - 1)
                nc.scalar.activation(r[:, j % 2, :], ps, ACT.Relu).then_inc(ra.sem, 1)
                eng.wait_ge(ra.sem, b_ra + j + 1)
                return nc.scalar.activation(hid.hi[:, j, :], r[:, j % 2, :], ACT.Square)
            Chain(eng, link2)(nc.vector.tensor_tensor(r2[:, j % 2, :], r[:, j % 2, :], r[:, j % 2, :], ALU.mult))
            return nc.vector.tensor_tensor(hid.lo[:, j, :], r2[:, j % 2, :], plain(hid.hi[:, j, :]), ALU.subtract)

        stage_gemm(k, steps, relu2, lambda j: "both")
        ra.base += H
        g = stage_down_product(k, g, hid, H, y, half == 1)
    stage_residual(k, "mlp1", y, "norm_mlp_post", 185)
    k.g = g
    return None


def stage_out_product(k, g, lhs, y):
    steps, j = [], 0
    for _ in range(2):
        s, j, g = gemm(k, g, KD, 4, token_tiles(lambda perm, f, t: lhs[:, f, t * P:(t + 1) * P], [(0, 512, 0)], 512), j)
        steps += s
    stage_gemm(k, steps, lambda who, eng, j, ps: copy_out(k, who, y[:, j % T, (j // T) * 512:(j // T) * 512 + 512], ps))
    return g


def stage_down_product(k, g, hid, kt, y, more):
    steps, j = [], 0
    for _ in range(2):
        s, j, g = gemm(k, g, kt, 4, token_tiles(lambda perm, f, t: hid[:, f, t * P:(t + 1) * P], [(0, 512, 0)], 512), j)
        steps += s

    def evac(who, eng, j, ps):
        dst = y[:, j % T, (j // T) * 512:(j // T) * 512 + 512]
        return k.nc.vector.tensor_tensor(dst, dst, ps, ALU.add) if more else copy_out(k, who, dst, ps)

    stage_gemm(k, steps, evac, (lambda j: "dve") if more else None)
    return g


def stage_combine(k, oA):
    nc, d = k.nc, k.d
    sent, back, done = k.sig("combine_sent"), k.sig("combine_back"), k.sig("combine_done")
    W = 260
    nat = k.sb("natA", 104, [P, 2, T, W])
    oc = k.sb("oc", 113, [P, T, 256])
    t2 = k.sb("combtmp", 117, [P, T, 256])
    w3 = k.sb("w3", 121, [P, 3, T, 4])
    mxw = k.sb("mxw", 121.25, [P, T, 4])
    sumw = k.sb("sumw", 121.5, [P, T, 4])
    k.oc = oc
    scr = d["scratch"]
    with nc.Block() as block:
        @block.sync
        def _(sp):
            n = 0
            for t in range(T):
                for i in range(2):
                    sp.dma_start(scr[i, t::T, :], oA[:, 1 + i, t, :]).then_inc(sent.sem, 16)
                    n += 1
            sp.wait_ge(sent.sem, 16 * n)
            for i in range(2):
                sp.dma_start(nat[:, i, :, :], scr[i].rearrange("(t p) n -> p t n", p=P)).then_inc(back.sem, 16)

        @block.vector
        def _(dve):
            link = Chain(dve, k.sig("dve_chain"))
            v = nc.vector
            dve.wait_ge(back.sem, 32)
            src = [oA[:, 0, :, :], nat[:, 0, :, :], nat[:, 1, :, :]]
            ls = [s[:, :, 256:260] for s in src]
            link(v.tensor_tensor(mxw[:, :, :], ls[0], ls[1], ALU.max))
            link(v.tensor_tensor(mxw[:, :, :], mxw[:, :, :], ls[2], ALU.max))
            for i in range(3):
                v.tensor_tensor(w3[:, i], ls[i], mxw[:, :, :], ALU.subtract).then_inc(done.sem, 1)
            dve.wait_ge(done.sem, 4)
            link(v.tensor_tensor(sumw[:, :, :], w3[:, 0], w3[:, 1], ALU.add))
            link(v.tensor_tensor(sumw[:, :, :], sumw[:, :, :], w3[:, 2], ALU.add))
            link(v.reciprocal(sumw[:, :, :], sumw[:, :, :]))
            link(v.tensor_tensor(w3[:, :, :, :], w3[:, :, :, :],
                                 sumw[:, :, :].unsqueeze(1).to_broadcast([P, 3, T, 4]), ALU.mult))
            for i in range(3):
                dst = (oc if i == 0 else t2)[:, :, :].rearrange("p t (h e) -> p (t h) e", h=4)
                link(v.tensor_tensor(
                    dst.rearrange("p (t h) e -> p t h e", t=T), src[i][:, :, 0:256].rearrange("p t (h e) -> p t h e", h=4),
                    w3[:, i].unsqueeze(3).to_broadcast([P, T, 4, DH]), ALU.mult))
                if i:
                    link(v.tensor_tensor(oc[:, :, :], oc[:, :, :], t2[:, :, :], ALU.add))

        @block.scalar
        def _(act):
            act.wait_ge(done.sem, 3)
            nc.scalar.activation(w3[:, :, :, :], w3[:, :, :, :], ACT.Exp).then_inc(done.sem, 1)


def second_block(k, out):
    nc, d, g = k.nc, k.d, k.g
    stage_norm_T(k, "h2", k.h, D, "mix_pre2", k.xT, 104)

    s5 = stage_s5_parameters(k)

    fm = k.sb("fm", 104, [P, 14, S])
    grow = k.sb("grow", 132, [P, 3, S])
    tm = k.sb("tm", 138, [P, 5, T, 256])
    steps, j = [], 0
    for c in range(3):
        s, j, g = gemm(k, g, KD, 4, feature_tiles(k.xT, range(0, 512, P), 512), j)
        steps += s
    s, j, g = gemm(k, g, KD, 4, feature_tiles(k.xT, (0, P), 352) + feature_tiles(k.xT, (2 * P,), 352, m=96), j)
    steps += s
    j_tm = j
    lhs = lambda perm, f, t: k.xT[:, f, t * P:(t + 1) * P]
    for c in range(2):
        s, j, g = gemm(k, g, KD, 4, token_tiles(lhs, [(0, 256, 0), (256, 256, 0)], 512), j)
        steps += s
    s, j, g = gemm(k, g, KD, 8, token_tiles(lhs, [(0, 256, 0)], 256), j)
    steps += s
    FOX_Q = 6

    def evac(who, eng, j, ps):
        if j < 14:
            if FOX_Q <= j < FOX_Q + 2:
                return (nc.scalar.mul(fm[:, j, :], ps, DH ** -0.5) if who == "act" else
                        nc.vector.tensor_scalar(fm[:, j, :], ps, DH ** -0.5, None, ALU.mult))
            return copy_out(k, who, fm[:, j, :], ps)
        if j == 14:
            for i in range(3):
                x = nc.scalar.activation(grow[0:4, i, :], ps[32 * i:32 * i + 4, :], ACT.Identity,
                                         bias=col(k, "gate_b", i)[0:4, :])
            return x
        i = j - j_tm
        return copy_out(k, who, tm[:, i // T, i % T, :], ps)

    stage_gemm(k, steps, evac)
    k.fm, k.grow, k.tm = fm, grow, tm
    k.ycat = k.sb("ycat", 16, [P, T, D])
    k.sel = k.sb("sel", 172.5, [P, 4, S])
    g = stage_s5(k, s5, g)
    stage_gate_rows(k)
    stage_fox(k)
    stage_mlstm(k)
    stage_hgrn(k)
    stage_finish(k)
    ycT = k.split("ycT", 104, [P, KD, S], 120)
    stage_turn(k, [([k.ycat[:, t, f * P:(f + 1) * P] for t in range(T)], P, ycT[:, f, :], col(k, "mix_gain2", f))
                   for f in range(KD)])
    y = k.sb("y3", 136, [P, T, D])
    g = stage_out_product(k, g, ycT, y)
    stage_residual(k, "mix2", y, "ln_mix_post_2", 152)

    stage_norm_T(k, "h3", k.h, D, "ffn_pre2", k.xT, 104)
    hid = k.split("hid2", 104, [P, FF2_PARTS[0], S], 128)
    y = k.sb("y4", 152, [P, T, D])
    for part, tiles in enumerate(FF2_PARTS):
        g = stage_swiglu(k, g, hid, tiles, part)
        g = stage_down_product(k, g, hid, tiles, y, part == 1)
    stage_residual(k, "mlp2", y, "ln_ffn_post_2", 176, out=out[0])
    return None


def stage_swiglu(k, g, hid, n, part):
    nc = k.nc
    done, sgd, made, high = k.sig("glu_done"), k.sig("glu_sigmoid"), k.sig("glu_made"), k.sig("glu_high")
    sg = k.sb(f"glu_sg{part}", 168, [P, 2, S])
    full = k.sb(f"glu_full{part}", 172, [P, 2, S])
    steps, j, g0 = [], 0, g
    for _ in range(n):
        s, j, g = gemm(k, g, KD, 8, feature_tiles(k.xT, (0, P), 2 * P), j)
        steps += s
    note_freed(k, steps, done)
    with nc.Block() as block:
        @block.sync
        def _(sp):
            issue_chunks(k, sp, g + SLOTS)

        @block.tensor
        def _(pe):
            for c, j, out, pairs, first, last in steps:
                if j % 2 == 0:
                    wait_chunk(k, pe, c)
                    if j >= 8:
                        pe.wait_ge(made.sem, made.base + j // 2 - 3)
                products(k, out, pairs, first, last).then_inc(done.sem, 1)

        @block.scalar
        def _(act):
            for f in range(n + 1):
                if f < n:
                    split_hi(k, act, g0 + f + LEAD)
                    act.wait_ge(done.sem, done.base + 2 * f + 1)
                    if f >= 2:
                        act.wait_ge(made.sem, made.base + f - 1)
                    nc.scalar.activation(sg[:, f % 2, :], k.pb[(2 * f) % 8][:, :], ACT.Sigmoid).then_inc(sgd.sem, 1)
                if f >= 1:
                    act.wait_ge(made.sem, made.base + f)
                    nc.scalar.copy(hid.hi[:, f - 1, :], full[:, (f - 1) % 2, :]).then_inc(high.sem, 1)
            split_hi(k, act, g + LEAD)

        @block.vector
        def _(dve):
            chain = Chain(dve, k.sig("dve_chain"))
            for f in range(n + 1):
                if f < n:
                    split_lo(k, dve, g0 + f + LEAD)
                    x = full[:, f % 2, :]
                    dve.wait_ge(sgd.sem, sgd.base + f + 1)
                    chain(nc.vector.tensor_tensor(x, sg[:, f % 2, :], k.pb[(2 * f) % 8][:, :], ALU.mult))
                    dve.wait_ge(done.sem, done.base + 2 * f + 2)
                    nc.vector.tensor_tensor(x, x, k.pb[(2 * f + 1) % 8][:, :], ALU.mult).then_inc(made.sem, 1)
                if f >= 1:
                    dve.wait_ge(high.sem, high.base + f)
                    dve.wait_ge(made.sem, made.base + f)
                    chain(nc.vector.tensor_tensor(hid.lo[:, f - 1, :], full[:, (f - 1) % 2, :],
                                                  plain(hid.hi[:, f - 1, :]), ALU.subtract))
            split_lo(k, dve, g + LEAD)
    done.base += 2 * n
    sgd.base += n
    made.base += n
    high.base += n
    return g


def stage_s5_parameters(k):
    nc, d = k.nc, k.d
    v, a = nc.vector, nc.scalar
    sm = k.sb("s5_small", 206, [P, 24, 8])
    er, ei = k.sb("s5_er", 174, [P, 8, S]), k.sb("s5_ei", 190, [P, 8, S])
    br, bi = k.sb("s5_b_re", 136, [P, 8, 32]), k.sb("s5_b_im", 137, [P, 8, 32])
    bb = k.sb("s5_bb", 138, [P, 2, 8, 32])
    bt = k.sb("s5_bt", 140, [P, 2, 8, 32])
    bT = k.sb("s5_bT", 158, [P, 2, 2, P])
    cT = k.sb("s5_cT", 160, [P, 4, 8, 32])
    tmp = k.sb("s5_tmp", 120, [P, 2, 8, 256])
    (DT, LR, MAG, TH, N1, RE, SN, AB, CS, AR, AI, DEN, A1, T1, T2, CR, CI, WR, WI, W2, W3) = [
        sm[:, i, :] for i in range(21)]
    p_in, hand = k.sig("s5_in"), k.sig("s5_hand")
    s = k.sig("dve_chain")
    h0 = hand.base
    turned = k.sig("s5_turned")
    PI = float(np.pi)
    with nc.Block() as block:
        @block.sync
        def _(sp):
            for dst, n in ((br, "s5_b_re"), (bi, "s5_b_im")):
                sp.dma_start(dst[:, :, :], d[n]).then_inc(p_in.sem, 16)
            sp.dma_start(cT[:, 0:2, :, :], d["s5_cT"]).then_inc(p_in.sem, 16)

        @block.scalar
        def _(act):
            a.activation(DT, col(k, "log_dt", 0, 8), ACT.Exp).then_inc(hand.sem, 1)
            act.wait_ge(hand.sem, h0 + 2)
            a.activation(MAG, MAG, ACT.Exp).then_inc(hand.sem, 1)
            a.activation(SN, RE, ACT.Sin).then_inc(hand.sem, 1)
            a.activation(CS, AB, ACT.Sin).then_inc(hand.sem, 1)

        @block.vector
        def _(dve):
            link = Chain(dve, s)
            tt, ts = v.tensor_tensor, v.tensor_scalar
            link(ts(LR, col(k, "lam_re", 0, 8), -1e-4, None, ALU.min))
            dve.wait_ge(hand.sem, h0 + 1)
            tt(MAG, LR, DT, ALU.mult)
            link(tt(TH, col(k, "lam_im", 0, 8), DT, ALU.mult))
            link(ts(N1, TH, 1.0 / (2 * PI), 12582912.0, ALU.mult, ALU.add))
            link(ts(N1, N1, 12582912.0, None, ALU.subtract))
            link(v.scalar_tensor_tensor(out=RE, in0=N1, scalar=-6.28125, in1=TH, op0=ALU.mult, op1=ALU.add))
            c2 = float(np.float32(np.round((2 * np.pi - 6.28125) * 2 ** 22) / 2 ** 22))
            link(v.scalar_tensor_tensor(out=RE, in0=N1, scalar=-c2, in1=RE, op0=ALU.mult, op1=ALU.add))
            link(v.scalar_tensor_tensor(out=RE, in0=N1, scalar=-float(2 * np.pi - 6.28125 - c2), in1=RE,
                                        op0=ALU.mult, op1=ALU.add))
            link(ts(RE, RE, 3.1415925, -3.1415925, ALU.min, ALU.max))
            link(ts(AB, RE, -1.0, None, ALU.mult))
            link(tt(AB, AB, RE, ALU.max))
            ts(AB, AB, -1.0, PI / 2, ALU.mult, ALU.add).then_inc(hand.sem, 1)
            dve.wait_ge(hand.sem, h0 + 5)
            tt(AR, MAG, CS, ALU.mult)
            link(tt(AI, MAG, SN, ALU.mult))
            li = col(k, "lam_im", 0, 8)
            tt(T1, LR, LR, ALU.mult)
            link(tt(T2, li, li, ALU.mult))
            link(tt(DEN, T1, T2, ALU.add))
            link(v.reciprocal(DEN, DEN))
            link(ts(A1, AR, -1.0, None, ALU.add))
            tt(T1, A1, LR, ALU.mult)
            link(tt(T2, AI, li, ALU.mult))
            link(tt(CR, T1, T2, ALU.add))
            tt(CR, CR, DEN, ALU.mult)
            tt(T1, AI, LR, ALU.mult)
            link(tt(T2, A1, li, ALU.mult))
            link(tt(CI, T1, T2, ALU.subtract))
            link(tt(CI, CI, DEN, ALU.mult))
            dve.wait_ge(p_in.sem, p_in.base + 48)
            crb, cib = (c.unsqueeze(2).to_broadcast([P, 8, 32]) for c in (CR, CI))
            tt(bb[:, 0], br[:, :, :], crb, ALU.mult)
            tt(bb[:, 1], bi[:, :, :], crb, ALU.mult)
            tt(bt[:, 0], bi[:, :, :], cib, ALU.mult)
            link(tt(bt[:, 1], br[:, :, :], cib, ALU.mult))
            link(tt(bb[:, 0], bb[:, 0], bt[:, 0], ALU.subtract))
            tt(bb[:, 1], bb[:, 1], bt[:, 1], ALU.add).then_inc(turned.sem, 1)
            ts(cT[:, 2], cT[:, 1], -1.0, None, ALU.mult)
            ts(cT[:, 3], cT[:, 0], -1.0, None, ALU.mult)
            for c in range(2):
                for jj in range(2):
                    dve.wait_ge(turned.sem, turned.base + 2 + 2 * c + jj)
                    v.tensor_copy(bT[:, c, jj, :], k.pb[c * 2 + jj][:, 0:P])
            v.memset(er[:, :, 0:1], 1.0)
            v.memset(ei[:, :, 0:1], 0.0)
            v.tensor_copy(WR, CS)
            link(v.tensor_copy(WI, SN))
            n = 1
            while n < S:
                wr, wi = (w.unsqueeze(2).to_broadcast([P, 8, n]) for w in (WR, WI))
                t0, t1 = tmp[:, 0, :, 0:n], tmp[:, 1, :, 0:n]
                tt(t0, er[:, :, 0:n], wr, ALU.mult)
                link(tt(t1, ei[:, :, 0:n], wi, ALU.mult))
                link(tt(er[:, :, n:2 * n], t0, t1, ALU.subtract))
                tt(t0, er[:, :, 0:n], wi, ALU.mult)
                link(tt(t1, ei[:, :, 0:n], wr, ALU.mult))
                tt(ei[:, :, n:2 * n], t0, t1, ALU.add)
                tt(T1, WR, WR, ALU.mult)
                tt(T2, WI, WI, ALU.mult)
                link(tt(W2, WR, WI, ALU.mult))
                link(tt(WR, T1, T2, ALU.subtract))
                link(ts(WI, W2, 2.0, None, ALU.mult))
                n *= 2

        @block.tensor
        def _(pe):
            pe.wait_ge(turned.sem, turned.base + 1)
            for c in range(2):
                for jj in range(2):
                    nc.tensor.transpose(k.pb[c * 2 + jj][:, 0:P],
                                        bb[:, c, 4 * jj:4 * jj + 4, :].rearrange("p j c -> p (j c)"),
                                        k.ident[:, :]).then_inc(turned.sem, 1)
    p_in.base += 48
    hand.base += 5
    turned.base += 5
    return dict(mag=MAG, er=er, ei=ei, bT=bT, cT=cT)


def stage_s5(k, s5, g):
    nc, d = k.nc, k.d
    er, ei, bT, cT, mag = s5["er"], s5["ei"], s5["bT"], s5["cT"], s5["mag"]
    pr = k.sb("s5_pr", 16, [P, 4, S])
    vv = k.sb("s5_v", 24, [P, 2, S])
    yy = k.sb("s5_y", 28, [P, 2, S])
    qq = k.sb("s5_q", 32, [P, 2, 4, S])
    yS = k.sb("s5_yS", 164, [P, 2, S])
    bu, scanned, prod, out_done, outp = (k.sig(x) for x in ("s5_bu", "s5_scan", "s5_prod", "s5_out", "s5_bu_free"))
    chain = k.sig("dve_chain")
    uT = k.fm[:, 0:2, :]
    with nc.Block() as block:
        @block.tensor
        def _(pe):
            def inject(j):
                q = 32 * (j % 4)
                if j >= 2:
                    pe.wait_ge(outp.sem, outp.base + j - 1)
                for c in range(2):
                    mm = nc.tensor.matmul(k.pb[2 * (j % 2) + c][:, :], bT[q:q + 32, c, j // 4, :],
                                          uT[q:q + 32, j // 4, :], start=True, stop=True,
                                          tile_position=(q, 0))
                mm.then_inc(bu.sem, 1)

            def project(j):
                q = 32 * (j % 4)
                pe.wait_ge(prod.sem, prod.base + j + 1)
                for m, c in enumerate((0, 3, 2, 2)):
                    mm = nc.tensor.matmul(k.pb[6 + j // 4][q:q + 32, :], cT[:, c, j, :],
                                          qq[:, j % 2, m, :], start=m == 0, stop=m == 3,
                                          tile_position=(0, q), skip_group_check=True)
                mm.then_inc(out_done.sem, 1)

            for j in range(9):
                if j < 8:
                    inject(j)
                if j >= 1:
                    project(j - 1)

        @block.vector
        def _(dve):
            v = nc.vector
            link = Chain(dve, chain)
            for j in range(8):
                dve.wait_ge(bu.sem, bu.base + j + 1)
                r, i = k.pb[2 * (j % 2)][:, :], k.pb[2 * (j % 2) + 1][:, :]
                v.tensor_tensor(pr[:, 0, :], er[:, j, :], r, ALU.mult)
                v.tensor_tensor(pr[:, 1, :], ei[:, j, :], i, ALU.mult)
                v.tensor_tensor(pr[:, 2, :], er[:, j, :], i, ALU.mult)
                x = v.tensor_tensor(pr[:, 3, :], ei[:, j, :], r, ALU.mult)
                x.then_inc(outp.sem, 1)
                dve.wait_ge(outp.sem, outp.base + j + 1)
                v.tensor_tensor(vv[:, 0, :], pr[:, 0, :], pr[:, 1, :], ALU.add)
                link(v.tensor_tensor(vv[:, 1, :], pr[:, 2, :], pr[:, 3, :], ALU.subtract))
                if j >= 1:
                    dve.wait_ge(prod.sem, prod.base + j)
                m = mag[:, j:j + 1].to_broadcast([P, S])
                v.tensor_tensor_scan(yy[:, 0, :], m, vv[:, 0, :], 0.0, ALU.mult, ALU.add)
                v.tensor_tensor_scan(yy[:, 1, :], m, vv[:, 1, :], 0.0, ALU.mult, ALU.add).then_inc(scanned.sem, 1)
            dve.wait_ge(out_done.sem, out_done.base + 8)
            for f in range(2):
                v.scalar_tensor_tensor(out=yS[:, f, :], in0=uT[:, f, :], scalar=col(k, "s5_d", f),
                                       in1=k.pb[6 + f][:, :], op0=ALU.mult, op1=ALU.add)

        @block.gpsimd
        def _(pool):
            for j in range(8):
                pool.wait_ge(scanned.sem, scanned.base + j + 1)
                if j >= 2:
                    pool.wait_ge(out_done.sem, out_done.base + j - 1)
                nc.gpsimd.tensor_tensor(qq[:, j % 2, 0, :], yy[:, 0, :], er[:, j, :], ALU.mult)
                nc.gpsimd.tensor_tensor(qq[:, j % 2, 1, :], yy[:, 1, :], ei[:, j, :], ALU.mult)
                nc.gpsimd.tensor_tensor(qq[:, j % 2, 2, :], yy[:, 0, :], ei[:, j, :], ALU.mult)
                nc.gpsimd.tensor_tensor(qq[:, j % 2, 3, :], yy[:, 1, :], er[:, j, :], ALU.mult).then_inc(prod.sem, 1)
    for s in (bu, scanned, prod, out_done, outp):
        s.base += 8

    t1 = k.sb("s5_g1", 32, [P, 2, S])
    gT = k.sb("s5_gT", 36, [P, 2, S])
    gs = k.split("s5_g", 40, [P, 2, S], 44)
    sgd = k.sb("s5_sg", 168, [P, T, 256])
    hand = k.sig("s5_gelu")
    free = k.sig("s5_glu")
    turned = k.sig("s5_turned")
    k.freed[g] = (free.sem, free.base + T)
    with nc.Block() as block:
        @block.sync
        def _(sp):
            issue_chunks(k, sp, g + 1 + SLOTS)

        @block.vector
        def _(dve):
            v = nc.vector
            link = Chain(dve, chain)
            link(v.tensor_tensor(t1[:, :, :], yS[:, :, :], yS[:, :, :], ALU.mult))
            link(v.tensor_scalar(t1[:, :, :], t1[:, :, :], 0.044715, 1.0, ALU.mult, ALU.add))
            v.tensor_tensor(t1[:, :, :], t1[:, :, :], yS[:, :, :], ALU.mult).then_inc(hand.sem, 1)
            dve.wait_ge(hand.sem, hand.base + 2)
            v.tensor_tensor(gT[:, :, :], yS[:, :, :], t1[:, :, :], ALU.mult).then_inc(hand.sem, 1)
            dve.wait_ge(hand.sem, hand.base + 4)
            v.tensor_tensor(gs.lo[:, :, :], gT[:, :, :], plain(gs.hi[:, :, :]), ALU.subtract).then_inc(hand.sem, 1)
            dve.wait_ge(hand.sem, hand.base + 5 + T)
            dve.wait_ge(turned.sem, turned.base + T)
            for t in range(T):
                v.tensor_tensor(k.ycat[:, t, 0:256], sgd[:, t, :], k.pb[4 + t // 2][:, (t % 2) * 256:(t % 2) * 256 + 256],
                                ALU.mult)

        @block.scalar
        def _(act):
            act.wait_ge(hand.sem, hand.base + 1)
            nc.scalar.activation(t1[:, :, :], t1[:, :, :], ACT.Sigmoid,
                                 scale=2.0 * float(np.sqrt(2.0 / np.pi))).then_inc(hand.sem, 1)
            act.wait_ge(hand.sem, hand.base + 3)
            nc.scalar.copy(gs.hi[:, :, :], gT[:, :, :]).then_inc(hand.sem, 1)
            for t in range(T):
                act.wait_ge(hand.sem, hand.base + 5)
                act.wait_ge(free.sem, free.base + t + 1)
                nc.scalar.activation(sgd[:, t, :], k.pb[t][:, 0:256], ACT.Sigmoid).then_inc(hand.sem, 1)

        @block.tensor
        def _(pe):
            pe.wait_ge(hand.sem, hand.base + 5)
            wait_chunk(k, pe, g)
            for t in range(T):
                products(k, k.pb[t][:, 0:256], [(gs[:, f, t * P:(t + 1) * P], slot(k, g, f * 256, f * 256 + 256))
                                                for f in range(2)], True, True).then_inc(free.sem, 1)
            for t in range(T):
                for f in range(2):
                    c = (t % 2) * 256 + f * P
                    mm = nc.tensor.transpose(k.pb[4 + t // 2][:, c:c + P], gT[:, f, t * P:(t + 1) * P], k.ident[:, :])
                mm.then_inc(turned.sem, 1)
    hand.base += 5 + T
    free.base += T
    turned.base += T
    return g + 1


def stage_gate_rows(k):
    nc, d = k.nc, k.d
    grow = k.grow
    rows = k.rows = k.sb("rows", 180.5, [P, 5, S])
    e = k.sb("rows_e", 191, [P, 2, S])
    mn = k.sb("rows_mn", 195, [P, 2, S])
    zero = k.sb("rows_zero", 199, [P, S])
    k.acol = k.sb("acol", 172, [P, T, 4])
    k.mcol = k.sb("mcol", 172.25, [P, T, 4])
    s_in, hand = k.sig("rows_in"), k.sig("rows_hand")
    chain = k.sig("dve_chain")
    with nc.Block() as block:
        @block.sync
        def _(sp):
            sp.dma_start(k.sel[0:4, :, :], d["sel"]).then_inc(s_in.sem, 16)
            sp.wait_ge(s_in.sem, s_in.base + 16)

        @block.scalar
        def _(act):
            act.wait_ge(hand.sem, hand.base + 1)
            nc.scalar.activation(e[0:4, :, :], e[0:4, :, :], ACT.Exp).then_inc(hand.sem, 1)
            act.wait_ge(hand.sem, hand.base + 2)
            nc.scalar.activation(e[0:4, :, :], e[0:4, :, :], ACT.Ln, bias=1.0).then_inc(hand.sem, 1)

        @block.vector
        def _(dve):
            v = nc.vector
            link = Chain(dve, chain)
            z = grow[0:4, 0::2, :]
            en, m = e[0:4, :, :], mn[0:4, :, :]
            v.memset(zero[0:4, :], 0.0)
            v.tensor_scalar(m, z, 0.0, None, ALU.min)
            link(v.tensor_scalar(en, z, -1.0, None, ALU.mult))
            v.tensor_tensor(en, en, z, ALU.min).then_inc(hand.sem, 1)
            dve.wait_ge(hand.sem, hand.base + 3)
            link(v.tensor_tensor(m, m, en, ALU.subtract))
            R = [rows[0:4, i, :] for i in range(5)]
            zz = zero[0:4, :]
            v.tensor_tensor_scan(R[0], m[:, 0, :], zz, 0.0, ALU.add, ALU.add)
            link(v.tensor_tensor_scan(e[0:4, 0, :], m[:, 1, :], zz, 0.0, ALU.add, ALU.add))
            v.tensor_scalar(R[1], R[0], -1.0, None, ALU.mult)
            link(v.tensor_tensor(R[2], grow[0:4, 1, :], e[0:4, 0, :], ALU.subtract))
            link(v.tensor_tensor_scan(e[0:4, 1, :], R[2], zz, 0.0, ALU.max, ALU.max))
            v.tensor_scalar(R[3], e[0:4, 1, :], -1.0, None, ALU.mult)
            link(v.tensor_tensor(e[0:4, 1, :], e[0:4, 1, :], e[0:4, 0, :], ALU.add))
            v.tensor_scalar(R[4], e[0:4, 1, :], -1.0, None, ALU.mult).then_inc(hand.sem, 1)

        @block.tensor
        def _(pe):
            pe.wait_ge(hand.sem, hand.base + 4)
            for t in range(T):
                nc.tensor.transpose(k.pb[0][:, 4 * t:4 * t + 4], rows[0:4, 2, t * P:(t + 1) * P], k.ident[0:4, 0:4])
                mm = nc.tensor.transpose(k.pb[1][:, 4 * t:4 * t + 4], rows[0:4, 4, t * P:(t + 1) * P],
                                         k.ident[0:4, 0:4])
            mm.then_inc(hand.sem, 1)
    hand.base += 5
    s_in.base += 16
    with nc.Block() as block:
        @block.scalar
        def _(act):
            nc.scalar.activation(k.mcol[:, :, :].rearrange("p t h -> p (t h)"), k.pb[1][:, 0:16], ACT.Exp)

        @block.vector
        def _(dve):
            nc.vector.tensor_copy(k.acol[:, :, :].rearrange("p t h -> p (t h)"), k.pb[0][:, 0:16])


def stage_fox(k):
    batches = []
    for h in range(4):
        lo = DH * (h % 2)
        q, kk = k.fm[lo:lo + DH, 6 + h // 2, :], k.fm[lo:lo + DH, 8 + h // 2, :]
        for t in range(T):
            w = (t + 1) * P
            batches.append(dict(
                segs=[(0, w)],
                scores=[[(q[:, t * P:w], kk[:, 0:w], 0, w),
                         (k.rows[0:4, 0, t * P:w], k.sel[0:4, h, 0:w], 0, w),
                         (k.sel[0:4, h, 0:P], k.rows[0:4, 1, 0:w], 0, w),
                         (k.identb[:, :], k.mask_row[:, :], t * P, w)]],
                values=[[k.tm[:, 2, u, h * DH:(h + 1) * DH] for u in range(t + 1)]],
                out=k.ycat[:, t, 512 + h * DH:512 + (h + 1) * DH]))
    stage_attention(k, batches, 1.0, 158)


def stage_mlstm(k):
    nc = k.nc
    fm = k.fm
    cv = k.sb("conv", 32, [P, 4, S])
    cs = k.sb("convs", 40, [P, 4, S])
    v1 = k.sb("v_one", 158, [P, T, 4, DH + 1])
    hand = k.sig("conv_hand")
    chain = k.sig("dve_chain")
    with nc.Block() as block:
        @block.vector
        def _(dve):
            v = nc.vector
            link = Chain(dve, chain)
            v.tensor_copy(v1[:, :, :, 0:DH], k.tm[:, 3, :, :].rearrange("p t (h e) -> p t h e", h=4))
            v.memset(v1[:, :, :, DH:DH + 1], 1.0)
            for f in range(4):
                x = fm[:, 10 + f, :]
                link(v.tensor_scalar(cv[:, f, :], x, col(k, "conv_w", 4 * f + 3), None, ALU.mult))
                for i in (1, 2):
                    link(v.scalar_tensor_tensor(out=cv[:, f, i:], in0=x[:, 0:S - i],
                                                scalar=col(k, "conv_w", 4 * f + 3 - i), in1=cv[:, f, i:],
                                                op0=ALU.mult, op1=ALU.add))
                v.scalar_tensor_tensor(out=cv[:, f, 3:], in0=x[:, 0:S - 3], scalar=col(k, "conv_w", 4 * f),
                                       in1=cv[:, f, 3:], op0=ALU.mult, op1=ALU.add).then_inc(hand.sem, 1)
            for f in range(4):
                dve.wait_ge(hand.sem, hand.base + 5 + f)
                v.scalar_tensor_tensor(out=cv[:, f, :], in0=cs[:, f, :], scalar=1.0 if f < 2 else DH ** -0.5,
                                       in1=cv[:, f, :], op0=ALU.mult, op1=ALU.mult)

        @block.scalar
        def _(act):
            act.wait_ge(hand.sem, hand.base + 4)
            for f in range(4):
                nc.scalar.activation(cs[:, f, :], cv[:, f, :], ACT.Sigmoid).then_inc(hand.sem, 1)
    hand.base += 8

    decay = k.sb("ml_decay", 163, [P, 2, S])
    pT = k.sb("ml_pT", 190.5, [P, 2, T, S])
    nb = 16
    dm, qk, ex, pp, mixed, outd = (k.sig(x) for x in ("ml_logs", "ml_scores", "ml_decay", "ml_probs", "ml_mixed", "ml_out"))
    dn = k.sb("ml_den", 167.125, [P, 3, T])
    with nc.Block() as block:
        @block.tensor
        def _(pe):
            def scores(b):
                h, u = divmod(b, T)
                lo = DH * (h % 2)
                c0 = u * P
                if b >= 2:
                    pe.wait_ge(ex.sem, ex.base + b - 1)
                nc.tensor.matmul(k.pb[b % 2][:, c0:S], k.sel[0:4, h, 0:P], k.rows[0:4, 3, c0:S], start=True,
                                 stop=False, skip_group_check=True)
                nc.tensor.matmul(k.pb[b % 2][:, c0:c0 + P], k.identb[:, :], k.mask_col[:, :], start=False,
                                 stop=True, skip_group_check=True).then_inc(dm.sem, 1)
                if b >= 2:
                    pe.wait_ge(pp.sem, pp.base + b - 1)
                nc.tensor.matmul(k.pb[2 + b % 2][:, c0:S], cv[lo:lo + DH, 2 + h // 2, c0:c0 + P],
                                 cv[lo:lo + DH, h // 2, c0:S], start=True, stop=True).then_inc(qk.sem, 1)

            def mix(h):
                pe.wait_ge(pp.sem, pp.base + 4 * h + 4)
                if h >= 2:
                    pe.wait_ge(outd.sem, outd.base + h - 1)
                for t in range(T):
                    for u in range(t + 1):
                        mm = nc.tensor.matmul(k.pb[4 + h % 2][:, t * 65:t * 65 + 65], pT[:, h % 2, u, t * P:(t + 1) * P],
                                              v1[:, u, h, :], start=u == 0, stop=u == t, skip_group_check=True)
                mm.then_inc(mixed.sem, 1)

            for h in range(5):
                if h < 4:
                    for u in range(T):
                        scores(4 * h + u)
                if h >= 1:
                    mix(h - 1)

        @block.scalar
        def _(act):
            for b in range(nb):
                h, u = divmod(b, T)
                act.wait_ge(dm.sem, dm.base + b + 1)
                if b >= 2:
                    act.wait_ge(pp.sem, pp.base + b - 1)
                nc.scalar.activation(decay[:, b % 2, u * P:S], k.pb[b % 2][:, u * P:S], ACT.Exp,
                                     bias=k.acol[:, u, h:h + 1]).then_inc(ex.sem, 1)

        @block.vector
        def _(dve):
            v = nc.vector
            link = Chain(dve, chain)

            def finish(h):
                dve.wait_ge(mixed.sem, mixed.base + h + 1)
                o = k.pb[4 + h % 2][:, 0:260].rearrange("p (t e) -> p t e", e=65)
                den = o[:, :, 64]
                link(v.tensor_scalar(dn[:, 0, :], den, -1.0, None, ALU.mult))
                link(v.tensor_tensor(dn[:, 0, :], dn[:, 0, :], den, ALU.max))
                link(v.tensor_tensor(dn[:, 0, :], dn[:, 0, :], k.mcol[:, :, h], ALU.max))
                link(v.reciprocal(dn[:, 1, :], dn[:, 0, :]))
                v.tensor_tensor(k.ycat[:, :, 768 + h * DH:768 + (h + 1) * DH], o[:, :, 0:DH],
                                dn[:, 1, :].unsqueeze(2).to_broadcast([P, T, DH]), ALU.mult).then_inc(outd.sem, 1)

            for b in range(nb):
                h, u = divmod(b, T)
                dve.wait_ge(ex.sem, ex.base + b + 1)
                dve.wait_ge(qk.sem, qk.base + b + 1)
                if u == 0 and h >= 2:
                    dve.wait_ge(mixed.sem, mixed.base + h - 1)
                v.tensor_tensor(pT[:, h % 2, u, u * P:S], decay[:, b % 2, u * P:S], k.pb[2 + b % 2][:, u * P:S],
                                ALU.mult).then_inc(pp.sem, 1)
                if u == 3 and h >= 1:
                    finish(h - 1)
            finish(3)
    for s in (dm, qk, ex, pp):
        s.base += nb
    mixed.base += 4
    outd.base += 4


def stage_hgrn(k):
    nc = k.nc
    q, z = k.fm[:, 2:4, :], k.fm[:, 4:6, :]
    lf = k.sb("hg_lf", 32, [P, 2, S])
    b = k.sb("hg_b", 36, [P, 2, S])
    kk = k.sb("hg_k", 40, [P, 2, S])
    X = k.sb("hg_x", 158, [P, 2, 2, S])
    Z = k.sb("hg_z", 172.5, [P, 2, 2, S])
    acc = k.sb("hg_acc", 180.5, [P, 4, S])
    off = k.sb("hg_off", 188.5, [P, 4, 6, P])
    rst = k.sb("hg_reset", 44, [P, 2, S])
    lbt = k.sb("hg_lbt", 200.5, [P, 4, 2])
    hand = k.sig("hg_hand")
    chain = k.sig("dve_chain")
    chain_a = k.sig("act_chain")
    with nc.Block() as block:
        @block.scalar
        def _(act):
            link = Chain(act, chain_a)
            act.wait_ge(hand.sem, hand.base + 1)
            nc.scalar.activation(lbt[:, 0, :], lbt[:, 0, :], ACT.Exp)
            link(nc.scalar.activation(X[:, 0], X[:, 0], ACT.Exp))
            nc.scalar.activation(X[:, 0], X[:, 0], ACT.Ln, bias=1.0)
            nc.scalar.activation(X[:, 1], X[:, 1], ACT.Exp).then_inc(hand.sem, 1)
            act.wait_ge(hand.sem, hand.base + 3)
            nc.scalar.activation(X[:, 1], X[:, 1], ACT.Ln, bias=1.0)
            nc.scalar.activation(kk[:, :, :], z, ACT.Sigmoid, scale=-1.0).then_inc(hand.sem, 1)

        @block.vector
        def _(dve):
            v = nc.vector
            link = Chain(dve, chain)
            lb = col(k, "hg_lb", 0, 2)
            v.tensor_tensor(lbt[:, 0, :], lb, lb, ALU.subtract)
            v.tensor_scalar(X[:, 1], z, -1.0, 60.0, ALU.mult, ALU.min)
            v.tensor_scalar(lf[:, :, :], z, 0.0, None, ALU.min)
            link(v.tensor_scalar(X[:, 0], z, -1.0, None, ALU.mult))
            v.tensor_tensor(X[:, 0], X[:, 0], z, ALU.min).then_inc(hand.sem, 1)
            v.memset(acc[:, :, :], 0.0)
            v.memset(rst[:, :, :], 1.0)
            dve.wait_ge(hand.sem, hand.base + 2)
            link(v.reciprocal(lbt[:, 1, :], lbt[:, 0, :]))
            link(v.tensor_tensor(lbt[:, 1, :], lbt[:, 1, :], lbt[:, 0, :], ALU.mult))
            link(v.tensor_tensor(lbt[:, 2, :], lbt[:, 1, :], lbt[:, 1, :], ALU.subtract))
            link(v.tensor_scalar(lbt[:, 2, :], lbt[:, 2, :], 0.0, None, ALU.max))
            v.tensor_scalar(lbt[:, 3, :], lbt[:, 2, :], -1.0, 1.0, ALU.mult, ALU.add)
            link(v.tensor_tensor(lf[:, :, :], lf[:, :, :], X[:, 0], ALU.subtract))
            v.tensor_tensor(X[:, 1], X[:, 1], lbt[:, 2, :].unsqueeze(2).to_broadcast([P, 2, S]),
                            ALU.mult).then_inc(hand.sem, 1)
            dve.wait_ge(hand.sem, hand.base + 4)
            link(v.tensor_tensor(lf[:, :, :], lf[:, :, :], X[:, 1], ALU.add))
            v.tensor_tensor(kk[:, :, :], kk[:, :, :], lbt[:, 3, :].unsqueeze(2).to_broadcast([P, 2, S]), ALU.mult)
            link(v.memset(rst[:, :, 0::64], 0.0))
            v.tensor_tensor_scan(b[:, :, :].rearrange("p f s -> p (f s)"), rst[:, :, :].rearrange("p f s -> p (f s)"),
                                 lf[:, :, :].rearrange("p f s -> p (f s)"), 0.0, ALU.mult, ALU.add)
    hand.base += 4

    halves = [0, 1, 2, 4, 8, 16, 32, 64, 128, 256]
    made, ex, sc, sel = (k.sig(x) for x in ("hg_exponent", "hg_exp", "hg_scores", "hg_selected"))
    zr = k.sig("hg_z")
    nl = len(halves)
    with nc.Block() as block:
        @block.vector
        def _(dve):
            v = nc.vector
            link = Chain(dve, chain)

            def cut(t, n):
                return t.rearrange("p f (b c h) -> p (f b) c h", c=2, h=n)

            def exponents(i):
                n = halves[i]
                x = cut(X[:, i % 2], n)
                if i >= 3:
                    dve.wait_ge(zr.sem, zr.base + i - 2)
                if n <= 32:
                    bb = cut(b[:, :, :], n)
                    ref = bb[:, :, 0, n - 1:n].to_broadcast([P, S // n, n])
                    v.tensor_tensor(x[:, :, 1, :], bb[:, :, 1, :], ref, ALU.subtract)
                    v.tensor_tensor(x[:, :, 0, :], ref, bb[:, :, 0, :], ALU.subtract).then_inc(made.sem, 1)
                    return
                if n > 64:
                    link(v.memset(rst[:, :, n // 2::n], 1.0))
                    link(v.tensor_tensor_scan(
                        b[:, :, :].rearrange("p f s -> p (f s)"), rst[:, :, :].rearrange("p f s -> p (f s)"),
                        lf[:, :, :].rearrange("p f s -> p (f s)"), 0.0, ALU.mult, ALU.add))
                bb = cut(b[:, :, :], n)
                v.tensor_copy(x[:, :, 1, :], bb[:, :, 1, :])
                v.tensor_tensor(x[:, :, 0, :], bb[:, :, 0, n - 1:n].to_broadcast([P, S // n, n]), bb[:, :, 0, :],
                                ALU.subtract).then_inc(made.sem, 1)

            def operands(i):
                n = halves[i]
                dve.wait_ge(ex.sem, ex.base + i)
                if i >= 2:
                    dve.wait_ge(sc.sem, sc.base + 4 * (i - 1))
                x, zz = cut(X[:, i % 2], n), cut(Z[:, i % 2], n)
                v.tensor_tensor(zz[:, :, 1, :], x[:, :, 1, :], cut(q, n)[:, :, 1, :], ALU.mult)
                v.tensor_tensor(zz[:, :, 0, :], x[:, :, 0, :], cut(kk[:, :, :], n)[:, :, 0, :],
                                ALU.mult).then_inc(zr.sem, 1)

            def select(i, h):
                m = 4 * i + h
                dve.wait_ge(sc.sem, sc.base + m + 1)
                ps = k.pb[m % 4]
                n = halves[i]
                if n <= 64:
                    mask = k.mask_lev[:, i, :].bitcast(mybir.dt.uint16).unsqueeze(1).to_broadcast([P, T, P])
                    v.copy_predicated(acc[:, h, :].rearrange("p (t s) -> p t s", t=T), mask,
                                      ps[:, :].rearrange("p (t s) -> p t s", t=T)).then_inc(sel.sem, 1)
                elif n == 128:
                    v.tensor_copy(off[:, h, 0:2, :], ps[:, 0:256].rearrange("p (c s) -> p c s", c=2)).then_inc(sel.sem, 1)
                else:
                    v.tensor_copy(off[:, h, 2:6, :], ps[:, :].rearrange("p (c s) -> p c s", c=4)).then_inc(sel.sem, 1)

            exponents(1)
            exponents(2)
            for i in range(nl):
                if i + 1 < nl:
                    operands(i + 1)
                if 1 <= i < nl - 2:
                    exponents(i + 2)
                for h in range(4):
                    select(i, h)

        @block.scalar
        def _(act):
            for i in range(1, nl):
                act.wait_ge(made.sem, made.base + i)
                nc.scalar.activation(X[:, i % 2], X[:, i % 2], ACT.Exp).then_inc(ex.sem, 1)

        @block.tensor
        def _(pe):
            for i in range(nl):
                if i >= 1:
                    pe.wait_ge(zr.sem, zr.base + i)
                for h in range(4):
                    m = 4 * i + h
                    if m >= 4:
                        pe.wait_ge(sel.sem, sel.base + m - 3)
                    lo, f = DH * (h % 2), h // 2
                    L = kk[lo:lo + DH, f, :] if i == 0 else Z[lo:lo + DH, i % 2, f, :]
                    R = q[lo:lo + DH, f, :] if i == 0 else Z[lo:lo + DH, i % 2, f, :]
                    ps = k.pb[m % 4]
                    n = halves[i]
                    if n <= 64:
                        blocks = [(t * P, t * P, P, t * P) for t in range(T)]
                    elif n == 128:
                        blocks = [(0, 128, P, 0), (256, 384, P, 128)]
                    else:
                        blocks = [(0, 256, 256, 0), (128, 256, 256, 256)]
                    for s0, t0, w, c in blocks:
                        mm = nc.tensor.matmul(ps[:, c:c + w], L[:, s0:s0 + P], R[:, t0:t0 + w], start=True, stop=True,
                                              skip_group_check=True)
                    mm.then_inc(sc.sem, 1)
    for s, n in ((made, nl - 1), (ex, nl - 1), (zr, nl - 1), (sc, 4 * nl), (sel, 4 * nl)):
        s.base += n

    mixed, evd = k.sig("hg_mixed"), k.sig("hg_out")
    at = {(0, 1): 0, (2, 3): 1, (0, 2): 2, (0, 3): 3, (1, 2): 4, (1, 3): 5}
    with nc.Block() as block:
        @block.tensor
        def _(pe):
            for h in range(4):
                for t in range(T):
                    for u in range(t + 1):
                        a = acc[:, h, t * P:(t + 1) * P] if u == t else off[:, h, at[(u, t)], :]
                        mm = nc.tensor.matmul(k.pb[4 + h][:, t * DH:(t + 1) * DH], a, k.tm[:, 0, u, h * DH:(h + 1) * DH],
                                              start=u == 0, stop=u == t, skip_group_check=True)
                mm.then_inc(mixed.sem, 1)

        @block.vector
        def _(dve):
            for h in range(4):
                dve.wait_ge(mixed.sem, mixed.base + h + 1)
                nc.vector.tensor_copy(k.ycat[:, :, 256 + h * DH:256 + (h + 1) * DH],
                                      k.pb[4 + h][:, 0:256].rearrange("p (t e) -> p t e", t=T))
    mixed.base += 4


def stage_finish(k):
    nc = k.nc
    sq = k.sb("fin_sq", 32, [P, T * 16, DH])
    ss = k.sb("fin_ss", 158, [P, T, 16])
    rs = k.sb("fin_rs", 158.25, [P, T, 16])
    mh = k.sb("fin_half", 158.5, [P, T, 16])
    s4 = k.sb("fin_s4", 158.75, [P, T])
    sg = k.sb("fin_sg", 160, [P, 2, T, 256])
    hand, sgs = k.sig("fin_hand"), k.sig("fin_gates")
    chain = k.sig("dve_chain")
    yh = k.ycat[:, :, :].rearrange("p t (h e) -> p (t h) e", e=DH)
    with nc.Block() as block:
        @block.scalar
        def _(act):
            nc.scalar.activation(sg[:, 0], k.tm[:, 1], ACT.Sigmoid).then_inc(sgs.sem, 1)
            nc.scalar.activation(sg[:, 1], k.tm[:, 4], ACT.Sigmoid).then_inc(sgs.sem, 1)

        @block.gpsimd
        def _(pool):
            pool.wait_ge(hand.sem, hand.base + 1)
            nc.gpsimd.tensor_tensor(rs[:, :, :], ss[:, :, :], mh[:, :, :], ALU.pow).then_inc(hand.sem, 1)

        @block.vector
        def _(dve):
            v = nc.vector
            link = Chain(dve, chain)
            v.memset(mh[:, :, :], -0.5)
            link(v.tensor_tensor(sq[:, :, :], yh, yh, ALU.mult))
            link(v.tensor_reduce(ss[:, :, :].rearrange("p t h -> p (t h)"), sq[:, :, :], AX.X, ALU.add))
            link(v.tensor_reduce(s4[:, :], ss[:, :, 0:4], AX.X, ALU.add))
            link(v.tensor_scalar(ss[:, :, 0:4], s4[:, :].unsqueeze(2).to_broadcast([P, T, 4]), 0.25, None, ALU.mult))
            v.tensor_scalar(ss[:, :, :], ss[:, :, :], 1.0 / DH, EPS, ALU.mult, ALU.add).then_inc(hand.sem, 1)
            dve.wait_ge(hand.sem, hand.base + 2)
            link(v.tensor_tensor(yh, yh, rs[:, :, :].rearrange("p t h -> p (t h)").unsqueeze(2)
                                 .to_broadcast([P, T * 16, DH]), ALU.mult))
            dve.wait_ge(sgs.sem, sgs.base + 2)
            link(v.tensor_tensor(sg[:, 0], sg[:, 0], k.tm[:, 1], ALU.mult))
            v.tensor_tensor(k.ycat[:, :, 256:512], k.ycat[:, :, 256:512], sg[:, 0], ALU.mult)
            v.tensor_tensor(k.ycat[:, :, 768:1024], k.ycat[:, :, 768:1024], sg[:, 1], ALU.mult)
    hand.base += 2
    sgs.base += 2


def build(nc, d, out):
    with ExitStack() as ctx:
        k = allocate(nc, ctx, d)
        for name, first, n in CHUNKS:
            k.chunks += [d[name][i] for i in range(first, first + n)]
        stage_load(k)
        first_block(k)
        second_block(k, out)


def chunked(w, width, per):
    kk, n = w.shape
    return np.ascontiguousarray(w.reshape(kk // P // per, per, P, n // width, width)
                                .transpose(3, 0, 2, 1, 4).reshape(-1, P, per * width))


def columns(x):
    return np.ascontiguousarray(np.asarray(x).reshape(-1, P).T)


def constants():
    bf = mybir.dt.np(BF16)
    c = {"ident": np.eye(P, dtype=np.float32), "identb": np.eye(P).astype(bf)}
    q, kk = np.arange(P)[:, None], np.arange(3 * P)[None, :] - P
    c["mask_band"] = np.where(np.abs(q - kk) <= 64, 0.0, NEG).astype(bf)
    a, b = np.arange(P)[:, None], np.arange(P)[None, :]
    c["mask_d4"] = np.where(np.abs(a - b) <= 64, 0.0, NEG).astype(bf)
    c["mask_d16"] = np.where(a % 4 == b % 4, 0.0, NEG).astype(bf)
    c["mask_row"] = np.where(b <= a, 0.0, NEG).astype(bf)
    c["mask_col"] = np.where(a <= b, 0.0, NEG).astype(bf)
    lev = np.zeros((P, 8, P), np.float32)
    lev[:, 0, :] = a == b
    for i in range(7):
        hs = 1 << i
        lev[:, i + 1, :] = (a // (2 * hs) == b // (2 * hs)) & ((a // hs) % 2 == 0) & ((b // hs) % 2 == 1)
    c["mask_lev"] = lev.astype(bf)
    ra = np.zeros((P, 3, T, 16), np.float32)
    inv = np.float32(500000.0) ** (-(np.arange(8, dtype=np.float32) * 2.0 / 16))
    for g, r in enumerate(A_DIL):
        order = np.arange(S).reshape(T, P) if r == 1 else np.arange(S).reshape(P, T).T
        ang = order.T[:, :, None].astype(np.float32) * inv.astype(np.float32)
        ra[:, g, :, 0:8], ra[:, g, :, 8:16] = np.cos(ang), np.sin(ang)
    c["ropeA"] = ra
    c["sel"] = np.ascontiguousarray(np.broadcast_to(np.eye(4, dtype=np.float32)[:, :, None], (4, 4, S)))
    inv = (np.float32(10000.0) ** (-(np.arange(16, dtype=np.float32) * 2.0 / 32))).astype(np.float32)
    ang = np.arange(S).reshape(T, P).T[:, :, None].astype(np.float32) * inv
    c["ropeB"] = np.concatenate([np.cos(ang), np.sin(ang)], -1).astype(np.float32)
    return c


def layout(x):
    x = {n: np.asarray(a) for n, a in x.items()}
    a = {"x": x["x"].reshape(S, D)}
    w = x["w_in"]
    cols = []
    for g in range(3):
        cols += [w[:, 256 * g:256 * g + 256], w[:, 768 + 256 * g:1024 + 256 * g]]
    cols += [w[:, 1536:2304], w[:, 2816:3072], w[:, 2304:2816]]
    a["w_proj"] = chunked(np.concatenate(cols, 1), 512, 4)
    a["w_kpe"] = chunked(w[:, 3072:3104], 32, 8)
    a["w_gates"] = chunked(w[:, 3104:], 512, 4)
    a["w_uq"] = chunked(x["mla_w_uq"], 384, 4)
    a["w_ukv"] = chunked(x["mla_w_ukv"], 1024, 2)
    a["w_oa"] = chunked(x["w_o_a"], 1024, 2)
    a["w_ob"] = chunked(x["w_o_b"], 512, 4)
    a["w_out"] = chunked(x["w_out"], 512, 4)
    a["w_ff1"] = chunked(x["w_ff1"], 512, 4)
    half = FF1 // 2
    a["w_ff2"] = np.concatenate([chunked(x["w_ff2"][i:i + half], 512, 4) for i in (0, half)])
    z = np.zeros((P, 3), np.float32)
    gb = x["gate_bias_2"].reshape(3, 4)
    z[0:4, :] = gb.T
    lb = lambda n: columns(x[n][0])
    parts = {"mix_pre": columns(x["norm_mix_pre"]), "b_gate": columns(x["b_gate"]),
             "q_norm": columns(x["mla_q_norm"]), "kv_norm": columns(x["mla_kv_norm"]),
             "mlp_pre": columns(x["norm_mlp_pre"]), "mix_pre2": lb("ln_mix_pre_2"),
             "ffn_pre2": lb("ln_ffn_pre_2"), "mix_gain2": lb("mix_gain_2"),
             "hg_lb": lb("hgrn_lb_logits_2"),
             "conv_w": np.ascontiguousarray(x["mlstm_conv_w_2"][0].reshape(4, 4, P).transpose(2, 1, 0).reshape(P, 16)),
             "lam_re": columns(x["s5_lambda_re_2"][0].reshape(-1)), "lam_im": columns(x["s5_lambda_im_2"][0].reshape(-1)),
             "log_dt": columns(np.repeat(x["s5_log_dt_2"][0], 64)), "s5_d": lb("s5_d_2"), "gate_b": z}
    a["cols"] = np.concatenate([parts[n] for n in COLS], 1)
    for n, m in (("norm_mix_post", "norm_mix_post"), ("norm_mlp_post", "norm_mlp_post")):
        a[n] = x[m].reshape(D)
    a["ln_mix_post_2"], a["ln_ffn_post_2"] = x["ln_mix_post_2"][0], x["ln_ffn_post_2"][0]
    w = x["w_in_2"][0]
    at = dict(s5u=0, hgq=256, hgf=512, hgi=768, hgg=1024, foxq=1280, foxk=1536, foxv=1792, mlq=2052, mlk=2308,
              mlv=2564, mlo=2820)
    part = lambda *names: [w[:, at[n]:at[n] + 256] for n in names]
    a["w_fm"] = chunked(np.concatenate(part("s5u", "hgq", "hgf", "foxq", "foxk", "mlq"), 1), 512, 4)
    gates = np.zeros((D, 96), np.float32)
    for i, c in enumerate((2048, 3076, 3080)):
        gates[:, 32 * i:32 * i + 4] = w[:, c:c + 4]
    a["w_fg"] = chunked(np.concatenate(part("mlk") + [gates], 1), 352, 4)
    a["w_tm"] = chunked(np.concatenate(part("hgi", "hgg", "foxv", "mlv"), 1), 512, 4)
    a["w_tg"] = chunked(np.concatenate(part("mlo"), 1), 256, 8)
    a["w_glu"] = chunked(x["s5_w_glu_2"][0], 256, 2)
    a["w_out2"] = chunked(x["w_out_2"][0], 512, 4)
    f = FF2 // P
    up = np.concatenate([x["w_ffn_gate_2"][0].reshape(D, f, 1, P), x["w_ffn_up_2"][0].reshape(D, f, 1, P)], 2)
    a["w_up"] = chunked(up.reshape(D, 2 * FF2), 2 * P, KD)
    w = x["w_ffn_down_2"][0]
    a["w_dn_a"] = chunked(w[:12 * P], 512, 4)
    a["w_dn_b"] = chunked(w[12 * P:20 * P], 512, 4)
    a["w_dn_c"] = chunked(w[20 * P:], 512, 2)
    for n, m in (("s5_b_re", "s5_b_re_2"), ("s5_b_im", "s5_b_im_2")):
        z = np.zeros((8, 2, 64, 2, 16), np.float32)
        for i in range(2):
            z[:, i, :, i, :] = x[m][0].reshape(8, 2, 64, 16)[:, i]
        a[n] = np.ascontiguousarray(z.reshape(8, P, 32).transpose(1, 0, 2))
    z = np.zeros((2, 8, 2, 64, 2, 16), np.float32)
    for c, m in enumerate(("s5_c_re_2", "s5_c_im_2")):
        for i in range(2):
            z[c, :, i, :, i, :] = x[m][0].reshape(8, 2, 16, 64)[:, i].transpose(0, 2, 1)
    a["s5_cT"] = np.ascontiguousarray(z.reshape(2, 8, P, 32).transpose(2, 0, 1, 3))
    a.update(constants())
    return a


CHUNKS = [("w_proj", 0, 12), ("w_kpe", 0, 1), ("w_gates", 0, 8), ("w_uq", 0, 2), ("w_ukv", 0, 1), ("w_oa", 0, 1),
          ("w_ob", 0, 2), ("w_out", 0, 4), ("w_ff1", 0, 8), ("w_ff2", 0, 8), ("w_ff1", 8, 8), ("w_ff2", 8, 8),
          ("w_fm", 0, 6), ("w_fg", 0, 2), ("w_tm", 0, 4), ("w_tg", 0, 1), ("w_glu", 0, 1), ("w_out2", 0, 4),
          ("w_up", 0, 12), ("w_dn_a", 0, 6), ("w_up", 12, 10), ("w_dn_b", 0, 2), ("w_dn_c", 0, 1),
          ("w_dn_b", 2, 2), ("w_dn_c", 1, 1)]


def kernel(**inputs):
    import concourse.bacc as bacc
    from concourse.bass_utils import run_bass_kernel_spmd

    nc = bacc.Bacc("TRN2", target_bir_lowering=False, num_devices=1)
    arrays, d = {}, {}
    for name, a in layout(inputs).items():
        arrays[f"in_{name}"] = a
        d[name] = nc.dram_tensor(f"in_{name}", a.shape, mybir.dt.from_np(a.dtype), kind="ExternalInput").ap()
    d["scratch"] = nc.dram_tensor("scratch", (2, S, 260), F32, kind="Internal").ap()
    out = nc.dram_tensor("out_0_dram", (1, S, D), F32, kind="ExternalOutput").ap()
    build(nc, d, out)
    r = run_bass_kernel_spmd(nc, [arrays], core_ids=[0])
    return r.results[0]["out_0_dram"]
```

```python
from contextlib import ExitStack

import numpy as np

import concourse.bass as bass
from concourse import mybir

ALU = mybir.AluOpType
ACT = mybir.ActivationFunctionType
AX = mybir.AxisListType
F32 = mybir.dt.float32
BF16 = mybir.dt.bfloat16
F32R = mybir.dt.float32r

P = 128
S = 512
T = S // P
D = 1024
KD = D // P
EPS = 1e-6
KB = 1024
DH = 64
NEG = -1e30

A_HEADS = 4
A_DIL = (1, 4, 16)
B_HEADS = 8
B_QK = 96
FF1 = 4096
FF2 = 2816
FF2_PARTS = (12, 10)
SLOTS = 3
LEAD = 2
CHUNK = 2048
COLS = {}
_at = 0
for _name, _n in (("mix_pre", 8), ("b_gate", 16), ("q_norm", 4), ("kv_norm", 2), ("mlp_pre", 8),
                  ("mix_pre2", 8), ("ffn_pre2", 8), ("mix_gain2", 8), ("hg_lb", 2), ("conv_w", 16),
                  ("lam_re", 8), ("lam_im", 8), ("log_dt", 8), ("s5_d", 2), ("gate_b", 3)):
    COLS[_name] = (_at, _n)
    _at += _n
NCOLS = _at


class Signal:

    def __init__(self, sem):
        self.sem = sem
        self.base = 0


class Kernel:
    pass


class Split:

    def __init__(self, hi, lo):
        self.hi, self.lo = hi, lo

    def __getitem__(self, at):
        return Split(self.hi[at], self.lo[at])


def plain(x):
    return x.bitcast(F32)


def allocate(nc, ctx, d):
    k = Kernel()
    k.nc, k.d = nc, d

    def sb(name, kb, shape, dt=F32):
        return nc.alloc_sbuf_tensor_at(name, shape, dt, offset=int(kb * KB) + k.sb0)

    k.sb0 = (nc.sbuf_base + 63) // 64 * 64
    k.sb = sb
    k.split = lambda name, kb, shape, kb_lo: Split(sb(name + "_hi", kb, shape, F32R), sb(name + "_lo", kb_lo, shape, F32R))
    k.h = sb("h", 0, [P, T, D])
    k.xT = k.split("xT", 16, [P, KD, S], 32)
    k.raw = sb("ring_raw", 48, [P, SLOTS, CHUNK])
    k.ring = Split(sb("ring_hi", 72, [P, SLOTS, CHUNK], F32R), sb("ring_lo", 48, [P, SLOTS, CHUNK], F32R))
    k.ident = sb("ident", 96, [P, P])
    k.identb = sb("identb", 96.5, [P, P], BF16)
    k.mask_band = sb("mask_band", 96.75, [P, 3 * P], BF16)
    k.mask_d4 = sb("mask_d4", 97.5, [P, P], BF16)
    k.mask_d16 = sb("mask_d16", 97.75, [P, P], BF16)
    k.mask_row = sb("mask_row", 98, [P, P], BF16)
    k.mask_col = sb("mask_col", 98.25, [P, P], BF16)
    k.mask_lev = sb("mask_lev", 98.5, [P, 8, P], BF16)
    k.ropeA = sb("ropeA", 100.5, [P, 3, T, 16])
    k.ropeB = sb("ropeB", 101.25, [P, T, 32])
    k.cols = sb("cols", 101.75, [P, NCOLS])
    k.stat = sb("stat", 102.5, [P, 64])
    k.s5_small = sb("s5_small", 102.75, [P, 22, 8])
    k.pb = [ctx.enter_context(nc.psum_tensor(f"bank{i}", [P, 512], F32)) for i in range(8)]
    k.sems = {}

    def sig(name):
        if name not in k.sems:
            k.sems[name] = Signal(ctx.enter_context(nc.semaphore(name)))
        return k.sems[name]

    k.sig = sig
    k.w_landed = [sig(f"w_landed{i}") for i in range(SLOTS)]
    k.w_hi, k.w_split = sig("w_hi"), sig("w_split")
    k.hi_next = k.lo_next = 0
    k.w_used = sig("w_used")
    k.freed = {}
    k.c_in = sig("consts_in")
    k.x_in = [sig(f"x_in{t}") for t in range(T)]
    k.chunks = []
    k.att_n = 0
    k.issued = 0
    return k


def col(k, name, i=0, n=1):
    a, _ = COLS[name]
    return k.cols[:, a + i:a + i + n]


def issue_chunks(k, eng, upto):
    upto = min(upto, len(k.chunks))
    for g in range(k.issued, upto):
        src = k.chunks[g]
        if g >= SLOTS:
            sem, count = k.freed[g - SLOTS]
            eng.wait_ge(sem, count)
        eng.dma_start(k.raw[:, g % SLOTS, 0:src.shape[1]], src).then_inc(k.w_landed[g % SLOTS].sem, 16)
    k.issued = max(k.issued, upto)


def split_hi(k, act, upto):
    upto = min(upto, len(k.chunks))
    for g in range(k.hi_next, upto):
        n = k.chunks[g].shape[1]
        act.wait_ge(k.w_landed[g % SLOTS].sem, 16 * (g // SLOTS + 1))
        if g >= SLOTS:
            sem, count = k.freed[g - SLOTS]
            act.wait_ge(sem, count)
        k.nc.scalar.copy(k.ring.hi[:, g % SLOTS, 0:n], k.raw[:, g % SLOTS, 0:n]).then_inc(k.w_hi.sem, 1)
    k.hi_next = max(k.hi_next, upto)


def split_lo(k, dve, upto):
    upto = min(upto, len(k.chunks))
    for g in range(k.lo_next, upto):
        n = k.chunks[g].shape[1]
        dve.wait_ge(k.w_hi.sem, g + 1)
        k.nc.vector.tensor_tensor(k.ring.lo[:, g % SLOTS, 0:n], k.raw[:, g % SLOTS, 0:n],
                                  plain(k.ring.hi[:, g % SLOTS, 0:n]), ALU.subtract).then_inc(k.w_split.sem, 1)
    k.lo_next = max(k.lo_next, upto)


def wait_chunk(k, pe, g):
    pe.wait_ge(k.w_split.sem, g + 1)


def slot(k, g, a, b):
    return k.ring[:, g % SLOTS, a:b]


def products(k, out, pairs, first, last):
    n = 0
    for a, b in pairs:
        for x, y in ((a.hi, b.hi), (a.hi, b.lo), (a.lo, b.hi)):
            mm = k.nc.tensor.matmul(out, x, y, start=first and n == 0, stop=last and n == 3 * len(pairs) - 1)
            n += 1
    return mm


def note_freed(k, steps, done):
    final = {s[0]: i for i, s in enumerate(steps)}
    marks = set()
    for g, i in final.items():
        if steps[i][5]:
            k.freed[g] = (done.sem, done.base + sum(s[5] for s in steps[:i + 1]))
        else:
            k.w_used.base += 1
            k.freed[g] = (k.w_used.sem, k.w_used.base)
            marks.add(i)
    return marks


class Chain:

    def __init__(self, eng, signal):
        self.eng, self.s = eng, signal

    def __call__(self, ins):
        self.s.base += 1
        ins.then_inc(self.s.sem, 1)
        self.eng.wait_ge(self.s.sem, self.s.base)


def stage_load(k):
    nc, d = k.nc, k.d
    poles_act, poles_dve = s5_poles(k)
    cols_in = k.sig("cols_in")
    with nc.Block() as block:
        @block.sync
        def _(sp):
            for t in range(T):
                sp.dma_start(k.h[:, t, :], d["x"][t * P:(t + 1) * P, :]).then_inc(k.x_in[t].sem, 16)
            issue_chunks(k, sp, SLOTS)

        @block.scalar
        def _(act):
            act.dma_start(k.cols[:, :], d["cols"]).then_inc(cols_in.sem, 16)
            for dst, name in ((k.ident[:, :], "ident"),
                              (k.identb[:, :], "identb"), (k.mask_band[:, :], "mask_band"),
                              (k.mask_d4[:, :], "mask_d4"), (k.mask_d16[:, :], "mask_d16"),
                              (k.mask_row[:, :], "mask_row"), (k.mask_col[:, :], "mask_col"),
                              (k.mask_lev[:, :, :], "mask_lev"), (k.ropeA[:, :, :, :], "ropeA"),
                              (k.ropeB[:, :, :], "ropeB")):
                act.dma_start(dst, d[name]).then_inc(k.c_in.sem, 16)
            act.wait_ge(cols_in.sem, 16)
            poles_act(act)

        @block.vector
        def _(dve):
            dve.wait_ge(cols_in.sem, 16)
            poles_dve(dve)


def stage_norm_T(k, tag, src, width, gain, dst, xn_kb, arrive=None, sync=None):
    nc = k.nc
    kt = width // P
    sq, root, scaled, turned, ev_act, ev_dve = (
        k.sig(n) for n in ("norm_sumsq", "norm_root", "norm_scaled", "norm_turned", "norm_evac_act", "norm_evac_dve"))
    ms, rs, half = k.stat[:, 0:T], k.stat[:, T:2 * T], k.stat[:, 2 * T:3 * T]
    xn = k.sb(f"xn_{tag}", xn_kb, [P, T, width])
    with nc.Block() as block:
        @block.sync
        def _(sp):
            if sync is not None:
                sync(sp)

        @block.scalar
        def _(act):
            for t in range(T):
                if arrive is not None:
                    act.wait_ge(arrive[t].sem, 16)
                nc.scalar.activation(xn[:, t, :], src[:, t, :], ACT.Square,
                                     accum_out=k.stat[:, t:t + 1]).then_inc(sq.sem, 1)
            for f in range(kt):
                act.wait_ge(turned.sem, turned.base + f + 1)
                nc.scalar.mul(dst.hi[:, f, :], k.pb[f % 4][:, :], col(k, gain, f)).then_inc(ev_act.sem, 1)

        @block.gpsimd
        def _(pool):
            pool.wait_ge(root.sem, root.base + 1)
            nc.gpsimd.tensor_tensor(rs, ms, half, ALU.pow).then_inc(root.sem, 1)

        @block.vector
        def _(dve):
            nc.vector.memset(half, -0.5).then_inc(sq.sem, 1)
            dve.wait_ge(sq.sem, sq.base + T + 1)
            nc.vector.tensor_scalar(ms, ms, 1.0 / width, EPS, ALU.mult, ALU.add).then_inc(root.sem, 1)
            dve.wait_ge(root.sem, root.base + 2)
            for t in range(T):
                nc.vector.tensor_scalar(xn[:, t, :], src[:, t, :], rs[:, t:t + 1], None,
                                        ALU.mult).then_inc(scaled.sem, 1)
            for f in range(kt):
                dve.wait_ge(ev_act.sem, ev_act.base + f + 1)
                nc.vector.scalar_tensor_tensor(out=dst.lo[:, f, :], in0=k.pb[f % 4][:, :], scalar=col(k, gain, f),
                                               in1=plain(dst.hi[:, f, :]), op0=ALU.mult,
                                               op1=ALU.subtract).then_inc(ev_dve.sem, 1)

        @block.tensor
        def _(pe):
            for f in range(kt):
                if f >= 4:
                    pe.wait_ge(ev_dve.sem, ev_dve.base + f - 3)
                for t in range(T):
                    if f == 0 and t == 0 and arrive is not None:
                        pe.wait_ge(k.c_in.sem, 16 * 10)
                    if f == 0:
                        pe.wait_ge(scaled.sem, scaled.base + t + 1)
                    last = nc.tensor.transpose(k.pb[f % 4][:, t * P:(t + 1) * P],
                                               xn[:, t, f * P:(f + 1) * P], k.ident[:, :])
                last.then_inc(turned.sem, 1)
    sq.base += T + 1
    root.base += 2
    scaled.base += T
    turned.base += kt
    ev_act.base += kt
    ev_dve.base += kt


def schedule(k, steps):
    chunks, fin = [], {}
    for g, j, _, _, _, last in steps:
        if not chunks or chunks[-1] != g:
            chunks.append(g)
        if last:
            fin[j] = g
    return chunks, fin


def stage_gemm(k, steps, evac, owner=None, act_each=None, dve_each=None, dve_tail=None, pool=None,
               needs=()):
    nc = k.nc
    done, free_act, free_dve = (k.sig(n) for n in ("gemm_done", "gemm_free_act", "gemm_free_dve"))
    n = 1 + max(s[1] for s in steps)
    owner = owner or (lambda j: ("act", "dve")[j % 2])
    outs = {s[1]: s[2] for s in steps}
    chunks, fin = schedule(k, steps)
    end = chunks[-1] + 1
    marks = note_freed(k, steps, done)
    counts, release, a, v = {}, {}, free_act.base, free_dve.base
    for j in range(n):
        if owner(j) in ("act", "both"):
            a += 1
        if owner(j) in ("dve", "both"):
            v += 1
        counts[j] = (a, v)
        release[j] = (free_act.sem, a) if owner(j) == "act" else (free_dve.sem, v)
    with nc.Block() as block:
        @block.sync
        def _(sp):
            issue_chunks(k, sp, end + SLOTS)

        @block.tensor
        def _(pe):
            seen = set()
            for i, (g, j, out, pairs, first, last) in enumerate(steps):
                if g not in seen:
                    seen.add(g)
                    wait_chunk(k, pe, g)
                    if g in needs:
                        sem, count = needs[g] if isinstance(needs[g], tuple) else release[needs[g]]
                        pe.wait_ge(sem, count)
                if first and j >= 8:
                    sem, count = release[j - 8]
                    pe.wait_ge(sem, count)
                mm = products(k, out, pairs, first, last)
                if last:
                    mm.then_inc(done.sem, 1)
                elif i in marks:
                    mm.then_inc(k.w_used.sem, 1)

        @block.scalar
        def _(act):
            split_hi(k, act, chunks[0] + LEAD)
            for j in range(n):
                split_hi(k, act, fin[j] + LEAD)
                if act_each is not None:
                    act_each(act, j)
                if owner(j) in ("act", "both"):
                    act.wait_ge(done.sem, done.base + j + 1)
                    evac("act", act, j, outs[j]).then_inc(free_act.sem, 1)
            if act_each is not None:
                act_each(act, n)
            split_hi(k, act, end + LEAD)

        @block.vector
        def _(dve):
            split_lo(k, dve, chunks[0] + LEAD)
            for j in range(n):
                if dve_each is not None:
                    dve_each(dve, j)
                split_lo(k, dve, fin[j] + LEAD)
                if owner(j) == "both":
                    dve.wait_ge(free_act.sem, counts[j][0])
                elif owner(j) == "dve":
                    dve.wait_ge(done.sem, done.base + j + 1)
                if owner(j) != "act":
                    evac("dve", dve, j, outs[j]).then_inc(free_dve.sem, 1)
            if dve_tail is not None:
                dve_tail(dve)
            split_lo(k, dve, end + LEAD)

        @block.gpsimd
        def _(eng):
            if pool is not None:
                pool(eng)
    done.base += n
    free_act.base, free_dve.base = a, v


def copy_out(k, who, dst, src):
    return k.nc.scalar.copy(dst, src) if who == "act" else k.nc.vector.tensor_copy(dst, src)


def tokens(k, perm, kt, t):
    if perm == 0:
        return k.xT[:, kt, t * P:(t + 1) * P]
    return k.xT[:, kt, t::T]


class Beside:

    def __init__(self, k, steps, evac, rounds):
        self.k, self.steps, self.evac, self.rounds = k, steps, evac, rounds
        self.done, self.free = k.sig("beside_done"), k.sig("beside_free")
        note_freed(k, steps, self.done)
        self.first, self.end = steps[0][0], steps[-1][0] + 1
        self.units = [(i, u) for i in range(len(steps)) for u in range(2)]

    def span(self, r, n):
        return range(n * r // self.rounds, n * (r + 1) // self.rounds)

    def tiles(self, r):
        return [self.units[u][0] for u in self.span(r, len(self.units)) if self.units[u][1] == 1]

    def sync(self, sp):
        issue_chunks(self.k, sp, self.end + SLOTS)

    def pe(self, pe, r):
        for u in self.span(r, len(self.units)):
            i, half = self.units[u]
            g, j, out, pairs, _, _ = self.steps[i]
            wait_chunk(self.k, pe, g)
            if half == 0 and j >= 2:
                pe.wait_ge(self.free.sem, self.free.base + j - 1)
            n = len(pairs) // 2
            mm = products(self.k, out, pairs[half * n:half * n + n], half == 0, half == 1)
            if half:
                mm.then_inc(self.done.sem, 1)

    def upto(self, tiles):
        return self.steps[tiles[-1]][0] + LEAD if tiles else self.first + LEAD

    def act(self, act, r):
        if r == 0:
            split_hi(self.k, act, self.first + LEAD)
            return
        for i in self.tiles(r - 1):
            _, j, out, _, _, _ = self.steps[i]
            act.wait_ge(self.done.sem, self.done.base + j + 1)
            self.evac(act, j, out).then_inc(self.free.sem, 1)
            if i % 2:
                split_hi(self.k, act, min(self.steps[i][0] + 1 + LEAD, self.end + LEAD))

    def dve(self, dve, r):
        if r == 0:
            split_lo(self.k, dve, self.first + LEAD)
            return
        for i in self.tiles(r - 1):
            if i % 2:
                split_lo(self.k, dve, min(self.steps[i][0] + 1 + LEAD, self.end + LEAD))

    def close(self):
        self.done.base += len(self.steps)
        self.free.base += len(self.steps)


def stage_attention(k, batches, scale, bufs_kb, lse=None, beside=None):
    nc = k.nc
    nb = len(batches)
    scored, negmax, expd, turned, ev_act, ev_dve, mixed, out_free = (
        k.sig(n) for n in ("att_scored", "att_negmax", "att_exp", "att_turned", "att_ptT_act", "att_ptT_dve",
                           "att_mixed", "att_out"))
    k.att_n += 1
    probs = k.sb(f"probs{k.att_n}", bufs_kb, [P, 2, 512])
    probsT = k.sb(f"probsT{k.att_n}", bufs_kb + 4, [P, 2, 512])
    ns = max(len(b["segs"]) for b in batches)
    mx = k.sb(f"mx{k.att_n}", bufs_kb + 8, [P, nb, ns])
    nm = k.sb(f"nm{k.att_n}", bufs_kb + 8.5, [P, nb, ns])
    ls = k.sb(f"ls{k.att_n}", bufs_kb + 9, [P, nb, ns])
    li = k.sb(f"li{k.att_n}", bufs_kb + 9.5, [P, nb, ns])
    chain = k.sig("dve_chain")
    chain_act = k.sig("act_chain")

    def width(b):
        return b["segs"][-1][1]

    with nc.Block() as block:
        @block.sync
        def _(sp):
            if beside is not None:
                beside.sync(sp)

        @block.tensor
        def _(pe):
            def scores(i):
                b = batches[i]
                if i >= 2:
                    pe.wait_ge(expd.sem, expd.base + i - 1)
                for (c0, c1), parts in zip(b["segs"], b["scores"]):
                    for m, (a, r, lo, hi, *row) in enumerate(parts):
                        at = dict(tile_position=(row[0], 0)) if row else {}
                        mm = nc.tensor.matmul(k.pb[i % 2][:, lo:hi], a, r, start=m == 0,
                                              stop=m == len(parts) - 1, skip_group_check=True, **at)
                mm.then_inc(scored.sem, 1)

            def turn(i):
                b = batches[i]
                pe.wait_ge(expd.sem, expd.base + i + 1)
                if i >= 2:
                    ev = (ev_act, ev_dve)[i % 2]
                    pe.wait_ge(ev.sem, ev.base + i // 2)
                for c in range(0, width(b), P):
                    mm = nc.tensor.transpose(k.pb[2 + i % 2][:, c:c + P], probs[:, i % 2, c:c + P], k.ident[:, :])
                mm.then_inc(turned.sem, 1)

            def mix(i):
                b = batches[i]
                ev = (ev_act, ev_dve)[i % 2]
                pe.wait_ge(ev.sem, ev.base + i // 2 + 1)
                if i >= 2:
                    pe.wait_ge(out_free.sem, out_free.base + i - 1)
                for n, ((c0, c1), vs) in enumerate(zip(b["segs"], b["values"])):
                    for m, v in enumerate(vs):
                        mm = nc.tensor.matmul(k.pb[4 + i % 2][:, n * DH:(n + 1) * DH],
                                              probsT[:, i % 2, c0 + m * P:c0 + (m + 1) * P], v,
                                              start=m == 0, stop=m == len(vs) - 1, skip_group_check=True)
                mm.then_inc(mixed.sem, 1)

            for i in range(nb + 2):
                if i < nb:
                    scores(i)
                    if beside is not None:
                        beside.pe(pe, i)
                if 1 <= i <= nb:
                    turn(i - 1)
                if i >= 2:
                    mix(i - 2)

        def evac(who, eng, i):
            w = width(batches[i])
            eng.wait_ge(turned.sem, turned.base + i + 1)
            if i >= 2:
                eng.wait_ge(mixed.sem, mixed.base + i - 1)
            copy_out(k, who, probsT[:, i % 2, 0:w], k.pb[2 + i % 2][:, 0:w]).then_inc(
                (ev_act if who == "act" else ev_dve).sem, 1)

        @block.scalar
        def _(act):
            for i in range(nb + 1):
                if i < nb:
                    b = batches[i]
                    act.wait_ge(negmax.sem, negmax.base + i + 1)
                    if i >= 2:
                        act.wait_ge(turned.sem, turned.base + i - 1)
                    for n, (c0, c1) in enumerate(b["segs"]):
                        e = nc.scalar.activation(probs[:, i % 2, c0:c1], k.pb[i % 2][:, c0:c1], ACT.Exp,
                                                 bias=nm[:, i, n:n + 1], scale=scale,
                                                 accum_out=ls[:, i, n:n + 1])
                    e.then_inc(expd.sem, 1)
                if i >= 1 and (i - 1) % 2 == 0:
                    evac("act", act, i - 1)
                if beside is not None:
                    beside.act(act, i)
            if lse is not None:
                act.wait_ge(expd.sem, expd.base + nb)
                nc.scalar.activation(mx[:, :, :], ls[:, :, :], ACT.Ln).then_inc(chain_act.sem, 1)

        @block.vector
        def _(dve):
            link = Chain(dve, chain)
            if lse is not None:
                link(nc.vector.memset(ls[:, :, :], 1.0))
            for i in range(nb + 2):
                if i < nb:
                    b = batches[i]
                    m = len(b["segs"])
                    dve.wait_ge(scored.sem, scored.base + i + 1)
                    w = width(b)
                    link(nc.vector.tensor_reduce(
                        mx[:, i, 0:m], k.pb[i % 2][:, 0:w].rearrange("p (m w) -> p m w", m=m), AX.X, ALU.max))
                    nc.vector.tensor_scalar(nm[:, i, 0:m], mx[:, i, 0:m], -scale, None,
                                            ALU.mult).then_inc(negmax.sem, 1)
                if 1 <= i <= nb and (i - 1) % 2 == 1:
                    evac("dve", dve, i - 1)
                if beside is not None and i <= nb:
                    beside.dve(dve, i)
                if i >= 2:
                    j = i - 2
                    b = batches[j]
                    m = len(b["segs"])
                    dve.wait_ge(expd.sem, expd.base + j + 1)
                    link(nc.vector.reciprocal(li[:, j, 0:m], ls[:, j, 0:m]))
                    dve.wait_ge(mixed.sem, mixed.base + j + 1)
                    if m == 1:
                        nc.vector.tensor_scalar(b["out"], k.pb[4 + j % 2][:, 0:DH], li[:, j, 0:1], None,
                                                ALU.mult).then_inc(out_free.sem, 1)
                    else:
                        nc.vector.tensor_tensor(
                            b["out"], k.pb[4 + j % 2][:, 0:m * DH].rearrange("p (m e) -> p m e", m=m),
                            li[:, j, 0:m].unsqueeze(2).to_broadcast([P, m, DH]), ALU.mult).then_inc(out_free.sem, 1)
            if lse is not None:
                dve.wait_ge(chain_act.sem, chain_act.base + 1)
                for dst, i, n in lse:
                    nc.vector.tensor_tensor(dst, mx[:, i, 0:n], nm[:, i, 0:n], ALU.subtract)
                chain_act.base += 1
    for s in (scored, negmax, expd, turned, mixed, out_free):
        s.base += nb
    ev_act.base += (nb + 1) // 2
    ev_dve.base += nb // 2
    if beside is not None:
        beside.close()


def stage_turn(k, items, before=None):
    nc = k.nc
    n = len(items)
    turned, ev_act, ev_dve, fed = (k.sig(x) for x in ("turn_done", "turn_evac_act", "turn_evac_dve", "turn_fed"))
    release, a, v = [], ev_act.base, ev_dve.base
    for j, it in enumerate(items):
        both = isinstance(it[2], Split)
        a += both or j % 2 == 0
        v += both or j % 2 == 1
        release.append((ev_dve.sem, v) if both or j % 2 else (ev_act.sem, a))
    a0 = ev_act.base
    with nc.Block() as block:
        @block.vector
        def _(dve):
            if before is not None:
                before(dve).then_inc(fed.sem, 1)
            for j, (_, m, dst, gain) in enumerate(items):
                src = k.pb[j % 4][0:m, :]
                if isinstance(dst, Split):
                    dve.wait_ge(ev_act.sem, a0 + j + 1)
                    nc.vector.scalar_tensor_tensor(out=dst.lo, in0=src, scalar=1.0 if gain is None else gain,
                                                   in1=plain(dst.hi), op0=ALU.mult,
                                                   op1=ALU.subtract).then_inc(ev_dve.sem, 1)
                elif j % 2:
                    dve.wait_ge(turned.sem, turned.base + j + 1)
                    nc.vector.tensor_copy(dst, src).then_inc(ev_dve.sem, 1)

        @block.scalar
        def _(act):
            for j, (_, m, dst, gain) in enumerate(items):
                src = k.pb[j % 4][0:m, :]
                if isinstance(dst, Split):
                    act.wait_ge(turned.sem, turned.base + j + 1)
                    nc.scalar.mul(dst.hi, src, 1.0 if gain is None else gain).then_inc(ev_act.sem, 1)
                elif j % 2 == 0:
                    act.wait_ge(turned.sem, turned.base + j + 1)
                    nc.scalar.copy(dst, src).then_inc(ev_act.sem, 1)

        @block.tensor
        def _(pe):
            if before is not None:
                pe.wait_ge(fed.sem, fed.base + 1)
            for j, (srcs, m, dst, gain) in enumerate(items):
                if j >= 4:
                    sem, count = release[j - 4]
                    pe.wait_ge(sem, count)
                for t, s in enumerate(srcs):
                    last = nc.tensor.transpose(k.pb[j % 4][0:m, t * P:(t + 1) * P], s, k.ident[:, :])
                last.then_inc(turned.sem, 1)
    turned.base += n
    ev_act.base, ev_dve.base = a, v
    fed.base += before is not None


def rotate(k, dve, x1, x2, cos, sin, tmp):
    v, s = k.nc.vector, k.sig("dve_chain")
    link = Chain(dve, s)
    for dst, a, b in ((tmp[0], x1, cos), (tmp[1], x2, sin), (tmp[2], x2, cos)):
        v.tensor_tensor(dst, a, b, ALU.mult)
    link(v.tensor_tensor(tmp[3], x1, sin, ALU.mult))
    v.tensor_tensor(x1, tmp[0], tmp[1], ALU.subtract)
    return v.tensor_tensor(x2, tmp[2], tmp[3], ALU.add)


def stage_residual(k, tag, y, gain_name, tmp_kb, xn_kb, norm_gain=None, out=None):
    nc, d = k.nc, k.d
    sq, made, root, g_in, scaled, added, xs, turned, high = (
        k.sig("res_" + x) for x in ("sumsq", "mean", "root", "gain", "scaled", "added", "xn", "turned", "high"))
    stored = k.sig("stored")
    gain = k.sb(f"resgain_{tag}", tmp_kb, [P, D])
    tmp = k.sb(f"restmp_{tag}", tmp_kb + 4, [P, 2, D])
    xn = k.sb(f"resxn_{tag}", xn_kb, [P, T, D])
    ms, rs, half = k.stat[:, 0:2 * T], k.stat[:, 2 * T:4 * T], k.stat[:, 4 * T:4 * T + 1]
    norm = norm_gain is not None
    order = [0, 1] + ([2, 3, T, T + 1, T + 2, T + 3] if norm else [2, 3])
    nth = {c: i + 1 for i, c in enumerate(order)}
    with nc.Block() as block:
        @block.sync
        def _(sp):
            sp.dma_start(gain[:, :], d[gain_name].rearrange("(a n) -> a n", a=1).to_broadcast([P, D])).then_inc(g_in.sem, 16)
            if out is not None:
                for t in range(T):
                    sp.wait_ge(added.sem, added.base + t + 1)
                    sp.dma_start(out[t * P:(t + 1) * P, :], k.h[:, t, :]).then_inc(stored.sem, 16)
                sp.wait_ge(stored.sem, 16 * T)

        @block.scalar
        def _(act):
            def square(src, t, c):
                nc.scalar.activation(xn[:, t, :], src[:, t, :], ACT.Square, accum_out=ms[:, c:c + 1]).then_inc(sq.sem, 1)

            for t in range(T):
                square(y, t, t)
            for t in range(T + 1 if norm else 0):
                if t < T:
                    act.wait_ge(added.sem, added.base + t + 1)
                    square(k.h, t, T + t)
                if t >= 1:
                    act.wait_ge(root.sem, root.base + nth[T + t - 1])
                    nc.scalar.mul(xn[:, t - 1, :], k.h[:, t - 1, :], rs[:, T + t - 1:T + t]).then_inc(xs.sem, 1)
            for f in range(KD if norm else 0):
                act.wait_ge(turned.sem, turned.base + f + 1)
                nc.scalar.mul(k.xT.hi[:, f, :], k.pb[f][:, :], col(k, norm_gain, f)).then_inc(high.sem, 1)

        @block.gpsimd
        def _(pool):
            for c in order:
                pool.wait_ge(made.sem, made.base + nth[c])
                nc.gpsimd.tensor_tensor(rs[:, c:c + 1], ms[:, c:c + 1], half, ALU.pow).then_inc(root.sem, 1)

        @block.vector
        def _(dve):
            link = Chain(dve, k.sig("dve_chain"))

            def mean(c):
                dve.wait_ge(sq.sem, sq.base + c + 1)
                nc.vector.tensor_scalar(ms[:, c:c + 1], ms[:, c:c + 1], 1.0 / D, EPS, ALU.mult,
                                        ALU.add).then_inc(made.sem, 1)

            link(nc.vector.memset(half, -0.5))
            mean(0)
            mean(1)
            dve.wait_ge(g_in.sem, g_in.base + 16)
            for t in range(T):
                dve.wait_ge(root.sem, root.base + nth[t])
                nc.vector.scalar_tensor_tensor(out=tmp[:, t % 2, :], in0=y[:, t, :], scalar=rs[:, t:t + 1],
                                               in1=gain[:, :], op0=ALU.mult, op1=ALU.mult).then_inc(scaled.sem, 1)
                dve.wait_ge(scaled.sem, scaled.base + t + 1)
                nc.vector.tensor_tensor(k.h[:, t, :], k.h[:, t, :], tmp[:, t % 2, :], ALU.add).then_inc(added.sem, 1)
                if t < 2:
                    mean(t + 2)
                elif norm:
                    mean(T + t - 2)
            for c in (T + 2, T + 3) if norm else ():
                mean(c)
            for f in range(KD if norm else 0):
                dve.wait_ge(high.sem, high.base + f + 1)
                nc.vector.scalar_tensor_tensor(out=k.xT.lo[:, f, :], in0=k.pb[f][:, :], scalar=col(k, norm_gain, f),
                                               in1=plain(k.xT.hi[:, f, :]), op0=ALU.mult, op1=ALU.subtract)

        @block.tensor
        def _(pe):
            for t in range(T if norm else 0):
                pe.wait_ge(xs.sem, xs.base + t + 1)
                for f in range(KD):
                    mm = nc.tensor.transpose(k.pb[f][:, t * P:(t + 1) * P], xn[:, t, f * P:(f + 1) * P], k.ident[:, :])
                    if t == T - 1:
                        mm.then_inc(turned.sem, 1)
    for s, n in ((sq, T), (made, T), (root, T), (g_in, 16), (scaled, T), (added, T)):
        s.base += n
    if norm:
        for s, n in ((sq, T), (made, T), (root, T), (xs, T), (turned, KD), (high, KD)):
            s.base += n


def gemm(k, g, kt, per, tiles, j, banks=range(8)):
    steps = []
    for k0 in range(0, kt, per):
        k1 = min(k0 + per, kt)
        for n, (m, cols, lhs, rhs, (c0, width, row)) in enumerate(tiles):
            pairs = []
            for f in range(k0, k1):
                w = slot(k, g, (f - k0) * row + c0, (f - k0) * row + c0 + width)
                pairs.append((lhs(f) if lhs else w, rhs(f) if rhs else w))
            steps.append((g, j + n, k.pb[banks[(j + n) % len(banks)]][0:m, 0:cols], pairs, k0 == 0, k1 == kt))
        g += 1
    return steps, j + len(tiles), g


def token_tiles(lhs, cols, row):
    return [(P, n, lambda f, t=t, perm=perm: lhs(perm, f, t), None, (c0, n, row)) for c0, n, perm in cols for t in range(T)]


def feature_tiles(rhs, cols, row, m=P):
    return [(m, S, None, lambda f: rhs[:, f, :], (c0, m, row)) for c0 in cols]


def first_block(k):
    nc = k.nc
    g = 0
    stage_norm_T(k, "x", k.h, D, "mix_pre", k.xT, 104, k.x_in)

    qk = k.sb("qkA", 104, [P, 3, T, 512])
    v = k.sb("vA", 128, [P, 3, T, 256])
    kvc = k.sb("kvc", 140, [P, T, 256])
    qc = k.sb("qc", 144, [P, T, 512])
    kpe = k.sb("kpe", 152, [P, T, 32])
    gates = k.sb("gates", 152.5, [P, 16, S])
    steps, dst, j = [], [], 0
    plan = [([(0, 512, 0)], [qk[:, 0]]), ([(0, 512, 1)], [qk[:, 1]]), ([(0, 512, 2)], [qk[:, 2]]),
            ([(0, 256, 0), (256, 256, 1)], [v[:, 0], v[:, 1]]), ([(0, 256, 2), (256, 256, 0)], [v[:, 2], kvc]),
            ([(0, 512, 0)], [qc])]
    lhs = lambda perm, f, t: tokens(k, perm, f, t)
    for cols, dsts in plan:
        s, j, g = gemm(k, g, KD, 4, token_tiles(lhs, cols, 512), j)
        steps += s
        for x in dsts:
            dst += [x[:, t, :] for t in range(T)]
    s, j, g = gemm(k, g, KD, 8, token_tiles(lhs, [(0, 32, 0)], 32), j)
    steps += s
    dst += [kpe[:, t, :] for t in range(T)]
    stage_gemm(k, steps, lambda who, eng, j, ps: copy_out(k, who, dst[j], ps))

    tmp = k.sb("ropetmp", 185, [P, 4, 3 * T, 8, 8])
    qh = qk[:, :, :, :].rearrange("p g t (h e) -> p (g t) h e", h=8)
    tab = k.ropeA[:, :, :, :].rearrange("p g t c -> p (g t) c")
    cos = tab[:, :, 0:8].unsqueeze(2).to_broadcast([P, 3 * T, 8, 8])
    sin = tab[:, :, 8:16].unsqueeze(2).to_broadcast([P, 3 * T, 8, 8])
    qkT = lambda grp, f, lo: qk[lo:lo + DH, grp, :, f * P:(f + 1) * P]
    items = [([qk[:, g_, t, f * P:(f + 1) * P] for t in range(T)], P, qk[:, g_, :, f * P:(f + 1) * P], None)
             for g_ in range(3) for f in range(4)]

    def rope_a(dve):
        return rotate(k, dve, qh[:, :, :, 0:8], qh[:, :, :, 8:16], cos, sin, [tmp[:, i] for i in range(4)])

    stage_turn(k, items, rope_a)
    oA = k.sb("oA", 195, [P, 3, T, 260])
    batches, lse = [], []
    for grp in range(3):
        for h in range(A_HEADS):
            lo = DH * (h % 2)
            q, kk = qkT(grp, h // 2, lo), qkT(grp, 2 + h // 2, lo)
            if grp:
                mask = (k.mask_d4, k.mask_d16)[grp - 1]
                batches.append(dict(
                    segs=[(t * P, (t + 1) * P) for t in range(T)],
                    scores=[[(q[:, t, :], kk[:, t, :], t * P, (t + 1) * P),
                             (k.identb[:, :], mask[:, :], t * P, (t + 1) * P)] for t in range(T)],
                    values=[[v[:, grp, t, h * DH:(h + 1) * DH]] for t in range(T)],
                    out=oA[:, grp, :, h * DH:(h + 1) * DH]))
                lse.append((oA[:, grp, :, 256 + h], len(batches) - 1, T))
            else:
                for t in range(T):
                    a, b = max(t - 1, 0), min(t + 2, T)
                    w = (b - a) * P
                    m0 = (a - t + 1) * P
                    batches.append(dict(
                        segs=[(0, w)],
                        scores=[[(q[:, t, :], kk[:, a:b, :], 0, w),
                                 (k.identb[:, :], k.mask_band[:, m0:m0 + w], 0, w)]],
                        values=[[v[:, grp, u, h * DH:(h + 1) * DH] for u in range(a, b)]],
                        out=oA[:, grp, t, h * DH:(h + 1) * DH]))
                    lse.append((oA[:, grp, t, 256 + h:257 + h], len(batches) - 1, 1))
    steps, j = [], 0
    for _ in range(8):
        s, j, g = gemm(k, g, KD, 8, feature_tiles(k.xT, (0, P), 2 * P), j, banks=(6, 7))
        steps += s

    def evac_gates(act, j, ps):
        return nc.scalar.activation(gates[:, j, :], ps, ACT.Identity, bias=col(k, "b_gate", j))

    stage_attention(k, batches, DH ** -0.5, 185, lse, Beside(k, steps, evac_gates, len(batches)))

    qcT = k.split("qcT", 16, [P, 4, S], 24)
    kvcT = k.split("kvcT", 32, [P, 2, S], 36)
    stage_norm_T(k, "qc", qc, 512, "q_norm", qcT, 104, sync=reorder(k, oA))
    stage_norm_T(k, "kvc", kvc, 256, "kv_norm", kvcT, 104)
    qB = k.sb("qB", 104, [P, T, 8, 96])
    kB = k.sb("kB", 130, [P, T, 8, 96])
    vB = k.sb("vB", 142, [P, T, 8, DH])
    steps, dst, j = [], [], 0
    for _ in range(2):
        s, j, g = gemm(k, g, 4, 4, token_tiles(lambda perm, f, t: qcT[:, f, t * P:(t + 1) * P], [(0, 384, 0)], 384), j)
        steps += s
    s, j, g = gemm(k, g, 2, 2, token_tiles(lambda perm, f, t: kvcT[:, f, t * P:(t + 1) * P],
                                           [(0, 512, 0), (512, 512, 0)], 1024), j)
    steps += s

    def evac_b(who, eng, j, ps):
        t, half = j % 4, (j // 4) % 2
        if j < 8:
            return copy_out(k, who, qB[:, t, half * 4:half * 4 + 4, :].rearrange("p h e -> p (h e)"), ps)
        kv = ps.rearrange("p (h e) -> p h e", h=4)
        copy_out(k, who, kB[:, t, half * 4:half * 4 + 4, 0:DH], kv[:, :, 0:DH])
        return copy_out(k, who, vB[:, t, half * 4:half * 4 + 4, :], kv[:, :, DH:])

    stage_gemm(k, steps, evac_b)

    mixAT = k.split("mixAT", 122, [P, 2, S], 126)
    oc = stage_combine(k, oA)
    stage_turn(k, [([oc[:, t, f * P:(f + 1) * P] for t in range(T)], P, mixAT[:, f, :], None) for f in range(2)])

    tmpq = k.sb("ropetmpq", 195, [P, 4, T, 8, 16])
    tmpk = k.sb("ropetmpk", 203, [P, 4, T, 16])
    qTb = k.sb("qTb", 16, [P, 8, S])
    kTb = k.sb("kTb", 32, [P, 8, S])

    def rope_b(dve):
        link = Chain(dve, k.sig("dve_chain"))
        cos, sin = k.ropeB[:, :, 0:16], k.ropeB[:, :, 16:32]
        rotate(k, dve, qB[:, :, :, 64:80], qB[:, :, :, 80:96], cos.unsqueeze(2).to_broadcast([P, T, 8, 16]),
               sin.unsqueeze(2).to_broadcast([P, T, 8, 16]), [tmpq[:, i] for i in range(4)])
        link(rotate(k, dve, kpe[:, :, 0:16], kpe[:, :, 16:32], cos, sin, [tmpk[:, i] for i in range(4)]))
        return nc.vector.tensor_copy(kB[:, :, :, DH:96], kpe[:, :, :].unsqueeze(2).to_broadcast([P, T, 8, 32]))

    items = []
    for h in range(B_HEADS):
        items.append(([qB[:, t, h, :] for t in range(T)], 96, qTb[0:96, h, :], None))
        items.append(([kB[:, t, h, :] for t in range(T)], 96, kTb[0:96, h, :], None))
    stage_turn(k, items, rope_b)
    oB = k.sb("oB", 104, [P, T, 512])
    batches = []
    for t in range(T):
        for h in range(B_HEADS):
            batches.append(dict(
                segs=[(0, S)], scores=[[(qTb[0:96, h, t * P:(t + 1) * P], kTb[0:96, h, :], 0, S)]],
                values=[[vB[:, u, h, :] for u in range(T)]], out=oB[:, t, h * DH:(h + 1) * DH]))
    stage_attention(k, batches, B_QK ** -0.5, 185)
    oBT = k.split("oBT", 130, [P, 4, S], 138)
    stage_turn(k, [([oB[:, t, f * P:(f + 1) * P] for t in range(T)], P, oBT[:, f, :], None) for f in range(4)])

    mixT = k.split("mixT", 16, [P, KD, S], 32)
    ga, gb = k.sb("gated_a", 185, [P, KD, S]), k.sb("gated_b", 104, [P, 2, S])
    steps, j = [], 0
    s, j, g = gemm(k, g, 2, 2, feature_tiles(mixAT, range(0, D, P), D), j)
    steps += s
    for _ in range(2):
        s, j, g = gemm(k, g, 4, 4, feature_tiles(oBT, range(0, 512, P), 512), j)
        steps += s
    gate_made = k.sig("gate_made")
    free, summed, high = k.sig("gemm_free_dve"), k.sig("gated_sum"), k.sig("gated_high")

    def low(dve, f):
        dve.wait_ge(high.sem, high.base + f + 1)
        return nc.vector.tensor_tensor(mixT.lo[:, f, :], ga[:, f, :], plain(mixT.hi[:, f, :]), ALU.subtract)

    def gated(who, eng, j, ps):
        eng.wait_ge(gate_made.sem, gate_made.base + j + 1)
        if j < KD:
            return nc.vector.tensor_tensor(ga[:, j, :], gates[:, j, :], ps, ALU.mult)
        f = j - KD
        if f >= 2:
            low(eng, f - 2)
        return nc.vector.tensor_tensor(gb[:, f % 2, :], gates[:, j, :], ps, ALU.mult)

    def add(pool):
        for f in range(KD):
            pool.wait_ge(free.sem, free.base + KD + f + 1)
            nc.gpsimd.tensor_tensor(ga[:, f, :], ga[:, f, :], gb[:, f % 2, :], ALU.add).then_inc(summed.sem, 1)

    def split_sum(act, j):
        if j < 2 * KD:
            nc.scalar.activation(gates[:, j, :], gates[:, j, :], ACT.Sigmoid).then_inc(gate_made.sem, 1)
        for f in (j - KD - 2,) if j < 2 * KD else (KD - 2, KD - 1):
            if f >= 0:
                act.wait_ge(summed.sem, summed.base + f + 1)
                nc.scalar.copy(mixT.hi[:, f, :], ga[:, f, :]).then_inc(high.sem, 1)

    def last_low(dve):
        low(dve, KD - 2)
        low(dve, KD - 1)

    stage_gemm(k, steps, gated, lambda j: "dve", act_each=split_sum, dve_tail=last_low, pool=add)
    gate_made.base += 2 * KD
    summed.base += KD
    high.base += KD
    y = k.sb("y1", 104, [P, T, D])
    g = stage_out_product(k, g, mixT, y)
    stage_residual(k, "mix1", y, "norm_mix_post", 130, 142, "mlp_pre")

    H = FF1 // P // 2
    hid = k.split("hid1", 104, [P, H, S], 136)
    y = k.sb("y2", 168, [P, T, D])
    r, r2 = k.sb("relu", 185, [P, 2, S]), k.sb("relu2", 189, [P, 2, S])
    steps, j, needs, tile = [], 0, {}, []
    for half in range(2):
        f0 = j
        for _ in range(H // 4):
            s, j, g = gemm(k, g, KD, 4, feature_tiles(k.xT, range(0, 512, P), 512), j)
            steps += s
        tile += [("up", half, f) for f in range(H)]
        for c in range(2):
            first_chunk = g
            s, j, g = gemm(k, g, H, 4, token_tiles(lambda perm, f, t: hid[:, f, t * P:(t + 1) * P], [(0, 512, 0)], 512), j)
            steps += s
            needs.update({first_chunk + i: f0 + 4 * i + 3 for i in range(H // 4)})
            tile += [("down", half, y[:, t, c * 512:(c + 1) * 512]) for t in range(T)]
    ra, rr = k.sig("relu_done"), k.sig("relu_read")

    def evac_ff(who, eng, j, ps):
        kind, half, f = tile[j]
        if kind == "down":
            return nc.vector.tensor_tensor(f, f, ps, ALU.add) if half else nc.vector.tensor_copy(f, ps)
        n = half * H + f
        if who == "act":
            if n >= 2:
                eng.wait_ge(rr.sem, rr.base + n - 1)
            nc.scalar.activation(r[:, n % 2, :], ps, ACT.Relu).then_inc(ra.sem, 1)
            eng.wait_ge(ra.sem, ra.base + n + 1)
            return nc.scalar.activation(hid.hi[:, f, :], r[:, n % 2, :], ACT.Square)
        nc.vector.tensor_tensor(r2[:, n % 2, :], r[:, n % 2, :], r[:, n % 2, :], ALU.mult).then_inc(rr.sem, 1)
        eng.wait_ge(rr.sem, rr.base + n + 1)
        return nc.vector.tensor_tensor(hid.lo[:, f, :], r2[:, n % 2, :], plain(hid.hi[:, f, :]), ALU.subtract)

    stage_gemm(k, steps, evac_ff, lambda j: "both" if tile[j][0] == "up" else "dve", needs=needs)
    stage_residual(k, "mlp1", y, "norm_mlp_post", 185, 104, "mix_pre2")
    k.g = g
    return None


def stage_out_product(k, g, lhs, y):
    steps, j = [], 0
    for _ in range(2):
        s, j, g = gemm(k, g, KD, 4, token_tiles(lambda perm, f, t: lhs[:, f, t * P:(t + 1) * P], [(0, 512, 0)], 512), j)
        steps += s
    stage_gemm(k, steps, lambda who, eng, j, ps: copy_out(k, who, y[:, j % T, (j // T) * 512:(j // T) * 512 + 512], ps))
    return g


W_OA = 260


def reorder(k, oA):
    d, sent, back = k.d, k.sig("combine_sent"), k.sig("combine_back")
    nat = k.natA = k.sb("natA", 116, [P, 2, T, W_OA])

    def sync(sp):
        for t in range(T):
            for i in range(2):
                sp.dma_start(d["scratch"][i, t::T, :], oA[:, 1 + i, t, :]).then_inc(sent.sem, 16)
        sp.wait_ge(sent.sem, 16 * 2 * T)
        for i in range(2):
            sp.dma_start(nat[:, i, :, :], d["scratch"][i].rearrange("(t p) n -> p t n", p=P)).then_inc(back.sem, 16)

    return sync


def stage_combine(k, oA):
    nc = k.nc
    back, done = k.sig("combine_back"), k.sig("combine_done")
    nat = k.natA
    oc = k.sb("oc", 185, [P, T, 256])
    t2 = k.sb("combtmp", 189, [P, T, 256])
    w3 = k.sb("w3", 193, [P, 3, T, 4])
    mxw = k.sb("mxw", 193.25, [P, T, 4])
    sumw = k.sb("sumw", 193.5, [P, T, 4])
    with nc.Block() as block:
        @block.vector
        def _(dve):
            link = Chain(dve, k.sig("dve_chain"))
            v = nc.vector
            dve.wait_ge(back.sem, 32)
            src = [oA[:, 0, :, :], nat[:, 0, :, :], nat[:, 1, :, :]]
            ls = [s[:, :, 256:260] for s in src]
            link(v.tensor_tensor(mxw[:, :, :], ls[0], ls[1], ALU.max))
            link(v.tensor_tensor(mxw[:, :, :], mxw[:, :, :], ls[2], ALU.max))
            for i in range(3):
                v.tensor_tensor(w3[:, i], ls[i], mxw[:, :, :], ALU.subtract).then_inc(done.sem, 1)
            dve.wait_ge(done.sem, 4)
            link(v.tensor_tensor(sumw[:, :, :], w3[:, 0], w3[:, 1], ALU.add))
            link(v.tensor_tensor(sumw[:, :, :], sumw[:, :, :], w3[:, 2], ALU.add))
            link(v.reciprocal(sumw[:, :, :], sumw[:, :, :]))
            link(v.tensor_tensor(w3[:, :, :, :], w3[:, :, :, :],
                                 sumw[:, :, :].unsqueeze(1).to_broadcast([P, 3, T, 4]), ALU.mult))
            for i in range(3):
                dst = (oc if i == 0 else t2)[:, :, :].rearrange("p t (h e) -> p (t h) e", h=4)
                link(v.tensor_tensor(
                    dst.rearrange("p (t h) e -> p t h e", t=T), src[i][:, :, 0:256].rearrange("p t (h e) -> p t h e", h=4),
                    w3[:, i].unsqueeze(3).to_broadcast([P, T, 4, DH]), ALU.mult))
                if i:
                    link(v.tensor_tensor(oc[:, :, :], oc[:, :, :], t2[:, :, :], ALU.add))

        @block.scalar
        def _(act):
            act.wait_ge(done.sem, 3)
            nc.scalar.activation(w3[:, :, :, :], w3[:, :, :, :], ACT.Exp).then_inc(done.sem, 1)
    return oc


def second_block(k, out):
    nc, g = k.nc, k.g
    bT, cT = stage_s5_inputs(k)

    fm = k.sb("fm", 104, [P, 14, S])
    grow = k.sb("grow", 132, [P, 3, S])
    tm = k.sb("tm", 138, [P, 5, T, 256])
    steps, j = [], 0
    for c in range(3):
        s, j, g = gemm(k, g, KD, 4, feature_tiles(k.xT, range(0, 512, P), 512), j)
        steps += s
    s, j, g = gemm(k, g, KD, 4, feature_tiles(k.xT, (0, P), 352) + feature_tiles(k.xT, (2 * P,), 352, m=96), j)
    steps += s
    j_tm = j
    lhs = lambda perm, f, t: k.xT[:, f, t * P:(t + 1) * P]
    for c in range(2):
        s, j, g = gemm(k, g, KD, 4, token_tiles(lhs, [(0, 256, 0), (256, 256, 0)], 512), j)
        steps += s
    s, j, g = gemm(k, g, KD, 8, token_tiles(lhs, [(0, 256, 0)], 256), j)
    steps += s
    FOX_Q = 6

    def evac(who, eng, j, ps):
        if j < 14:
            if FOX_Q <= j < FOX_Q + 2:
                return (nc.scalar.mul(fm[:, j, :], ps, DH ** -0.5) if who == "act" else
                        nc.vector.tensor_scalar(fm[:, j, :], ps, DH ** -0.5, None, ALU.mult))
            return copy_out(k, who, fm[:, j, :], ps)
        if j == 14:
            for i in range(3):
                x = nc.scalar.activation(grow[0:4, i, :], ps[32 * i:32 * i + 4, :], ACT.Identity,
                                         bias=col(k, "gate_b", i)[0:4, :])
            return x
        i = j - j_tm
        return copy_out(k, who, tm[:, i // T, i % T, :], ps)

    er, ei = k.sb("s5_er", 174, [P, 8, S]), k.sb("s5_ei", 190, [P, 8, S])
    stage_gemm(k, steps, evac, pool=s5_powers(k, er, ei, 164))
    k.fm, k.grow, k.tm = fm, grow, tm
    k.ycat = k.sb("ycat", 16, [P, T, D])
    yS = stage_s5(k, er, ei, bT, cT)
    stage_gate_rows(k)
    g = stage_s5_gelu(k, yS, g)
    stage_fox(k)
    hg = HgrnGates(k)
    stage_mlstm(k, hg)
    stage_hgrn(k, hg)
    ycT = k.split("ycT", 104, [P, KD, S], 120)
    stage_turn(k, [([k.ycat[:, t, f * P:(f + 1) * P] for t in range(T)], P, ycT[:, f, :], col(k, "mix_gain2", f))
                   for f in range(KD)])
    y = k.sb("y3", 136, [P, T, D])
    g = stage_out_product(k, g, ycT, y)
    stage_residual(k, "mix2", y, "ln_mix_post_2", 152, 104, "ffn_pre2")

    hid = k.split("hid2", 104, [P, FF2_PARTS[0], S], 128)
    y = k.sb("y4", 152, [P, T, D])
    sg, full = k.sb("glu_sg", 168, [P, 2, S]), k.sb("glu_full", 172, [P, 2, S])
    taken, high, low = k.sig("gemm_free_dve"), k.sig("glu_high"), k.sig("glu_low")
    steps, j, needs, tile, n = [], 0, {}, [], 0
    for part, tiles in enumerate(FF2_PARTS):
        for f in range(tiles):
            s, j, g = gemm(k, g, KD, 8, feature_tiles(k.xT, (0, P), 2 * P), j)
            steps += s
            tile += [("gate", n + f, f), ("up", n + f, f)]
        for c in range(2):
            first_chunk = g
            s, j, g = gemm(k, g, tiles, 4, token_tiles(lambda perm, f, t: hid[:, f, t * P:(t + 1) * P], [(0, 512, 0)], 512), j)
            steps += s
            needs.update({first_chunk + i: (low.sem, low.base + n + min(4 * i + 4, tiles))
                          for i in range(g - first_chunk)})
            tile += [("down", part, y[:, t, c * 512:(c + 1) * 512]) for t in range(T)]
        n += tiles
    b_taken = taken.base

    def evac_glu(who, eng, j, ps):
        kind, n, f = tile[j]
        if kind == "down":
            return nc.vector.tensor_tensor(f, f, ps, ALU.add) if n else nc.vector.tensor_copy(f, ps)
        x = full[:, n % 2, :]
        if who == "act":
            if n >= 2:
                eng.wait_ge(low.sem, low.base + n - 1)
            return nc.scalar.activation(sg[:, n % 2, :], ps, ACT.Sigmoid)
        if kind == "gate":
            if n >= 2:
                eng.wait_ge(low.sem, low.base + n - 1)
            return nc.vector.tensor_tensor(x, sg[:, n % 2, :], ps, ALU.mult)
        eng.wait_ge(taken.sem, b_taken + j)
        return nc.vector.tensor_tensor(x, x, ps, ALU.mult)

    def high_part(act, j):
        if j < len(tile) and tile[j][0] == "up":
            act.wait_ge(taken.sem, b_taken + j + 1)
            nc.scalar.copy(hid.hi[:, tile[j][2], :], full[:, tile[j][1] % 2, :]).then_inc(high.sem, 1)

    def low_part(dve, j):
        if j and tile[j - 1][0] == "up":
            _, n, f = tile[j - 1]
            dve.wait_ge(high.sem, high.base + n + 1)
            dve.wait_ge(taken.sem, b_taken + j)
            nc.vector.tensor_tensor(hid.lo[:, f, :], full[:, n % 2, :], plain(hid.hi[:, f, :]),
                                    ALU.subtract).then_inc(low.sem, 1)

    stage_gemm(k, steps, evac_glu, lambda j: "both" if tile[j][0] == "gate" else "dve", act_each=high_part,
               dve_each=low_part, needs=needs)
    stage_residual(k, "mlp2", y, "ln_ffn_post_2", 176, 104, out=out[0])
    return None


def s5_poles(k):
    nc = k.nc
    v, a = nc.vector, nc.scalar
    (DT, LR, MAG, TH, N1, RE, SN, AB, CS, AR, AI, DEN, A1, T1, T2, CR, CI) = [k.s5_small[:, i, :] for i in range(17)]
    hand = k.sig("s5_hand")
    PI = float(np.pi)

    def by_act(act):
        a.activation(DT, col(k, "log_dt", 0, 8), ACT.Exp).then_inc(hand.sem, 1)
        act.wait_ge(hand.sem, 2)
        a.activation(MAG, MAG, ACT.Exp).then_inc(hand.sem, 1)
        a.activation(SN, RE, ACT.Sin).then_inc(hand.sem, 1)
        a.activation(CS, AB, ACT.Sin).then_inc(hand.sem, 1)

    def by_dve(dve):
        link = Chain(dve, k.sig("dve_chain"))
        tt, ts = v.tensor_tensor, v.tensor_scalar
        link(ts(LR, col(k, "lam_re", 0, 8), -1e-4, None, ALU.min))
        dve.wait_ge(hand.sem, 1)
        tt(MAG, LR, DT, ALU.mult)
        link(tt(TH, col(k, "lam_im", 0, 8), DT, ALU.mult))
        link(ts(N1, TH, 1.0 / (2 * PI), 12582912.0, ALU.mult, ALU.add))
        link(ts(N1, N1, 12582912.0, None, ALU.subtract))
        link(v.scalar_tensor_tensor(out=RE, in0=N1, scalar=-6.28125, in1=TH, op0=ALU.mult, op1=ALU.add))
        c2 = float(np.float32(np.round((2 * np.pi - 6.28125) * 2 ** 22) / 2 ** 22))
        link(v.scalar_tensor_tensor(out=RE, in0=N1, scalar=-c2, in1=RE, op0=ALU.mult, op1=ALU.add))
        link(v.scalar_tensor_tensor(out=RE, in0=N1, scalar=-float(2 * np.pi - 6.28125 - c2), in1=RE,
                                    op0=ALU.mult, op1=ALU.add))
        link(ts(RE, RE, 3.1415925, -3.1415925, ALU.min, ALU.max))
        link(ts(AB, RE, -1.0, None, ALU.mult))
        link(tt(AB, AB, RE, ALU.max))
        ts(AB, AB, -1.0, PI / 2, ALU.mult, ALU.add).then_inc(hand.sem, 1)
        dve.wait_ge(hand.sem, 5)
        tt(AR, MAG, CS, ALU.mult)
        link(tt(AI, MAG, SN, ALU.mult))
        li = col(k, "lam_im", 0, 8)
        tt(T1, LR, LR, ALU.mult)
        link(tt(T2, li, li, ALU.mult))
        link(tt(DEN, T1, T2, ALU.add))
        link(v.reciprocal(DEN, DEN))
        link(ts(A1, AR, -1.0, None, ALU.add))
        tt(T1, A1, LR, ALU.mult)
        link(tt(T2, AI, li, ALU.mult))
        link(tt(CR, T1, T2, ALU.add))
        tt(CR, CR, DEN, ALU.mult)
        tt(T1, AI, LR, ALU.mult)
        link(tt(T2, A1, li, ALU.mult))
        link(tt(CI, T1, T2, ALU.subtract))
        tt(CI, CI, DEN, ALU.mult)

    hand.base += 5
    k.s5_phasor, k.s5_factor, k.s5_mag = (CS, SN), (CR, CI), MAG
    return by_act, by_dve


def stage_s5_inputs(k):
    nc, d = k.nc, k.d
    v = nc.vector
    br, bi = k.sb("s5_b_re", 136, [P, 8, 32]), k.sb("s5_b_im", 137, [P, 8, 32])
    bb = k.sb("s5_bb", 138, [P, 2, 8, 32])
    bt = k.sb("s5_bt", 140, [P, 2, 8, 32])
    bT = k.sb("s5_bT", 158, [P, 2, 2, P])
    cT = k.sb("s5_cT", 160, [P, 4, 8, 32])
    p_in, turned = k.sig("s5_in"), k.sig("s5_turned")
    with nc.Block() as block:
        @block.sync
        def _(sp):
            for dst, n in ((br, "s5_b_re"), (bi, "s5_b_im")):
                sp.dma_start(dst[:, :, :], d[n]).then_inc(p_in.sem, 16)
            sp.dma_start(cT[:, 0:2, :, :], d["s5_cT"]).then_inc(p_in.sem, 16)

        @block.vector
        def _(dve):
            link = Chain(dve, k.sig("dve_chain"))
            tt, ts = v.tensor_tensor, v.tensor_scalar
            dve.wait_ge(p_in.sem, p_in.base + 48)
            crb, cib = (c.unsqueeze(2).to_broadcast([P, 8, 32]) for c in k.s5_factor)
            tt(bb[:, 0], br[:, :, :], crb, ALU.mult)
            tt(bb[:, 1], bi[:, :, :], crb, ALU.mult)
            tt(bt[:, 0], bi[:, :, :], cib, ALU.mult)
            link(tt(bt[:, 1], br[:, :, :], cib, ALU.mult))
            link(tt(bb[:, 0], bb[:, 0], bt[:, 0], ALU.subtract))
            tt(bb[:, 1], bb[:, 1], bt[:, 1], ALU.add).then_inc(turned.sem, 1)
            ts(cT[:, 2], cT[:, 1], -1.0, None, ALU.mult)
            ts(cT[:, 3], cT[:, 0], -1.0, None, ALU.mult)
            for c in range(2):
                for jj in range(2):
                    dve.wait_ge(turned.sem, turned.base + 2 + 2 * c + jj)
                    v.tensor_copy(bT[:, c, jj, :], k.pb[c * 2 + jj][:, 0:P])

        @block.tensor
        def _(pe):
            pe.wait_ge(turned.sem, turned.base + 1)
            for c in range(2):
                for jj in range(2):
                    nc.tensor.transpose(k.pb[c * 2 + jj][:, 0:P],
                                        bb[:, c, 4 * jj:4 * jj + 4, :].rearrange("p j c -> p (j c)"),
                                        k.ident[:, :]).then_inc(turned.sem, 1)
    p_in.base += 48
    turned.base += 5
    return bT, cT


def s5_powers(k, er, ei, tmp_kb):
    g = k.nc.gpsimd
    tmp = k.sb("s5_tmp", tmp_kb, [P, 2, 4, S // 2])
    WR, WI, W2, T1, T2 = [k.s5_small[:, i, :] for i in range(17, 22)]

    def by_pool(pool):
        link = Chain(pool, k.sig("pool_chain"))
        tt = g.tensor_tensor
        g.memset(er[:, :, 0:1], 1.0)
        g.memset(ei[:, :, 0:1], 0.0)
        g.tensor_copy(WR, k.s5_phasor[0])
        link(g.tensor_copy(WI, k.s5_phasor[1]))
        n = 1
        while n < S:
            for j in (0, 4):
                wr, wi = (w[:, j:j + 4].unsqueeze(2).to_broadcast([P, 4, n]) for w in (WR, WI))
                t0, t1 = tmp[:, 0, :, 0:n], tmp[:, 1, :, 0:n]
                e_r, e_i = er[:, j:j + 4, 0:n], ei[:, j:j + 4, 0:n]
                tt(t0, e_r, wr, ALU.mult)
                link(tt(t1, e_i, wi, ALU.mult))
                link(tt(er[:, j:j + 4, n:2 * n], t0, t1, ALU.subtract))
                tt(t0, e_r, wi, ALU.mult)
                link(tt(t1, e_i, wr, ALU.mult))
                link(tt(ei[:, j:j + 4, n:2 * n], t0, t1, ALU.add))
            n *= 2
            if n < S:
                tt(T1, WR, WR, ALU.mult)
                tt(T2, WI, WI, ALU.mult)
                link(tt(W2, WR, WI, ALU.mult))
                link(tt(WR, T1, T2, ALU.subtract))
                link(tt(WI, W2, W2, ALU.add))

    return by_pool


def stage_s5(k, er, ei, bT, cT):
    nc = k.nc
    mag = k.s5_mag
    pr = k.sb("s5_pr", 16, [P, 4, S])
    vv = k.sb("s5_v", 24, [P, 2, S])
    yy = [k.sb("s5_y0", 28, [P, 2, S]), k.sb("s5_y1", 168, [P, 2, S])]
    qq = k.sb("s5_q", 32, [P, 2, 4, S])
    yS = k.sb("s5_yS", 164, [P, 2, S])
    bu, scanned, prod, out_done, outp = (k.sig(x) for x in ("s5_bu", "s5_scan", "s5_prod", "s5_out", "s5_bu_free"))
    chain = k.sig("dve_chain")
    uT = k.fm[:, 0:2, :]
    with nc.Block() as block:
        @block.tensor
        def _(pe):
            def inject(j):
                q = 32 * (j % 4)
                if j >= 2:
                    pe.wait_ge(outp.sem, outp.base + j - 1)
                for c in range(2):
                    mm = nc.tensor.matmul(k.pb[2 * (j % 2) + c][:, :], bT[q:q + 32, c, j // 4, :],
                                          uT[q:q + 32, j // 4, :], start=True, stop=True,
                                          tile_position=(q, 0))
                mm.then_inc(bu.sem, 1)

            def project(j):
                q = 32 * (j % 4)
                pe.wait_ge(prod.sem, prod.base + j + 1)
                for m, c in enumerate((0, 3, 2, 2)):
                    mm = nc.tensor.matmul(k.pb[6 + j // 4][q:q + 32, :], cT[:, c, j, :],
                                          qq[:, j % 2, m, :], start=m == 0, stop=m == 3,
                                          tile_position=(0, q), skip_group_check=True)
                mm.then_inc(out_done.sem, 1)

            for j in range(9):
                if j < 8:
                    inject(j)
                if j >= 1:
                    project(j - 1)

        @block.vector
        def _(dve):
            v = nc.vector
            link = Chain(dve, chain)
            for j in range(8):
                dve.wait_ge(bu.sem, bu.base + j + 1)
                r, i = k.pb[2 * (j % 2)][:, :], k.pb[2 * (j % 2) + 1][:, :]
                v.tensor_tensor(pr[:, 0, :], er[:, j, :], r, ALU.mult)
                v.tensor_tensor(pr[:, 1, :], ei[:, j, :], i, ALU.mult)
                v.tensor_tensor(pr[:, 2, :], er[:, j, :], i, ALU.mult)
                x = v.tensor_tensor(pr[:, 3, :], ei[:, j, :], r, ALU.mult)
                x.then_inc(outp.sem, 1)
                dve.wait_ge(outp.sem, outp.base + j + 1)
                v.tensor_tensor(vv[:, 0, :], pr[:, 0, :], pr[:, 1, :], ALU.add)
                link(v.tensor_tensor(vv[:, 1, :], pr[:, 2, :], pr[:, 3, :], ALU.subtract))
                if j >= 2:
                    dve.wait_ge(prod.sem, prod.base + j - 1)
                m = mag[:, j:j + 1].to_broadcast([P, S])
                v.tensor_tensor_scan(yy[j % 2][:, 0, :], m, vv[:, 0, :], 0.0, ALU.mult, ALU.add)
                v.tensor_tensor_scan(yy[j % 2][:, 1, :], m, vv[:, 1, :], 0.0, ALU.mult, ALU.add).then_inc(scanned.sem, 1)
            dve.wait_ge(out_done.sem, out_done.base + 8)
            for f in range(2):
                v.scalar_tensor_tensor(out=yS[:, f, :], in0=uT[:, f, :], scalar=col(k, "s5_d", f),
                                       in1=k.pb[6 + f][:, :], op0=ALU.mult, op1=ALU.add)

        @block.gpsimd
        def _(pool):
            for j in range(8):
                pool.wait_ge(scanned.sem, scanned.base + j + 1)
                if j >= 2:
                    pool.wait_ge(out_done.sem, out_done.base + j - 1)
                nc.gpsimd.tensor_tensor(qq[:, j % 2, 0, :], yy[j % 2][:, 0, :], er[:, j, :], ALU.mult)
                nc.gpsimd.tensor_tensor(qq[:, j % 2, 1, :], yy[j % 2][:, 1, :], ei[:, j, :], ALU.mult)
                nc.gpsimd.tensor_tensor(qq[:, j % 2, 2, :], yy[j % 2][:, 0, :], ei[:, j, :], ALU.mult)
                nc.gpsimd.tensor_tensor(qq[:, j % 2, 3, :], yy[j % 2][:, 1, :], er[:, j, :], ALU.mult).then_inc(prod.sem, 1)
    for s in (bu, scanned, prod, out_done, outp):
        s.base += 8

    return yS


def stage_s5_gelu(k, yS, g):
    nc = k.nc
    chain = k.sig("dve_chain")
    t1 = k.sb("s5_g1", 32, [P, 2, S])
    gT = k.sb("s5_gT", 36, [P, 2, S])
    gs = k.split("s5_g", 40, [P, 2, S], 44)
    sgd = k.sb("s5_sg", 168, [P, T, 256])
    hand = k.sig("s5_gelu")
    free = k.sig("s5_glu")
    turned = k.sig("s5_turned")
    k.freed[g] = (free.sem, free.base + T)
    with nc.Block() as block:
        @block.sync
        def _(sp):
            issue_chunks(k, sp, g + 1 + SLOTS)
            sp.wait_ge(k.sig("rows_moved").sem, 16 * 6)

        @block.vector
        def _(dve):
            v = nc.vector
            link = Chain(dve, chain)
            link(v.tensor_tensor(t1[:, :, :], yS[:, :, :], yS[:, :, :], ALU.mult))
            link(v.tensor_scalar(t1[:, :, :], t1[:, :, :], 0.044715, 1.0, ALU.mult, ALU.add))
            v.tensor_tensor(t1[:, :, :], t1[:, :, :], yS[:, :, :], ALU.mult).then_inc(hand.sem, 1)
            dve.wait_ge(hand.sem, hand.base + 2)
            v.tensor_tensor(gT[:, :, :], yS[:, :, :], t1[:, :, :], ALU.mult).then_inc(hand.sem, 1)
            dve.wait_ge(hand.sem, hand.base + 4)
            v.tensor_tensor(gs.lo[:, :, :], gT[:, :, :], plain(gs.hi[:, :, :]), ALU.subtract).then_inc(hand.sem, 1)
            dve.wait_ge(hand.sem, hand.base + 5 + T)
            dve.wait_ge(turned.sem, turned.base + T)
            for t in range(T):
                v.tensor_tensor(k.ycat[:, t, 0:256], sgd[:, t, :], k.pb[4 + t // 2][:, (t % 2) * 256:(t % 2) * 256 + 256],
                                ALU.mult)

        @block.scalar
        def _(act):
            act.wait_ge(hand.sem, hand.base + 1)
            nc.scalar.activation(t1[:, :, :], t1[:, :, :], ACT.Sigmoid,
                                 scale=2.0 * float(np.sqrt(2.0 / np.pi))).then_inc(hand.sem, 1)
            act.wait_ge(hand.sem, hand.base + 3)
            nc.scalar.copy(gs.hi[:, :, :], gT[:, :, :]).then_inc(hand.sem, 1)
            for t in range(T):
                act.wait_ge(hand.sem, hand.base + 5)
                act.wait_ge(free.sem, free.base + t + 1)
                nc.scalar.activation(sgd[:, t, :], k.pb[t][:, 0:256], ACT.Sigmoid).then_inc(hand.sem, 1)

        @block.tensor
        def _(pe):
            pe.wait_ge(hand.sem, hand.base + 5)
            wait_chunk(k, pe, g)
            for t in range(T):
                products(k, k.pb[t][:, 0:256], [(gs[:, f, t * P:(t + 1) * P], slot(k, g, f * 256, f * 256 + 256))
                                                for f in range(2)], True, True).then_inc(free.sem, 1)
            for t in range(T):
                for f in range(2):
                    c = (t % 2) * 256 + f * P
                    mm = nc.tensor.transpose(k.pb[4 + t // 2][:, c:c + P], gT[:, f, t * P:(t + 1) * P], k.ident[:, :])
                mm.then_inc(turned.sem, 1)
    hand.base += 5 + T
    free.base += T
    turned.base += T
    return g + 1


def stage_gate_rows(k):
    nc = k.nc
    grow = k.grow
    rows = k.sb("rows", 180.5, [P, 5, S])
    e = k.sb("rows_e", 191, [P, 2, S])
    mn = k.sb("rows_mn", 195, [P, 2, S])
    zero = k.sb("rows_zero", 199, [P, S])
    k.f_left, k.f_right, k.m_row = (k.sb(n, 172.5 + 2 * i, [P, S], F32R)
                                    for i, n in enumerate(("f_left", "f_right", "m_row")))
    parts = [k.sb(f"rows_split{i}", kb, [P, 2, S], F32R) for i, kb in enumerate((104, 158, 201.25))]
    k.acol = k.sb("acol", 172, [P, T, 4])
    k.mcol = k.sb("mcol", 172.25, [P, T, 4])
    moved, ones, hand = k.sig("rows_moved"), k.sig("rows_ones"), k.sig("rows_hand")
    split = k.sig("rows_parts")
    chain = k.sig("dve_chain")
    with nc.Block() as block:
        @block.sync
        def _(sp):
            sp.wait_ge(split.sem, split.base + 2)
            sp.wait_ge(ones.sem, ones.base + 3)
            for dst, row, i in ((k.f_left, 0, 0), (k.f_right, 2, 1), (k.m_row, 0, 2)):
                for p in range(2):
                    sp.dma_start(plain(dst[row + p::32, :]), plain(parts[i][0:4, p, :])).then_inc(moved.sem, 16)

        @block.scalar
        def _(act):
            act.wait_ge(hand.sem, hand.base + 1)
            nc.scalar.activation(e[0:4, :, :], e[0:4, :, :], ACT.Exp).then_inc(hand.sem, 1)
            act.wait_ge(hand.sem, hand.base + 2)
            nc.scalar.activation(e[0:4, :, :], e[0:4, :, :], ACT.Ln, bias=1.0).then_inc(hand.sem, 1)
            act.wait_ge(hand.sem, hand.base + 5)
            nc.scalar.activation(k.mcol[:, :, :].rearrange("p t h -> p (t h)"), k.pb[1][:, 0:16], ACT.Exp)

        @block.vector
        def _(dve):
            v = nc.vector
            link = Chain(dve, chain)
            z = grow[0:4, 0::2, :]
            en, m = e[0:4, :, :], mn[0:4, :, :]
            v.memset(zero[0:4, :], 0.0)
            v.tensor_scalar(m, z, 0.0, None, ALU.min)
            link(v.tensor_scalar(en, z, -1.0, None, ALU.mult))
            v.tensor_tensor(en, en, z, ALU.min).then_inc(hand.sem, 1)
            dve.wait_ge(hand.sem, hand.base + 3)
            link(v.tensor_tensor(m, m, en, ALU.subtract))
            R = [rows[0:4, i, :] for i in range(5)]
            zz = zero[0:4, :]
            v.tensor_tensor_scan(R[0], m[:, 0, :], zz, 0.0, ALU.add, ALU.add)
            link(v.tensor_tensor_scan(e[0:4, 0, :], m[:, 1, :], zz, 0.0, ALU.add, ALU.add))
            v.tensor_scalar(R[1], R[0], -1.0, None, ALU.mult)
            link(v.tensor_tensor(R[2], grow[0:4, 1, :], e[0:4, 0, :], ALU.subtract))
            link(v.tensor_tensor_scan(e[0:4, 1, :], R[2], zz, 0.0, ALU.max, ALU.max))
            v.tensor_scalar(R[3], e[0:4, 1, :], -1.0, None, ALU.mult)
            link(v.tensor_tensor(e[0:4, 1, :], e[0:4, 1, :], e[0:4, 0, :], ALU.add))
            v.tensor_scalar(R[4], e[0:4, 1, :], -1.0, None, ALU.mult).then_inc(hand.sem, 1)
            for i, row in enumerate((0, 1, 3)):
                x = v.tensor_copy(parts[i][0:4, 0, :], R[row])
            x.then_inc(split.sem, 1)
            dve.wait_ge(split.sem, split.base + 1)
            for i, row in enumerate((0, 1, 3)):
                x = v.tensor_tensor(parts[i][0:4, 1, :], R[row], plain(parts[i][0:4, 0, :]), ALU.subtract)
            x.then_inc(split.sem, 1)
            dve.wait_ge(hand.sem, hand.base + 5)
            nc.vector.tensor_copy(k.acol[:, :, :].rearrange("p t h -> p (t h)"), k.pb[0][:, 0:16])

        @block.gpsimd
        def _(pool):
            for dst in (k.f_left, k.f_right, k.m_row):
                nc.gpsimd.memset(plain(dst[:, :]), 1.0).then_inc(ones.sem, 1)

        @block.tensor
        def _(pe):
            pe.wait_ge(hand.sem, hand.base + 4)
            for t in range(T):
                nc.tensor.transpose(k.pb[0][:, 4 * t:4 * t + 4], rows[0:4, 2, t * P:(t + 1) * P], k.ident[0:4, 0:4])
                mm = nc.tensor.transpose(k.pb[1][:, 4 * t:4 * t + 4], rows[0:4, 4, t * P:(t + 1) * P],
                                         k.ident[0:4, 0:4])
            mm.then_inc(hand.sem, 1)
    hand.base += 5
    moved.base += 16 * 6
    ones.base += 3
    split.base += 2


class Convolution:

    def __init__(self, k):
        self.k = k
        k.conv = k.sb("conv", 32, [P, 4, S])
        self.cs = k.sb("convs", 40, [P, 4, S])
        self.summed, self.sigmoid = k.sig("conv_summed"), k.sig("conv_sigmoid")

    def sync(self, sp):
        pass

    def pe(self, pe, r):
        pass

    def act(self, act, r):
        if r == 5:
            for f in range(4):
                act.wait_ge(self.summed.sem, self.summed.base + f + 1)
                self.k.nc.scalar.activation(self.cs[:, f, :], self.k.conv[:, f, :],
                                            ACT.Sigmoid).then_inc(self.sigmoid.sem, 1)

    def dve(self, dve, r):
        k, v, cv = self.k, self.k.nc.vector, self.k.conv
        if r < 4:
            link = Chain(dve, k.sig("dve_chain"))
            x = k.fm[:, 10 + r, :]
            link(v.tensor_scalar(cv[:, r, :], x, col(k, "conv_w", 4 * r + 3), None, ALU.mult))
            for i in (1, 2):
                link(v.scalar_tensor_tensor(out=cv[:, r, i:], in0=x[:, 0:S - i],
                                            scalar=col(k, "conv_w", 4 * r + 3 - i), in1=cv[:, r, i:],
                                            op0=ALU.mult, op1=ALU.add))
            v.scalar_tensor_tensor(out=cv[:, r, 3:], in0=x[:, 0:S - 3], scalar=col(k, "conv_w", 4 * r),
                                   in1=cv[:, r, 3:], op0=ALU.mult, op1=ALU.add).then_inc(self.summed.sem, 1)
        elif 8 <= r < 12:
            f = r - 8
            dve.wait_ge(self.sigmoid.sem, self.sigmoid.base + f + 1)
            v.scalar_tensor_tensor(out=cv[:, f, :], in0=self.cs[:, f, :], scalar=1.0 if f < 2 else DH ** -0.5,
                                   in1=cv[:, f, :], op0=ALU.mult, op1=ALU.mult)

    def close(self):
        self.summed.base += 4
        self.sigmoid.base += 4


def stage_fox(k):
    batches = []
    for h in range(4):
        lo = DH * (h % 2)
        q, kk = k.fm[lo:lo + DH, 6 + h // 2, :], k.fm[lo:lo + DH, 8 + h // 2, :]
        for t in range(T):
            w = (t + 1) * P
            batches.append(dict(
                segs=[(0, w)],
                scores=[[(q[:, t * P:w], kk[:, 0:w], 0, w),
                         (k.f_left[32 * h:32 * h + 4, t * P:w], k.f_right[32 * h:32 * h + 4, 0:w], 0, w, 32 * h),
                         (k.identb[:, :], k.mask_row[:, :], t * P, w)]],
                values=[[k.tm[:, 2, u, h * DH:(h + 1) * DH] for u in range(t + 1)]],
                out=k.ycat[:, t, 512 + h * DH:512 + (h + 1) * DH]))
    stage_attention(k, batches, 1.0, 158, beside=Convolution(k))


def stage_mlstm(k, hg):
    nc = k.nc
    cv = k.conv
    v1 = k.sb("v_one", 158, [P, T, 4, DH + 1])
    chain = k.sig("dve_chain")
    v1_made = k.sig("v_one_made")
    decay = k.sb("ml_decay", 163, [P, 2, S])
    pT = k.sb("ml_pT", 190.5, [P, 2, T, S])
    nb = 16
    dm, qk, ex, pp, mixed, outd = (k.sig(x) for x in ("ml_logs", "ml_scores", "ml_decay", "ml_probs", "ml_mixed", "ml_out"))
    dn = k.sb("ml_den", 167.125, [P, 3, T])
    with nc.Block() as block:
        @block.tensor
        def _(pe):
            def scores(b):
                h, u = divmod(b, T)
                lo = DH * (h % 2)
                c0 = u * P
                if b >= 2:
                    pe.wait_ge(ex.sem, ex.base + b - 1)
                nc.tensor.matmul(k.pb[b % 2][:, c0:S], k.f_right[32 * h:32 * h + 2, 0:P],
                                 k.m_row[32 * h:32 * h + 2, c0:S], start=True, stop=False,
                                 tile_position=(32 * h, 0), skip_group_check=True)
                nc.tensor.matmul(k.pb[b % 2][:, c0:c0 + P], k.identb[:, :], k.mask_col[:, :], start=False,
                                 stop=True, skip_group_check=True).then_inc(dm.sem, 1)
                if b >= 2:
                    pe.wait_ge(pp.sem, pp.base + b - 1)
                nc.tensor.matmul(k.pb[2 + b % 2][:, c0:S], cv[lo:lo + DH, 2 + h // 2, c0:c0 + P],
                                 cv[lo:lo + DH, h // 2, c0:S], start=True, stop=True).then_inc(qk.sem, 1)

            def mix(h):
                pe.wait_ge(pp.sem, pp.base + 4 * h + 4)
                if h == 0:
                    pe.wait_ge(v1_made.sem, v1_made.base + 2)
                if h >= 2:
                    pe.wait_ge(outd.sem, outd.base + h - 1)
                for t in range(T):
                    for u in range(t + 1):
                        mm = nc.tensor.matmul(k.pb[4 + h % 2][:, t * 65:t * 65 + 65], pT[:, h % 2, u, t * P:(t + 1) * P],
                                              v1[:, u, h, :], start=u == 0, stop=u == t, skip_group_check=True)
                mm.then_inc(mixed.sem, 1)

            for h in range(5):
                if h < 4:
                    for u in range(T):
                        scores(4 * h + u)
                if h >= 1:
                    mix(h - 1)

        @block.scalar
        def _(act):
            for b in range(nb):
                hg.act(act, b)
                h, u = divmod(b, T)
                act.wait_ge(dm.sem, dm.base + b + 1)
                if b >= 2:
                    act.wait_ge(pp.sem, pp.base + b - 1)
                nc.scalar.activation(decay[:, b % 2, u * P:S], k.pb[b % 2][:, u * P:S], ACT.Exp,
                                     bias=k.acol[:, u, h:h + 1]).then_inc(ex.sem, 1)

        @block.vector
        def _(dve):
            v = nc.vector
            link = Chain(dve, chain)

            def finish(h):
                dve.wait_ge(mixed.sem, mixed.base + h + 1)
                o = k.pb[4 + h % 2][:, 0:260].rearrange("p (t e) -> p t e", e=65)
                den = o[:, :, 64]
                link(v.tensor_scalar(dn[:, 0, :], den, -1.0, None, ALU.mult))
                link(v.tensor_tensor(dn[:, 0, :], dn[:, 0, :], den, ALU.max))
                link(v.tensor_tensor(dn[:, 0, :], dn[:, 0, :], k.mcol[:, :, h], ALU.max))
                link(v.reciprocal(dn[:, 1, :], dn[:, 0, :]))
                v.tensor_tensor(k.ycat[:, :, 768 + h * DH:768 + (h + 1) * DH], o[:, :, 0:DH],
                                dn[:, 1, :].unsqueeze(2).to_broadcast([P, T, DH]), ALU.mult).then_inc(outd.sem, 1)

            v.tensor_copy(v1[:, :, :, 0:DH], k.tm[:, 3, :, :].rearrange("p t (h e) -> p t h e", h=4)).then_inc(
                v1_made.sem, 1)
            v.memset(v1[:, :, :, DH:DH + 1], 1.0).then_inc(v1_made.sem, 1)
            for b in range(nb):
                hg.dve(dve, b)
                h, u = divmod(b, T)
                dve.wait_ge(ex.sem, ex.base + b + 1)
                dve.wait_ge(qk.sem, qk.base + b + 1)
                if u == 0 and h >= 2:
                    dve.wait_ge(mixed.sem, mixed.base + h - 1)
                v.tensor_tensor(pT[:, h % 2, u, u * P:S], decay[:, b % 2, u * P:S], k.pb[2 + b % 2][:, u * P:S],
                                ALU.mult).then_inc(pp.sem, 1)
                if u == 3 and h >= 1:
                    finish(h - 1)
            finish(3)
    for s in (dm, qk, ex, pp):
        s.base += nb
    mixed.base += 4
    outd.base += 4
    v1_made.base += 2
    hg.close()


class HgrnGates:

    def __init__(self, k):
        self.k = k
        self.lf = k.sb("hg_lf", 40, [P, 2, S])
        self.b = k.sb("hg_b", 44, [P, 2, S])
        self.kk = k.sb("hg_k", 168, [P, 2, S])
        self.rst = k.sb("hg_reset", 178.5, [P, 2, S])
        self.X = k.sb("hg_x", 182.5, [P, 2, 2, S])
        self.lbt = k.sb("hg_lbt", 206.5, [P, 4, 2])
        self.hand = k.sig("hg_hand")

    def act(self, act, r):
        k, X, lbt, hand, a = self.k, self.X, self.lbt, self.hand, self.k.nc.scalar
        z = k.fm[:, 4:6, :]
        if r == 3:
            link = Chain(act, k.sig("act_chain"))
            act.wait_ge(hand.sem, hand.base + 1)
            a.activation(lbt[:, 0, :], lbt[:, 0, :], ACT.Exp)
            link(a.activation(X[:, 0], X[:, 0], ACT.Exp))
            a.activation(X[:, 0], X[:, 0], ACT.Ln, bias=1.0)
            a.activation(X[:, 1], X[:, 1], ACT.Exp).then_inc(hand.sem, 1)
        elif r == 7:
            act.wait_ge(hand.sem, hand.base + 3)
            a.activation(X[:, 1], X[:, 1], ACT.Ln, bias=1.0)
            a.activation(self.kk[:, :, :], z, ACT.Sigmoid, scale=-1.0).then_inc(hand.sem, 1)

    def dve(self, dve, r):
        k, X, lf, lbt, rst, hand, v = self.k, self.X, self.lf, self.lbt, self.rst, self.hand, self.k.nc.vector
        link = Chain(dve, k.sig("dve_chain"))
        z = k.fm[:, 4:6, :]
        if r == 1:
            lb = col(k, "hg_lb", 0, 2)
            v.tensor_tensor(lbt[:, 0, :], lb, lb, ALU.subtract)
            v.tensor_scalar(X[:, 1], z, -1.0, 60.0, ALU.mult, ALU.min)
            v.tensor_scalar(lf[:, :, :], z, 0.0, None, ALU.min)
            link(v.tensor_scalar(X[:, 0], z, -1.0, None, ALU.mult))
            v.tensor_tensor(X[:, 0], X[:, 0], z, ALU.min).then_inc(hand.sem, 1)
        elif r == 5:
            dve.wait_ge(hand.sem, hand.base + 2)
            link(v.reciprocal(lbt[:, 1, :], lbt[:, 0, :]))
            link(v.tensor_tensor(lbt[:, 1, :], lbt[:, 1, :], lbt[:, 0, :], ALU.mult))
            link(v.tensor_tensor(lbt[:, 2, :], lbt[:, 1, :], lbt[:, 1, :], ALU.subtract))
            link(v.tensor_scalar(lbt[:, 2, :], lbt[:, 2, :], 0.0, None, ALU.max))
            v.tensor_scalar(lbt[:, 3, :], lbt[:, 2, :], -1.0, 1.0, ALU.mult, ALU.add)
            link(v.tensor_tensor(lf[:, :, :], lf[:, :, :], X[:, 0], ALU.subtract))
            v.tensor_tensor(X[:, 1], X[:, 1], lbt[:, 2, :].unsqueeze(2).to_broadcast([P, 2, S]),
                            ALU.mult).then_inc(hand.sem, 1)
        elif r == 10:
            link(v.memset(rst[:, :, :], 1.0))
            link(v.memset(rst[:, :, 0::64], 0.0))
            dve.wait_ge(hand.sem, hand.base + 4)
            link(v.tensor_tensor(lf[:, :, :], lf[:, :, :], X[:, 1], ALU.add))
            v.tensor_tensor(self.kk[:, :, :], self.kk[:, :, :],
                            lbt[:, 3, :].unsqueeze(2).to_broadcast([P, 2, S]), ALU.mult)
            v.tensor_tensor_scan(self.b[:, :, :].rearrange("p f s -> p (f s)"),
                                 rst[:, :, :].rearrange("p f s -> p (f s)"),
                                 lf[:, :, :].rearrange("p f s -> p (f s)"), 0.0, ALU.mult, ALU.add)

    def close(self):
        self.hand.base += 4


def stage_hgrn(k, hg):
    nc = k.nc
    q = k.fm[:, 2:4, :]
    lf, b, kk, rst, X = hg.lf, hg.b, hg.kk, hg.rst, hg.X
    Z = k.sb("hg_z", 32, [P, 2, 2, S])
    acc = k.sb("hg_acc", 158, [P, 4, S])
    off = k.sb("hg_off", 190.5, [P, 4, 6, P])
    chain = k.sig("dve_chain")

    halves = [0, 1, 2, 4, 8, 16, 32, 64, 128, 256]
    made, ex, sc, sel = (k.sig(x) for x in ("hg_exponent", "hg_exp", "hg_scores", "hg_selected"))
    zr = k.sig("hg_z")
    nl = len(halves)
    with nc.Block() as block:
        @block.vector
        def _(dve):
            v = nc.vector
            link = Chain(dve, chain)

            def cut(t, n):
                return t.rearrange("p f (b c h) -> p (f b) c h", c=2, h=n)

            def exponents(i):
                n = halves[i]
                x = cut(X[:, i % 2], n)
                if i >= 3:
                    dve.wait_ge(zr.sem, zr.base + i - 2)
                if n <= 32:
                    bb = cut(b[:, :, :], n)
                    ref = bb[:, :, 0, n - 1:n].to_broadcast([P, S // n, n])
                    v.tensor_tensor(x[:, :, 1, :], bb[:, :, 1, :], ref, ALU.subtract)
                    v.tensor_tensor(x[:, :, 0, :], ref, bb[:, :, 0, :], ALU.subtract).then_inc(made.sem, 1)
                    return
                if n > 64:
                    link(v.memset(rst[:, :, n // 2::n], 1.0))
                    link(v.tensor_tensor_scan(
                        b[:, :, :].rearrange("p f s -> p (f s)"), rst[:, :, :].rearrange("p f s -> p (f s)"),
                        lf[:, :, :].rearrange("p f s -> p (f s)"), 0.0, ALU.mult, ALU.add))
                bb = cut(b[:, :, :], n)
                v.tensor_copy(x[:, :, 1, :], bb[:, :, 1, :])
                v.tensor_tensor(x[:, :, 0, :], bb[:, :, 0, n - 1:n].to_broadcast([P, S // n, n]), bb[:, :, 0, :],
                                ALU.subtract).then_inc(made.sem, 1)

            def operands(i):
                n = halves[i]
                dve.wait_ge(ex.sem, ex.base + i)
                if i >= 2:
                    dve.wait_ge(sc.sem, sc.base + 4 * (i - 1))
                x, zz = cut(X[:, i % 2], n), cut(Z[:, i % 2], n)
                v.tensor_tensor(zz[:, :, 1, :], x[:, :, 1, :], cut(q, n)[:, :, 1, :], ALU.mult)
                v.tensor_tensor(zz[:, :, 0, :], x[:, :, 0, :], cut(kk[:, :, :], n)[:, :, 0, :],
                                ALU.mult).then_inc(zr.sem, 1)

            def select(i, h):
                m = 4 * i + h
                dve.wait_ge(sc.sem, sc.base + m + 1)
                ps = k.pb[m % 4]
                n = halves[i]
                if n <= 64:
                    mask = k.mask_lev[:, i, :].bitcast(mybir.dt.uint16).unsqueeze(1).to_broadcast([P, T, P])
                    v.copy_predicated(acc[:, h, :].rearrange("p (t s) -> p t s", t=T), mask,
                                      ps[:, :].rearrange("p (t s) -> p t s", t=T)).then_inc(sel.sem, 1)
                elif n == 128:
                    v.tensor_copy(off[:, h, 0:2, :], ps[:, 0:256].rearrange("p (c s) -> p c s", c=2)).then_inc(sel.sem, 1)
                else:
                    v.tensor_copy(off[:, h, 2:6, :], ps[:, :].rearrange("p (c s) -> p c s", c=4)).then_inc(sel.sem, 1)

            link(v.memset(acc[:, :, :], 0.0))
            exponents(1)
            exponents(2)
            for i in range(nl):
                if i + 1 < nl:
                    operands(i + 1)
                if 1 <= i < nl - 2:
                    exponents(i + 2)
                for h in range(4):
                    select(i, h)

        @block.scalar
        def _(act):
            for i in range(1, nl):
                act.wait_ge(made.sem, made.base + i)
                nc.scalar.activation(X[:, i % 2], X[:, i % 2], ACT.Exp).then_inc(ex.sem, 1)

        @block.tensor
        def _(pe):
            for i in range(nl):
                if i >= 1:
                    pe.wait_ge(zr.sem, zr.base + i)
                for h in range(4):
                    m = 4 * i + h
                    if m >= 4:
                        pe.wait_ge(sel.sem, sel.base + m - 3)
                    lo, f = DH * (h % 2), h // 2
                    L = kk[lo:lo + DH, f, :] if i == 0 else Z[lo:lo + DH, i % 2, f, :]
                    R = q[lo:lo + DH, f, :] if i == 0 else Z[lo:lo + DH, i % 2, f, :]
                    ps = k.pb[m % 4]
                    n = halves[i]
                    if n <= 64:
                        blocks = [(t * P, t * P, P, t * P) for t in range(T)]
                    elif n == 128:
                        blocks = [(0, 128, P, 0), (256, 384, P, 128)]
                    else:
                        blocks = [(0, 256, 256, 0), (128, 256, 256, 256)]
                    for s0, t0, w, c in blocks:
                        mm = nc.tensor.matmul(ps[:, c:c + w], L[:, s0:s0 + P], R[:, t0:t0 + w], start=True, stop=True,
                                              skip_group_check=True)
                    mm.then_inc(sc.sem, 1)
    for s, n in ((made, nl - 1), (ex, nl - 1), (zr, nl - 1), (sc, 4 * nl), (sel, 4 * nl)):
        s.base += n

    mixed, first = k.sig("hg_mixed"), HeadNorms(k)
    at = {(0, 1): 0, (2, 3): 1, (0, 2): 2, (0, 3): 3, (1, 2): 4, (1, 3): 5}
    with nc.Block() as block:
        @block.tensor
        def _(pe):
            for h in range(4):
                for t in range(T):
                    for u in range(t + 1):
                        a = acc[:, h, t * P:(t + 1) * P] if u == t else off[:, h, at[(u, t)], :]
                        mm = nc.tensor.matmul(k.pb[4 + h][:, t * DH:(t + 1) * DH], a, k.tm[:, 0, u, h * DH:(h + 1) * DH],
                                              start=u == 0, stop=u == t, skip_group_check=True)
                mm.then_inc(mixed.sem, 1)

        @block.scalar
        def _(act):
            first.gates(act)
            first.squares(act, ((0, 256), (512, 1024)))

        @block.gpsimd
        def _(pool):
            first.roots(pool, ((0, 256), (512, 1024)))

        @block.vector
        def _(dve):
            first.means(dve, ((0, 256), (512, 1024)), 1)
            first.scale(dve, ((0, 256), (512, 1024)), 1)
            for h in range(4):
                dve.wait_ge(mixed.sem, mixed.base + h + 1)
                nc.vector.tensor_copy(k.ycat[:, :, 256 + h * DH:256 + (h + 1) * DH],
                                      k.pb[4 + h][:, 0:256].rearrange("p (t e) -> p t e", t=T))
    mixed.base += 4

    with nc.Block() as block:
        @block.scalar
        def _(act):
            first.squares(act, ((256, 512),))

        @block.gpsimd
        def _(pool):
            first.roots(pool, ((256, 512),))

        @block.vector
        def _(dve):
            first.means(dve, ((256, 512),), 2)
            first.scale(dve, ((256, 512),), 2)


class HeadNorms:

    def __init__(self, k):
        self.k = k
        self.sq = k.sb("fin_sq", 32, [P, T, D])
        self.sg = k.sb("fin_sg", 178.5, [P, 2, T, 256])
        self.ss, self.rs, self.half = (k.sb("fin_" + n, 186.5 + i / 4, [P, T, 16])
                                       for i, n in enumerate(("ss", "rs", "half")))
        self.s4 = k.sb("fin_s4", 187.25, [P, T])
        self.squared, self.mean, self.root, self.gated = (
            k.sig("fin_" + n) for n in ("squared", "mean", "root", "gates"))

    def heads(self, x, c):
        return x[:, :, c[0]:c[1]].rearrange("p t (h e) -> p t h e", e=DH)

    def gates(self, act):
        for i, m in ((0, 1), (1, 4)):
            self.k.nc.scalar.activation(self.sg[:, i], self.k.tm[:, m], ACT.Sigmoid).then_inc(self.gated.sem, 1)

    def squares(self, act, cols):
        for a, b in cols:
            self.k.nc.scalar.activation(self.sq[:, :, a:b], self.k.ycat[:, :, a:b],
                                        ACT.Square).then_inc(self.squared.sem, 1)
        self.squared.base += len(cols)

    def which(self, c):
        return slice(0, 1) if c[0] == 0 else slice(c[0] // DH, c[1] // DH)

    def roots(self, pool, cols):
        for c in cols:
            self.mean.base += 1
            pool.wait_ge(self.mean.sem, self.mean.base)
            h = self.which(c)
            self.k.nc.gpsimd.tensor_tensor(self.rs[:, :, h], self.ss[:, :, h], self.half[:, :, h],
                                           ALU.pow).then_inc(self.root.sem, 1)

    def means(self, dve, cols, n):
        v, ss = self.k.nc.vector, self.ss
        link = Chain(dve, self.k.sig("dve_chain"))
        if n == 1:
            link(v.memset(self.half[:, :, :], -0.5))
        for i, c in enumerate(cols):
            dve.wait_ge(self.squared.sem, self.squared.base - len(cols) + i + 1)
            h = slice(c[0] // DH, c[1] // DH)
            link(v.tensor_reduce(ss[:, :, h], self.heads(self.sq, c), AX.X, ALU.add))
            if c[0] == 0:
                link(v.tensor_reduce(self.s4[:, :], ss[:, :, 0:4], AX.X, ALU.add))
                v.tensor_scalar(ss[:, :, 0], self.s4[:, :], 1.0 / 256, EPS, ALU.mult, ALU.add).then_inc(self.mean.sem, 1)
            else:
                v.tensor_scalar(ss[:, :, h], ss[:, :, h], 1.0 / DH, EPS, ALU.mult, ALU.add).then_inc(self.mean.sem, 1)

    def scale(self, dve, cols, n):
        k, v, sg = self.k, self.k.nc.vector, self.sg
        link = Chain(dve, k.sig("dve_chain"))
        if n == 1:
            dve.wait_ge(self.gated.sem, 2)
            link(v.tensor_tensor(sg[:, 0], sg[:, 0], k.tm[:, 1], ALU.mult))
        for c in cols:
            self.root.base += 1
            dve.wait_ge(self.root.sem, self.root.base)
            y, n_h = self.heads(k.ycat, c), (c[1] - c[0]) // DH
            r = self.rs[:, :, self.which(c)]
            if c[0] == 0:
                y, n_h = k.ycat[:, :, 0:256].unsqueeze(2), 1
            link(v.tensor_tensor(y, y, r.unsqueeze(3).to_broadcast([P, T, n_h, y.shape[3]]), ALU.mult))
        c0 = 768 if n == 1 else 256
        v.tensor_tensor(k.ycat[:, :, c0:c0 + 256], k.ycat[:, :, c0:c0 + 256], sg[:, 2 - n], ALU.mult)


def build(nc, d, out):
    with ExitStack() as ctx:
        k = allocate(nc, ctx, d)
        for name, first, n in CHUNKS:
            k.chunks += [d[name][i] for i in range(first, first + n)]
        stage_load(k)
        first_block(k)
        second_block(k, out)


def chunked(w, width, per):
    kk, n = w.shape
    return np.ascontiguousarray(w.reshape(kk // P // per, per, P, n // width, width)
                                .transpose(3, 0, 2, 1, 4).reshape(-1, P, per * width))


def columns(x):
    return np.ascontiguousarray(np.asarray(x).reshape(-1, P).T)


def constants():
    bf = mybir.dt.np(BF16)
    c = {"ident": np.eye(P, dtype=np.float32), "identb": np.eye(P).astype(bf)}
    q, kk = np.arange(P)[:, None], np.arange(3 * P)[None, :] - P
    c["mask_band"] = np.where(np.abs(q - kk) <= 64, 0.0, NEG).astype(bf)
    a, b = np.arange(P)[:, None], np.arange(P)[None, :]
    c["mask_d4"] = np.where(np.abs(a - b) <= 64, 0.0, NEG).astype(bf)
    c["mask_d16"] = np.where(a % 4 == b % 4, 0.0, NEG).astype(bf)
    c["mask_row"] = np.where(b <= a, 0.0, NEG).astype(bf)
    c["mask_col"] = np.where(a <= b, 0.0, NEG).astype(bf)
    lev = np.zeros((P, 8, P), np.float32)
    lev[:, 0, :] = a == b
    for i in range(7):
        hs = 1 << i
        lev[:, i + 1, :] = (a // (2 * hs) == b // (2 * hs)) & ((a // hs) % 2 == 0) & ((b // hs) % 2 == 1)
    c["mask_lev"] = lev.astype(bf)
    ra = np.zeros((P, 3, T, 16), np.float32)
    inv = np.float32(500000.0) ** (-(np.arange(8, dtype=np.float32) * 2.0 / 16))
    for g, r in enumerate(A_DIL):
        order = np.arange(S).reshape(T, P) if r == 1 else np.arange(S).reshape(P, T).T
        ang = order.T[:, :, None].astype(np.float32) * inv.astype(np.float32)
        ra[:, g, :, 0:8], ra[:, g, :, 8:16] = np.cos(ang), np.sin(ang)
    c["ropeA"] = ra
    inv = (np.float32(10000.0) ** (-(np.arange(16, dtype=np.float32) * 2.0 / 32))).astype(np.float32)
    ang = np.arange(S).reshape(T, P).T[:, :, None].astype(np.float32) * inv
    c["ropeB"] = np.concatenate([np.cos(ang), np.sin(ang)], -1).astype(np.float32)
    return c


def layout(x):
    x = {n: np.asarray(a) for n, a in x.items()}
    a = {"x": x["x"].reshape(S, D)}
    w = x["w_in"]
    cols = []
    for g in range(3):
        cols += [w[:, 256 * g:256 * g + 256], w[:, 768 + 256 * g:1024 + 256 * g]]
    cols += [w[:, 1536:2304], w[:, 2816:3072], w[:, 2304:2816]]
    a["w_proj"] = chunked(np.concatenate(cols, 1), 512, 4)
    a["w_kpe"] = chunked(w[:, 3072:3104], 32, 8)
    a["w_gates"] = chunked(w[:, 3104:], 2 * P, KD)
    a["w_uq"] = chunked(x["mla_w_uq"], 384, 4)
    a["w_ukv"] = chunked(x["mla_w_ukv"], 1024, 2)
    a["w_oa"] = chunked(x["w_o_a"], 1024, 2)
    a["w_ob"] = chunked(x["w_o_b"], 512, 4)
    a["w_out"] = chunked(x["w_out"], 512, 4)
    a["w_ff1"] = chunked(x["w_ff1"], 512, 4)
    half = FF1 // 2
    a["w_ff2"] = np.concatenate([chunked(x["w_ff2"][i:i + half], 512, 4) for i in (0, half)])
    z = np.zeros((P, 3), np.float32)
    gb = x["gate_bias_2"].reshape(3, 4)
    z[0:4, :] = gb.T
    lb = lambda n: columns(x[n][0])
    parts = {"mix_pre": columns(x["norm_mix_pre"]), "b_gate": columns(x["b_gate"]),
             "q_norm": columns(x["mla_q_norm"]), "kv_norm": columns(x["mla_kv_norm"]),
             "mlp_pre": columns(x["norm_mlp_pre"]), "mix_pre2": lb("ln_mix_pre_2"),
             "ffn_pre2": lb("ln_ffn_pre_2"), "mix_gain2": lb("mix_gain_2"),
             "hg_lb": lb("hgrn_lb_logits_2"),
             "conv_w": np.ascontiguousarray(x["mlstm_conv_w_2"][0].reshape(4, 4, P).transpose(2, 1, 0).reshape(P, 16)),
             "lam_re": columns(x["s5_lambda_re_2"][0].reshape(-1)), "lam_im": columns(x["s5_lambda_im_2"][0].reshape(-1)),
             "log_dt": columns(np.repeat(x["s5_log_dt_2"][0], 64)), "s5_d": lb("s5_d_2"), "gate_b": z}
    a["cols"] = np.concatenate([parts[n] for n in COLS], 1)
    for n, m in (("norm_mix_post", "norm_mix_post"), ("norm_mlp_post", "norm_mlp_post")):
        a[n] = x[m].reshape(D)
    a["ln_mix_post_2"], a["ln_ffn_post_2"] = x["ln_mix_post_2"][0], x["ln_ffn_post_2"][0]
    w = x["w_in_2"][0]
    at = dict(s5u=0, hgq=256, hgf=512, hgi=768, hgg=1024, foxq=1280, foxk=1536, foxv=1792, mlq=2052, mlk=2308,
              mlv=2564, mlo=2820)
    part = lambda *names: [w[:, at[n]:at[n] + 256] for n in names]
    a["w_fm"] = chunked(np.concatenate(part("s5u", "hgq", "hgf", "foxq", "foxk", "mlq"), 1), 512, 4)
    gates = np.zeros((D, 96), np.float32)
    for i, c in enumerate((2048, 3076, 3080)):
        gates[:, 32 * i:32 * i + 4] = w[:, c:c + 4]
    a["w_fg"] = chunked(np.concatenate(part("mlk") + [gates], 1), 352, 4)
    a["w_tm"] = chunked(np.concatenate(part("hgi", "hgg", "foxv", "mlv"), 1), 512, 4)
    a["w_tg"] = chunked(np.concatenate(part("mlo"), 1), 256, 8)
    a["w_glu"] = chunked(x["s5_w_glu_2"][0], 256, 2)
    a["w_out2"] = chunked(x["w_out_2"][0], 512, 4)
    f = FF2 // P
    up = np.concatenate([x["w_ffn_gate_2"][0].reshape(D, f, 1, P), x["w_ffn_up_2"][0].reshape(D, f, 1, P)], 2)
    a["w_up"] = chunked(up.reshape(D, 2 * FF2), 2 * P, KD)
    w = x["w_ffn_down_2"][0]
    a["w_dn_a"] = chunked(w[:12 * P], 512, 4)
    a["w_dn_b"] = chunked(w[12 * P:20 * P], 512, 4)
    a["w_dn_c"] = chunked(w[20 * P:], 512, 2)
    for n, m in (("s5_b_re", "s5_b_re_2"), ("s5_b_im", "s5_b_im_2")):
        z = np.zeros((8, 2, 64, 2, 16), np.float32)
        for i in range(2):
            z[:, i, :, i, :] = x[m][0].reshape(8, 2, 64, 16)[:, i]
        a[n] = np.ascontiguousarray(z.reshape(8, P, 32).transpose(1, 0, 2))
    z = np.zeros((2, 8, 2, 64, 2, 16), np.float32)
    for c, m in enumerate(("s5_c_re_2", "s5_c_im_2")):
        for i in range(2):
            z[c, :, i, :, i, :] = x[m][0].reshape(8, 2, 16, 64)[:, i].transpose(0, 2, 1)
    a["s5_cT"] = np.ascontiguousarray(z.reshape(2, 8, P, 32).transpose(2, 0, 1, 3))
    a.update(constants())
    return a


CHUNKS = [("w_proj", 0, 12), ("w_kpe", 0, 1), ("w_gates", 0, 8), ("w_uq", 0, 2), ("w_ukv", 0, 1), ("w_oa", 0, 1),
          ("w_ob", 0, 2), ("w_out", 0, 4), ("w_ff1", 0, 8), ("w_ff2", 0, 8), ("w_ff1", 8, 8), ("w_ff2", 8, 8),
          ("w_fm", 0, 6), ("w_fg", 0, 2), ("w_tm", 0, 4), ("w_tg", 0, 1), ("w_glu", 0, 1), ("w_out2", 0, 4),
          ("w_up", 0, 12), ("w_dn_a", 0, 6), ("w_up", 12, 10), ("w_dn_b", 0, 2), ("w_dn_c", 0, 1),
          ("w_dn_b", 2, 2), ("w_dn_c", 1, 1)]


def kernel(**inputs):
    import concourse.bacc as bacc
    from concourse.bass_utils import run_bass_kernel_spmd

    nc = bacc.Bacc("TRN2", target_bir_lowering=False, num_devices=1)
    arrays, d = {}, {}
    for name, a in layout(inputs).items():
        arrays[f"in_{name}"] = a
        d[name] = nc.dram_tensor(f"in_{name}", a.shape, mybir.dt.from_np(a.dtype), kind="ExternalInput").ap()
    d["scratch"] = nc.dram_tensor("scratch", (2, S, 260), F32, kind="Internal").ap()
    out = nc.dram_tensor("out_0_dram", (1, S, D), F32, kind="ExternalOutput").ap()
    build(nc, d, out)
    r = run_bass_kernel_spmd(nc, [arrays], core_ids=[0])
    return r.results[0]["out_0_dram"]
```
